# Optimizing a Trainium2 kernel written in Bass

```python
import jax
import jax.numpy as jnp
from jax import lax
import numpy as np

D_MODEL = 1024
BATCH = 1
SEQ = 256
DEPTH = 1

GRID_W = 64
CTX_LEN = 256
MLSTM_HEADS = 4
MLSTM_DH = 128
MLSTM_W = MLSTM_HEADS * MLSTM_DH
MLSTM_CHUNK = 64
QK_CONV = 3
N_GATES = 4 * MLSTM_HEADS
ATTN_HEADS = 8
KV_HEADS = 2
ATTN_DH = 64
ATTN_W = ATTN_HEADS * ATTN_DH
KV_W = KV_HEADS * ATTN_DH
GQA_GROUP = ATTN_HEADS // KV_HEADS
WINDOW = 128
ATTN_BLOCK = 128
ROPE_BASE = 10000.0
ROPE_AXIS_PAIRS = ATTN_DH // 4
MIX_W = MLSTM_W + ATTN_W
IN_SPLITS = (2 * MLSTM_W, 3 * MLSTM_W, 4 * MLSTM_W, 4 * MLSTM_W + N_GATES,
             4 * MLSTM_W + N_GATES + ATTN_W, 4 * MLSTM_W + N_GATES + ATTN_W + KV_W)
IN_COLS = 4 * MLSTM_W + N_GATES + ATTN_W + 2 * KV_W
D_FF = 2816
FFN_CONV = 3
EPS = 1e-6


def rmsnorm(x, g):
    xf = x.astype(jnp.float32)
    y = xf * lax.rsqrt(jnp.mean(xf * xf, axis=-1, keepdims=True) + EPS)
    return (y * g.astype(jnp.float32)).astype(x.dtype)

def modulate(h, shift, scale):
    return h * (1 + scale) + shift

def dwconv(x, w, b):
    k = w.shape[0]
    y = lax.conv_general_dilated(x, w[:, None, :], window_strides=(1,), padding=[(k // 2, k // 2)],
                                 dimension_numbers=('NWC', 'WIO', 'NWC'),
                                 feature_group_count=x.shape[-1])
    return y + b

def heads_first(t, n_heads):
    b, l, _ = t.shape
    return t.reshape(b, l, n_heads, -1).transpose(0, 2, 1, 3)

def axial_rope(n_tokens):
    rows = n_tokens // GRID_W
    r, col = jnp.meshgrid(jnp.arange(rows, dtype=jnp.float32), jnp.arange(GRID_W, dtype=jnp.float32),
                          indexing='ij')
    inv = ROPE_BASE ** (-jnp.arange(ROPE_AXIS_PAIRS, dtype=jnp.float32) / ROPE_AXIS_PAIRS)
    ang = jnp.stack([r.reshape(-1)[:, None] * inv, col.reshape(-1)[:, None] * inv], axis=1)
    return jnp.cos(ang), jnp.sin(ang)

def apply_rope(x, cos, sin):
    b, l, h, _ = x.shape
    xr = x.astype(jnp.float32).reshape(b, l, h, 2, 2, ROPE_AXIS_PAIRS)
    x0, x1 = xr[..., 0, :], xr[..., 1, :]
    cs, sn = cos[:, None], sin[:, None]
    y = jnp.stack([x0 * cs - x1 * sn, x0 * sn + x1 * cs], axis=-2)
    return y.reshape(b, l, h, ATTN_DH).astype(x.dtype)

def project_tokens(h, w_in, qk_conv_w, qk_conv_b, gate_b):
    b, l, _ = h.shape
    u = h @ w_in
    qk, v_m, o_m, gates, q_a, k_a, v_a = jnp.split(u, IN_SPLITS, axis=-1)
    q_m, k_m = jnp.split(jax.nn.silu(dwconv(qk, qk_conv_w, qk_conv_b)), 2, axis=-1)
    q_m = heads_first(q_m, MLSTM_HEADS).astype(jnp.float32)
    k_m = heads_first(k_m, MLSTM_HEADS).astype(jnp.float32) * (MLSTM_DH ** -0.5)
    v_m = heads_first(v_m, MLSTM_HEADS).astype(jnp.float32)
    g = (gates + gate_b).astype(jnp.float32).reshape(b, l, 4, MLSTM_HEADS).transpose(2, 0, 3, 1)
    gates = (g[0], jax.nn.log_sigmoid(g[1]), g[2], jax.nn.log_sigmoid(g[3]))
    q_a = q_a.reshape(b, l, ATTN_HEADS, ATTN_DH)
    k_a = k_a.reshape(b, l, KV_HEADS, ATTN_DH)
    v_a = v_a.reshape(b, l, KV_HEADS, ATTN_DH)
    return q_m, k_m, v_m, o_m, gates, q_a, k_a, v_a

def init_state(b):
    return (jnp.zeros((b, MLSTM_HEADS, MLSTM_DH, MLSTM_DH), jnp.float32),
            jnp.zeros((b, MLSTM_HEADS, MLSTM_DH), jnp.float32),
            jnp.zeros((b, MLSTM_HEADS), jnp.float32))

def mlstm_scan(q, k, v, log_i, log_f, init, return_h):
    b, h, l, dh = k.shape
    nc = l // MLSTM_CHUNK
    chunk = lambda t: t.reshape((b, h, nc, MLSTM_CHUNK) + t.shape[3:])
    k, v, li, lf = chunk(k), chunk(v), chunk(log_i), chunk(log_f)
    cum = jnp.cumsum(lf, axis=-1)
    cum_end = cum[..., -1]
    g = cum_end[..., None] - cum + li
    m_loc = jnp.max(g, axis=-1)
    w = jnp.exp(g - m_loc[..., None])
    c_loc = jnp.einsum('bhnsd,bhnse->bhnde', w[..., None] * k, v)
    n_loc = jnp.einsum('bhns,bhnsd->bhnd', w, k)

    def step(carry, inp):
        c_st, n_st, m_st = carry
        c_l, n_l, m_l, bt = inp
        m_new = jnp.maximum(bt + m_st, m_l)
        a = jnp.exp(bt + m_st - m_new)
        s = jnp.exp(m_l - m_new)
        return (a[..., None, None] * c_st + s[..., None, None] * c_l,
                a[..., None] * n_st + s[..., None] * n_l, m_new), (c_st, n_st, m_st)

    final, starts = lax.scan(step, init, tuple(jnp.moveaxis(t, 2, 0) for t in (c_loc, n_loc, m_loc, cum_end)))
    if not return_h:
        return None, final
    c0, n0, m0 = (jnp.moveaxis(t, 0, 2) for t in starts)
    q = chunk(q)
    a_log = cum + m0[..., None]
    d_log = cum[..., :, None] - cum[..., None, :] + li[..., None, :]
    order = jnp.tril(jnp.ones((MLSTM_CHUNK, MLSTM_CHUNK), dtype=bool))
    d_log = jnp.where(order, d_log, -jnp.inf)
    m_t = jnp.maximum(a_log, jnp.max(d_log, axis=-1))
    dec = jnp.exp(d_log - m_t[..., None])
    inter = jnp.exp(a_log - m_t)
    s = jnp.einsum('bhntd,bhnsd->bhnts', q, k) * dec
    num = jnp.einsum('bhnts,bhnse->bhnte', s, v) + inter[..., None] * jnp.einsum('bhntd,bhnde->bhnte', q, c0)
    den = jnp.sum(s, axis=-1) + inter * jnp.einsum('bhntd,bhnd->bhnt', q, n0)
    hid = num / jnp.maximum(jnp.abs(den), jnp.exp(-m_t))[..., None]
    return hid.reshape(b, h, l, dh), final

def mlstm_bidirectional(q, k, v, gates, init_f, init_b, return_h):
    li_f, lf_f, li_b, lf_b = gates
    flip = lambda t: jnp.flip(t, axis=2)
    h_f, st_f = mlstm_scan(q, k, v, li_f, lf_f, init_f, return_h)
    h_b, st_b = mlstm_scan(flip(q), flip(k), flip(v), flip(li_b), flip(lf_b), init_b, return_h)
    hid = h_f + flip(h_b) if return_h else None
    return hid, st_f, st_b

def mlstm_merge(h, o, gain):
    b, _, l, _ = h.shape
    hn = h * lax.rsqrt(jnp.mean(h * h, axis=-1, keepdims=True) + EPS)
    hn = hn.transpose(0, 2, 1, 3).reshape(b, l, MLSTM_W) * gain.astype(jnp.float32)
    return (hn * jax.nn.sigmoid(o.astype(jnp.float32))).astype(o.dtype)

def window_attention(q, k, v, k_ctx, v_ctx, sink):
    b, l = q.shape[:2]
    nb = l // ATTN_BLOCK
    qb = q.reshape(b, nb, ATTN_BLOCK, KV_HEADS, GQA_GROUP, ATTN_DH)

    def band(t):
        tb = jnp.pad(t.reshape(b, nb, ATTN_BLOCK, KV_HEADS, ATTN_DH), ((0, 0), (1, 1), (0, 0), (0, 0), (0, 0)))
        return jnp.concatenate([tb[:, :-2], tb[:, 1:-1], tb[:, 2:]], axis=2)

    kb, vb = band(k), band(v)
    n_band = 3 * ATTN_BLOCK
    qpos = jnp.arange(l).reshape(nb, ATTN_BLOCK)
    kpos = qpos[:, :1] - ATTN_BLOCK + jnp.arange(n_band)
    valid = ((jnp.abs(kpos[:, None, :] - qpos[:, :, None]) <= WINDOW)
             & (kpos >= 0)[:, None, :] & (kpos < l)[:, None, :])
    s_band = jnp.einsum('bnqhgd,bnkhd->bnhgqk', qb, kb).astype(jnp.float32)
    s_band = jnp.where(valid[None, :, None, None], s_band, -jnp.inf)
    s_ctx = jnp.einsum('bnqhgd,bchd->bnhgqc', qb, k_ctx).astype(jnp.float32)
    s_sink = jnp.broadcast_to(sink.astype(jnp.float32).reshape(KV_HEADS, GQA_GROUP, 1, 1),
                              s_band.shape[:-1] + (1,))
    p = jax.nn.softmax(jnp.concatenate([s_band, s_ctx, s_sink], axis=-1), axis=-1).astype(v.dtype)
    out = (jnp.einsum('bnhgqk,bnkhd->bnqhgd', p[..., :n_band], vb)
           + jnp.einsum('bnhgqc,bchd->bnqhgd', p[..., n_band:n_band + k_ctx.shape[1]], v_ctx))
    return out.reshape(b, l, ATTN_W)

def context_attention(q, k, v, sink):
    b, n = q.shape[:2]
    qg = q.reshape(b, n, KV_HEADS, GQA_GROUP, ATTN_DH)
    s = jnp.einsum('bqhgd,bkhd->bhgqk', qg, k).astype(jnp.float32)
    s_sink = jnp.broadcast_to(sink.astype(jnp.float32).reshape(KV_HEADS, GQA_GROUP, 1, 1), s.shape[:-1] + (1,))
    p = jax.nn.softmax(jnp.concatenate([s, s_sink], axis=-1), axis=-1)[..., :-1].astype(v.dtype)
    return jnp.einsum('bhgqk,bkhd->bqhgd', p, v).reshape(b, n, ATTN_W)

def conv_glu(h, w_up, conv_w, conv_b, w_down):
    a, val = jnp.split(h @ w_up, 2, axis=-1)
    a = jax.nn.gelu(dwconv(a, conv_w, conv_b))
    return (a * val) @ w_down

def first_inputs(seed: int = 0) -> dict:
    key = jax.random.key(seed)
    ks = jax.random.split(key, 20)
    nrm = lambda k, shape, s: jax.random.normal(k, shape, jnp.float32) * s
    f_bias = jnp.linspace(3.0, 6.0, MLSTM_HEADS, dtype=jnp.float32)
    zero_h = jnp.zeros((MLSTM_HEADS,), jnp.float32)
    gate_base = jnp.stack([zero_h, f_bias, zero_h, f_bias]).reshape(-1)
    return {
        'x': nrm(ks[0], (BATCH, SEQ, D_MODEL), 1.0),
        'c': nrm(ks[1], (BATCH, D_MODEL), 1.0),
        'ctx': nrm(ks[2], (BATCH, CTX_LEN, D_MODEL), 1.0),
        'c_ctx': nrm(ks[3], (D_MODEL,), 1.0),
        'w_ada': nrm(ks[4], (DEPTH, D_MODEL, 6 * D_MODEL), 0.5 * D_MODEL ** -0.5),
        'b_ada': nrm(ks[5], (DEPTH, 6 * D_MODEL), 0.02),
        'norm_mix': 1.0 + nrm(ks[6], (DEPTH, D_MODEL), 0.02),
        'norm_ffn': 1.0 + nrm(ks[7], (DEPTH, D_MODEL), 0.02),
        'w_in': nrm(ks[8], (DEPTH, D_MODEL, IN_COLS), D_MODEL ** -0.5),
        'gate_b': gate_base[None, :] + nrm(ks[9], (DEPTH, N_GATES), 0.1),
        'qk_conv_w': nrm(ks[10], (DEPTH, QK_CONV, 2 * MLSTM_W), QK_CONV ** -0.5),
        'qk_conv_b': nrm(ks[11], (DEPTH, 2 * MLSTM_W), 0.02),
        'mlstm_norm': 1.0 + nrm(ks[12], (DEPTH, MLSTM_W), 0.02),
        'attn_sink': nrm(ks[13], (DEPTH, ATTN_HEADS), 0.5),
        'w_out': nrm(ks[14], (DEPTH, MIX_W, D_MODEL), MIX_W ** -0.5),
        'w_up': nrm(ks[15], (DEPTH, D_MODEL, 2 * D_FF), D_MODEL ** -0.5),
        'ffn_conv_w': nrm(ks[16], (DEPTH, FFN_CONV, D_FF), FFN_CONV ** -0.5),
        'ffn_conv_b': nrm(ks[17], (DEPTH, D_FF), 0.02),
        'w_down': nrm(ks[18], (DEPTH, D_FF, D_MODEL), D_FF ** -0.5),
        'final_norm': 1.0 + nrm(ks[19], (D_MODEL,), 0.02),
    }

def first_block(x, c, ctx, c_ctx, w_ada, b_ada, norm_mix, norm_ffn, w_in, gate_b, qk_conv_w, qk_conv_b,
              mlstm_norm, attn_sink, w_out, w_up, ffn_conv_w, ffn_conv_b, w_down, final_norm):
    cos, sin = axial_rope(x.shape[1])
    attn_scale = ATTN_DH ** -0.5
    for l in range(DEPTH):
        last = l == DEPTH - 1
        sh_a, sc_a, g_a, sh_f, sc_f, g_f = jnp.split(
            (jax.nn.silu(c) @ w_ada[l] + b_ada[l])[:, None, :], 6, axis=-1)
        csh_a, csc_a, cg_a, csh_f, csc_f, cg_f = jnp.split(
            jax.nn.silu(c_ctx) @ w_ada[l] + b_ada[l], 6, axis=-1)

        hc = modulate(rmsnorm(ctx, norm_mix[l]), csh_a, csc_a)
        qm_c, km_c, vm_c, om_c, gates_c, qa_c, ka_c, va_c = project_tokens(
            hc, w_in[l], qk_conv_w[l], qk_conv_b[l], gate_b[l])
        zero = init_state(ctx.shape[0])
        hm_c, st_f, st_b = mlstm_bidirectional(qm_c, km_c, vm_c, gates_c, zero, zero, not last)

        hx = modulate(rmsnorm(x, norm_mix[l]), sh_a, sc_a)
        qm, km, vm, om, gates_x, qa, ka, va = project_tokens(hx, w_in[l], qk_conv_w[l], qk_conv_b[l], gate_b[l])
        hm, _, _ = mlstm_bidirectional(qm, km, vm, gates_x, st_f, st_b, True)
        y_m = mlstm_merge(hm, om, mlstm_norm[l])
        y_a = window_attention(apply_rope(qa, cos, sin) * attn_scale, apply_rope(ka, cos, sin), va,
                               ka_c, va_c, attn_sink[l])
        x = x + g_a * (jnp.concatenate([y_m, y_a], axis=-1) @ w_out[l])
        x = x + g_f * conv_glu(modulate(rmsnorm(x, norm_ffn[l]), sh_f, sc_f),
                               w_up[l], ffn_conv_w[l], ffn_conv_b[l], w_down[l])

        if not last:
            y_mc = mlstm_merge(hm_c, om_c, mlstm_norm[l])
            y_ac = context_attention(qa_c * attn_scale, ka_c, va_c, attn_sink[l])
            ctx = ctx + cg_a * (jnp.concatenate([y_mc, y_ac], axis=-1) @ w_out[l])
            ctx = ctx + cg_f * conv_glu(modulate(rmsnorm(ctx, norm_ffn[l]), csh_f, csc_f),
                                        w_up[l], ffn_conv_w[l], ffn_conv_b[l], w_down[l])
    return rmsnorm(x, final_norm)


DEPTH_2 = 2

N_EVEN = (DEPTH_2 + 1) // 2
N_ODD = DEPTH_2 // 2
CHUNK = 128
Q_BLOCK = 128

RET_HEADS = 8
RET_DK = 64
RET_DV = 64
RET_WIDTH = RET_HEADS * RET_DV
SSD_HEADS = 8
SSD_HEADDIM = 64
SSD_INNER = SSD_HEADS * SSD_HEADDIM
SSD_GROUPS = 2
SSD_STATE = 128
SSD_CONV = 5
CONV_CH = SSD_INNER + 2 * SSD_GROUPS * SSD_STATE
IN0_SPLITS = [RET_WIDTH, 2 * RET_WIDTH, 3 * RET_WIDTH, 4 * RET_WIDTH, 4 * RET_WIDTH + SSD_INNER, 4 * RET_WIDTH + SSD_INNER + CONV_CH]
IN0_WIDTH = 4 * RET_WIDTH + SSD_INNER + CONV_CH + 2 * SSD_HEADS
MIX0_WIDTH = RET_WIDTH + SSD_INNER
MLA_HEADS = 16
QK_NOPE = 64
QK_ROPE = 32
V_HEAD = 64
KV_RANK = 256
Q_RANK = 768
IN1_WIDTH = Q_RANK + KV_RANK + QK_ROPE
MLA_WIDTH = MLA_HEADS * V_HEAD
_FF_CEIL = -(-8 * D_MODEL // 3)
D_FF_2 = -(-_FF_CEIL // 256) * 256


def rms_norm(x, w=None):
    xf = x.astype(jnp.float32)
    y = xf * lax.rsqrt(jnp.mean(xf * xf, axis=-1, keepdims=True) + EPS)
    if w is not None:
        y = y * w.astype(jnp.float32)
    return y.astype(x.dtype)

def adaln_params(cond, w_ada, b_ada):
    m = jax.nn.silu(cond) @ w_ada + b_ada
    return jnp.split(m[:, None, :], 6, axis=-1)

def modulate_2(h, shift, scale):
    return h * (1 + scale) + shift

def axial_rope_tables(n_tok, rot_dim):
    rows = n_tok // GRID_W
    row = jnp.repeat(jnp.arange(rows), GRID_W).astype(jnp.float32)
    col = jnp.tile(jnp.arange(GRID_W), rows).astype(jnp.float32)
    n_freq = rot_dim // 4
    inv_freq = ROPE_BASE ** (-jnp.arange(n_freq, dtype=jnp.float32) / n_freq)
    ang = jnp.concatenate([row[:, None] * inv_freq, col[:, None] * inv_freq], axis=-1)
    return jnp.cos(ang), jnp.sin(ang)

def apply_rope_2(x, cos, sin):
    half = x.shape[-1] // 2
    x1 = x[..., :half].astype(jnp.float32)
    x2 = x[..., half:].astype(jnp.float32)
    c = cos[:, None, :]
    s = sin[:, None, :]
    return jnp.concatenate([x1 * c - x2 * s, x1 * s + x2 * c], axis=-1).astype(x.dtype)

def bhld(t):
    return jnp.transpose(t, (0, 2, 1, 3))

def depthwise_conv_centred(x, w, b):
    k = w.shape[0]
    y = lax.conv_general_dilated(x, w[:, None, :].astype(x.dtype), window_strides=(1,), padding=[(k // 2, k // 2)],
                                 dimension_numbers=('NWC', 'WIO', 'NWC'), feature_group_count=x.shape[-1])
    return y + b

def chunked_decay_scan(q, k, v, log_a, s0):
    b, h, l, dk = q.shape
    dv = v.shape[-1]
    n = l // CHUNK
    qc = q.astype(jnp.float32).reshape(b, h, n, CHUNK, dk)
    kc = k.astype(jnp.float32).reshape(b, h, n, CHUNK, dk)
    vc = v.astype(jnp.float32).reshape(b, h, n, CHUNK, dv)
    cum = jnp.cumsum(log_a.astype(jnp.float32).reshape(b, h, n, CHUNK), axis=-1)
    idx = jnp.arange(CHUNK)
    lower = idx[:, None] >= idx[None, :]
    decay = jnp.exp(jnp.where(lower, cum[..., :, None] - cum[..., None, :], -jnp.inf))
    scores = jnp.einsum('bhnid,bhnjd->bhnij', qc, kc) * decay
    y_intra = jnp.einsum('bhnij,bhnjv->bhniv', scores, vc)
    to_end = jnp.exp(cum[..., -1:] - cum)
    kv_chunk = jnp.einsum('bhnjd,bhnj,bhnjv->bhndv', kc, to_end, vc)
    total = jnp.exp(cum[..., -1])

    def step(s, inp):
        kv_n, tot_n = inp
        return tot_n[..., None, None] * s + kv_n, s

    s_final, s_before = lax.scan(step, s0, (jnp.moveaxis(kv_chunk, 2, 0), jnp.moveaxis(total, 2, 0)))
    s_before = jnp.moveaxis(s_before, 0, 2)
    y_inter = jnp.einsum('bhnid,bhni,bhndv->bhniv', qc, jnp.exp(cum), s_before)
    return (y_intra + y_inter).reshape(b, h, l, dv), s_final

def bidir_prefix_scan(ctx_in, lat_in):
    qc, kc, vfc, vbc, lafc, labc = ctx_in
    ql, kl, vfl, vbl, lafl, labl = lat_in
    b, h, _, dk = qc.shape
    dv = vfc.shape[-1]
    s0 = jnp.zeros((b, h, dk, dv), jnp.float32)
    flip = lambda t: jnp.flip(t, axis=2)
    yc_f, sc_f = chunked_decay_scan(qc, kc, vfc, lafc, s0)
    yc_b, sc_b = chunked_decay_scan(flip(qc), flip(kc), flip(vbc), flip(labc), s0)
    yl_f, _ = chunked_decay_scan(ql, kl, vfl, lafl, sc_f)
    yl_b, _ = chunked_decay_scan(flip(ql), flip(kl), flip(vbl), flip(labl), sc_b)

    def merge(q, k, vb, yf, yb):
        diag = jnp.einsum('bhld,bhld->bhl', q.astype(jnp.float32), k.astype(jnp.float32))[..., None] * vb.astype(jnp.float32)
        return (yf + flip(yb) - diag).astype(vb.dtype)

    return merge(qc, kc, vbc, yc_f, yc_b), merge(ql, kl, vbl, yl_f, yl_b)

def ret_ssd_project(h, w_in, conv_w, conv_b, dt_bias, a_log, decay_logit, rope):
    b, l, _ = h.shape
    q, k, v, g, z, xbc, dt_raw = jnp.split(h @ w_in, IN0_SPLITS, axis=-1)
    q = q.reshape(b, l, RET_HEADS, RET_DK)
    k = k.reshape(b, l, RET_HEADS, RET_DK) * (RET_DK ** -0.5)
    if rope is not None:
        q = apply_rope_2(q, *rope)
        k = apply_rope_2(k, *rope)
    v = v.reshape(b, l, RET_HEADS, RET_DV)
    ret_la = jax.nn.log_sigmoid(decay_logit.astype(jnp.float32))
    la_r = [jnp.broadcast_to(ret_la[d][None, :, None], (b, RET_HEADS, l)) for d in range(2)]
    ret_in = (bhld(q), bhld(k), bhld(v), bhld(v), la_r[0], la_r[1])
    xbc = jax.nn.silu(depthwise_conv_centred(xbc, conv_w, conv_b))
    xs, bm, cm = jnp.split(xbc, [SSD_INNER, SSD_INNER + SSD_GROUPS * SSD_STATE], axis=-1)
    xs = xs.reshape(b, l, SSD_HEADS, SSD_HEADDIM)
    rep = SSD_HEADS // SSD_GROUPS
    bm = jnp.repeat(bm.reshape(b, l, SSD_GROUPS, SSD_STATE), rep, axis=2)
    cm = jnp.repeat(cm.reshape(b, l, SSD_GROUPS, SSD_STATE), rep, axis=2)
    dt = jax.nn.softplus(dt_raw.astype(jnp.float32).reshape(b, l, 2, SSD_HEADS) + dt_bias.astype(jnp.float32))
    log_a = dt * (-jnp.exp(a_log.astype(jnp.float32)))
    v_f = xs * dt[:, :, 0, :, None].astype(xs.dtype)
    v_b = xs * dt[:, :, 1, :, None].astype(xs.dtype)
    ssd_in = (bhld(cm), bhld(bm), bhld(v_f), bhld(v_b),
              jnp.transpose(log_a[:, :, 0], (0, 2, 1)), jnp.transpose(log_a[:, :, 1], (0, 2, 1)))
    return ret_in, ssd_in, g, z, xs

def retention_ssd_mixer(a_ctx, a_lat, w_in, conv_w, conv_b, dt_bias, a_log, d_skip, ssd_norm_w,
                        decay_logit, gn_w, w_out, rope, need_ctx):
    pc = ret_ssd_project(a_ctx, w_in, conv_w, conv_b, dt_bias, a_log, decay_logit, None)
    pl = ret_ssd_project(a_lat, w_in, conv_w, conv_b, dt_bias, a_log, decay_logit, rope)
    ret_c, ret_l = bidir_prefix_scan(pc[0], pl[0])
    ssd_c, ssd_l = bidir_prefix_scan(pc[1], pl[1])

    def finish(proj, y_ret, y_ssd):
        _, _, g, z, xs = proj
        b, l = g.shape[:2]
        yr = bhld(y_ret).astype(jnp.float32)
        mu = jnp.mean(yr, axis=-1, keepdims=True)
        var = jnp.mean(jnp.square(yr - mu), axis=-1, keepdims=True)
        yr = ((yr - mu) * lax.rsqrt(var + EPS)).reshape(b, l, RET_WIDTH) * gn_w.astype(jnp.float32)
        yr = yr.astype(g.dtype) * jax.nn.silu(g)
        ys = bhld(y_ssd) + d_skip[:, None] * xs
        ys = rms_norm(ys.reshape(b, l, SSD_INNER) * jax.nn.silu(z), ssd_norm_w)
        return jnp.concatenate([yr, ys], axis=-1) @ w_out

    out_l = finish(pl, ret_l, ssd_l)
    out_c = finish(pc, ret_c, ssd_c) if need_ctx else None
    return out_c, out_l

def mla_project(h, w_in, q_norm_w, w_uq, kv_norm_w, w_ukv, rope):
    b, l, _ = h.shape
    c_q, c_kv, k_pe = jnp.split(h @ w_in, [Q_RANK, Q_RANK + KV_RANK], axis=-1)
    q = (rms_norm(c_q, q_norm_w) @ w_uq).reshape(b, l, MLA_HEADS, QK_NOPE + QK_ROPE)
    q_nope, q_pe = jnp.split(q, [QK_NOPE], axis=-1)
    kv = (rms_norm(c_kv, kv_norm_w) @ w_ukv).reshape(b, l, MLA_HEADS, QK_NOPE + V_HEAD)
    k_nope, v = jnp.split(kv, [QK_NOPE], axis=-1)
    k_pe = k_pe[:, :, None, :]
    if rope is not None:
        q_pe = apply_rope_2(q_pe, *rope)
        k_pe = apply_rope_2(k_pe, *rope)
    q = jnp.concatenate([q_nope, q_pe], axis=-1)
    k = jnp.concatenate([k_nope, jnp.broadcast_to(k_pe, (b, l, MLA_HEADS, QK_ROPE))], axis=-1)
    return q, k, v

def softmax_attention(q, k, v):
    s = jnp.einsum('bqhd,bkhd->bhqk', q, k).astype(jnp.float32) * ((QK_NOPE + QK_ROPE) ** -0.5)
    p = jax.nn.softmax(s, axis=-1)
    return jnp.einsum('bhqk,bkhd->bqhd', p.astype(v.dtype), v)

def mla_mixer(a_ctx, a_lat, w_in, q_norm_w, w_uq, kv_norm_w, w_ukv, w_out, rope, need_ctx):
    q_c, k_c, v_c = mla_project(a_ctx, w_in, q_norm_w, w_uq, kv_norm_w, w_ukv, None)
    q_l, k_l, v_l = mla_project(a_lat, w_in, q_norm_w, w_uq, kv_norm_w, w_ukv, rope)
    k_all = jnp.concatenate([k_c, k_l], axis=1)
    v_all = jnp.concatenate([v_c, v_l], axis=1)
    b, l = a_lat.shape[:2]
    nb = l // Q_BLOCK
    q_blocks = jnp.moveaxis(q_l.reshape(b, nb, Q_BLOCK, MLA_HEADS, QK_NOPE + QK_ROPE), 1, 0)
    o_l = lax.map(lambda qb: softmax_attention(qb, k_all, v_all), q_blocks)
    out_l = jnp.moveaxis(o_l, 0, 1).reshape(b, l, MLA_WIDTH) @ w_out
    out_c = None
    if need_ctx:
        out_c = softmax_attention(q_c, k_c, v_c).reshape(b, a_ctx.shape[1], MLA_WIDTH) @ w_out
    return out_c, out_l

def swiglu(h, w_gate, w_up, w_down):
    return (jax.nn.silu(h @ w_gate) * (h @ w_up)) @ w_down

def second_inputs(seed: int = 0) -> dict:
    key = jax.random.key(seed)
    ks = iter(jax.random.split(key, 40))
    f32 = jnp.float32

    def normal(shape, scale=1.0):
        return scale * jax.random.normal(next(ks), shape, f32)

    def dense(shape):
        return normal(shape, shape[-2] ** -0.5)

    def gain(shape):
        return 1.0 + normal(shape, 0.02)

    gammas = 1.0 - 2.0 ** (-5.0 - np.arange(RET_HEADS))
    base_logit = jnp.asarray(np.log(gammas / (1.0 - gammas)), dtype=f32)
    dt0 = jnp.exp(jax.random.uniform(next(ks), (N_EVEN, 2, SSD_HEADS), f32, np.log(1e-3), np.log(1e-1)))
    return {
        'x': normal((BATCH, SEQ, D_MODEL)),
        'c': normal((BATCH, D_MODEL)),
        'ctx': normal((BATCH, CTX_LEN, D_MODEL)),
        'c_ctx': normal((D_MODEL,)),
        'w_ada': dense((DEPTH_2, D_MODEL, 6 * D_MODEL)),
        'b_ada': normal((DEPTH_2, 6 * D_MODEL), 0.02),
        'w_ffn_gate': dense((DEPTH_2, D_MODEL, D_FF_2)),
        'w_ffn_up': dense((DEPTH_2, D_MODEL, D_FF_2)),
        'w_ffn_down': dense((DEPTH_2, D_FF_2, D_MODEL)),
        'ret_ssd_w_in': dense((N_EVEN, D_MODEL, IN0_WIDTH)),
        'ssd_conv_w': dense((N_EVEN, SSD_CONV, CONV_CH)),
        'ssd_conv_b': normal((N_EVEN, CONV_CH), 0.02),
        'ssd_dt_bias': dt0 + jnp.log(-jnp.expm1(-dt0)),
        'ssd_a_log': jnp.log(jax.random.uniform(next(ks), (N_EVEN, 2, SSD_HEADS), f32, 1.0, 16.0)),
        'ssd_d': gain((N_EVEN, SSD_HEADS)),
        'ssd_norm_w': gain((N_EVEN, SSD_INNER)),
        'ret_decay_logit': base_logit + normal((N_EVEN, 2, RET_HEADS), 0.1),
        'ret_gn_w': gain((N_EVEN, RET_WIDTH)),
        'ret_ssd_w_out': dense((N_EVEN, MIX0_WIDTH, D_MODEL)),
        'mla_w_in': dense((N_ODD, D_MODEL, IN1_WIDTH)),
        'mla_q_norm_w': gain((N_ODD, Q_RANK)),
        'mla_w_uq': dense((N_ODD, Q_RANK, MLA_HEADS * (QK_NOPE + QK_ROPE))),
        'mla_kv_norm_w': gain((N_ODD, KV_RANK)),
        'mla_w_ukv': dense((N_ODD, KV_RANK, MLA_HEADS * (QK_NOPE + V_HEAD))),
        'mla_w_out': dense((N_ODD, MLA_WIDTH, D_MODEL)),
        'final_norm_w': gain((D_MODEL,)),
    }

def second_block(x, c, ctx, c_ctx, w_ada, b_ada, w_ffn_gate, w_ffn_up, w_ffn_down,
              ret_ssd_w_in, ssd_conv_w, ssd_conv_b, ssd_dt_bias, ssd_a_log, ssd_d, ssd_norm_w,
              ret_decay_logit, ret_gn_w, ret_ssd_w_out,
              mla_w_in, mla_q_norm_w, mla_w_uq, mla_kv_norm_w, mla_w_ukv, mla_w_out, final_norm_w):
    lat_len = x.shape[1]
    rope_ret = axial_rope_tables(lat_len, RET_DK)
    rope_mla = axial_rope_tables(lat_len, QK_ROPE)
    h_ctx, h_lat = ctx, x
    for i in range(DEPTH_2):
        last = i == DEPTH_2 - 1
        j = i // 2
        m_lat = adaln_params(c, w_ada[i], b_ada[i])
        m_ctx = adaln_params(c_ctx[None], w_ada[i], b_ada[i])
        a_ctx = modulate_2(rms_norm(h_ctx), m_ctx[0], m_ctx[1])
        a_lat = modulate_2(rms_norm(h_lat), m_lat[0], m_lat[1])
        if i % 2 == 0:
            o_ctx, o_lat = retention_ssd_mixer(a_ctx, a_lat, ret_ssd_w_in[j], ssd_conv_w[j], ssd_conv_b[j],
                                               ssd_dt_bias[j], ssd_a_log[j], ssd_d[j], ssd_norm_w[j],
                                               ret_decay_logit[j], ret_gn_w[j], ret_ssd_w_out[j], rope_ret, not last)
        else:
            o_ctx, o_lat = mla_mixer(a_ctx, a_lat, mla_w_in[j], mla_q_norm_w[j], mla_w_uq[j], mla_kv_norm_w[j],
                                     mla_w_ukv[j], mla_w_out[j], rope_mla, not last)
        h_lat = h_lat + m_lat[2] * o_lat
        h_lat = h_lat + m_lat[5] * swiglu(modulate_2(rms_norm(h_lat), m_lat[3], m_lat[4]),
                                          w_ffn_gate[i], w_ffn_up[i], w_ffn_down[i])
        if not last:
            h_ctx = h_ctx + m_ctx[2] * o_ctx
            h_ctx = h_ctx + m_ctx[5] * swiglu(modulate_2(rms_norm(h_ctx), m_ctx[3], m_ctx[4]),
                                              w_ffn_gate[i], w_ffn_up[i], w_ffn_down[i])
    return rms_norm(h_lat, final_norm_w)


def setup_inputs(seed=0):
    out = dict(first_inputs(seed))
    for name, value in second_inputs(seed + 1).items():
        if name != "x":
            out[name + "_2"] = value
    return out


def reference(
    x, c, ctx, c_ctx, w_ada, b_ada, norm_mix, norm_ffn, w_in, gate_b, qk_conv_w, qk_conv_b,
    mlstm_norm, attn_sink, w_out, w_up, ffn_conv_w, ffn_conv_b, w_down, final_norm, c_2, ctx_2,
    c_ctx_2, w_ada_2, b_ada_2, w_ffn_gate_2, w_ffn_up_2, w_ffn_down_2, ret_ssd_w_in_2,
    ssd_conv_w_2, ssd_conv_b_2, ssd_dt_bias_2, ssd_a_log_2, ssd_d_2, ssd_norm_w_2,
    ret_decay_logit_2, ret_gn_w_2, ret_ssd_w_out_2, mla_w_in_2, mla_q_norm_w_2, mla_w_uq_2,
    mla_kv_norm_w_2, mla_w_ukv_2, mla_w_out_2, final_norm_w_2,
):
    x = first_block(
        x, c, ctx, c_ctx, w_ada, b_ada, norm_mix, norm_ffn, w_in, gate_b, qk_conv_w, qk_conv_b,
        mlstm_norm, attn_sink, w_out, w_up, ffn_conv_w, ffn_conv_b, w_down, final_norm,
    )
    return second_block(
        x, c_2, ctx_2, c_ctx_2, w_ada_2, b_ada_2, w_ffn_gate_2, w_ffn_up_2, w_ffn_down_2,
        ret_ssd_w_in_2, ssd_conv_w_2, ssd_conv_b_2, ssd_dt_bias_2, ssd_a_log_2, ssd_d_2,
        ssd_norm_w_2, ret_decay_logit_2, ret_gn_w_2, ret_ssd_w_out_2, mla_w_in_2,
        mla_q_norm_w_2, mla_w_uq_2, mla_kv_norm_w_2, mla_w_ukv_2, mla_w_out_2, final_norm_w_2,
    )


_drawn_inputs = setup_inputs


def setup_inputs(seed=0):
    import zlib

    import numpy as np

    out = dict(_drawn_inputs(seed))
    spreads = {}
    factors = {'norm_mix': 8.0,
     'norm_ffn': 6.684,
     'qk_conv_b': 43.503,
     'mlstm_norm': 8.0,
     'attn_sink': 8.0,
     'ffn_conv_b': 8.0,
     'ssd_conv_b_2': 6.353,
     'ssd_d_2': 8.0,
     'ssd_norm_w_2': 7.917,
     'ret_gn_w_2': 8.0,
     'mla_q_norm_w_2': 8.0,
     'mla_kv_norm_w_2': 8.0,
     'final_norm_w_2': 7.741}
    for name, (base, spread) in spreads.items():
        noise = np.random.default_rng([zlib.crc32(name.encode()), seed]).standard_normal(out[name].shape)
        drawn = base * np.exp(spread * noise) if base else spread * noise
        out[name] = jnp.asarray(drawn.astype(out[name].dtype))
    for name, factor in factors.items():
        out[name] = (out[name] * factor).astype(out[name].dtype)
    return out
```

```python
from contextlib import ExitStack

import numpy as np

import concourse.bass as bass
from concourse import mybir
from concourse.alu_op_type import AluOpType as ALU

ACT = mybir.ActivationFunctionType
F32 = mybir.dt.float32
AX_X = mybir.AxisListType.X

P = 128
D = 1024
KD = D // P
CTX = LAT = 256
TOK = CTX + LAT
TT = TOK // P
L0, L1 = CTX, TOK
EPS = 1e-6
NEG = -1e30
FF = 2816
KF = FF // P
SLOTS = 4
SLOT = KF * P
BANKS = 4

MH, MD = 4, 128
AH, AD = 8, 64
RH = 8
LH, LN, LR, LV = 16, 64, 32, 64
LQ = LN + LR



def constant_tables():
    p = np.arange(P)
    out = {"ident": np.eye(P), "ones": np.ones((P, P)),
           "upto": (p[:, None] <= p[None, :]), "from": (p[:, None] >= p[None, :]),
           "half_mean": (p[:, None] // 64 == p[None, :] // 64) / 64.0}
    s = np.arange(2)[None, :, None] * P + p[:, None, None]
    t = np.arange(256)[None, None, :]
    out["after"] = np.where(s <= t, 0.0, NEG)
    out["before"] = np.where(s >= t, 0.0, NEG)
    out["before_strict"] = np.where(s > t, 0.0, NEG)
    q = s
    win = np.where(np.abs(q - t) <= 128, 0.0, NEG)
    out["window"] = np.concatenate([np.zeros((P, 2, CTX)), win], axis=2)
    out["dist_f"] = np.maximum(t - s, 0)
    out["dist_b"] = np.maximum(s - t, 0)
    out["far_f"] = CTX + t - s
    out["far_b"] = CTX + s - t
    row, col = np.arange(LAT) // 64, np.arange(LAT) % 64

    def rope(dim_axis_freq, sign):
        ang = np.stack([np.float32(np.where(a, col, row)) * f for a, f in dim_axis_freq])
        return np.cos(ang), np.sin(ang) * np.asarray(sign)[:, None]

    inv = np.float32(10000.0) ** (-np.arange(16, dtype=np.float32) / np.float32(16))
    d = np.arange(P) % 64
    out["cos_a"], out["sin_a"] = rope([(x // 32, inv[x % 16]) for x in d],
                                      np.where(d % 32 < 16, -1.0, 1.0))
    out["cos_r"], out["sin_r"] = rope([((x % 32) // 16, inv[x % 16]) for x in d],
                                      np.where(d < 32, -1.0, 1.0))
    inv8 = np.float32(10000.0) ** (-np.arange(8, dtype=np.float32) / np.float32(8))
    d = np.arange(P) % 32
    out["cos_l"], out["sin_l"] = rope([((x % 16) // 8, inv8[x % 8]) for x in d],
                                      np.where(d < 16, -1.0, 1.0))
    return {k: np.asarray(v, np.float32).reshape(P, -1) for k, v in out.items()}


def packed(parts):
    at, n = {}, 0
    for name, a in parts.items():
        at[name] = (n, n + a.shape[1])
        n += a.shape[1]
    return at, n



class Phase:

    def __init__(self, name, units, width, products, counted=True):
        self.name, self.units, self.width, self.products = name, units, width, products
        self.counted = counted


def weight_phases():
    out = []

    def ffn(n, pair):
        out.append(Phase(f"up{n}", KF, KD * 256, 2))
        out.append(Phase(f"down{n}", KD, KF * P, 1))

    out.append(Phase("ada0", 24, KD * 256, 1, counted=False))
    out.append(Phase("vm", 2, KD * 256, TT))
    out.append(Phase("va_gates", 1, KD * 144, TT))
    out.append(Phase("km", 2, KD * 256, 2))
    out.append(Phase("qm", 2, KD * 256, 2))
    out.append(Phase("ka", 1, KD * 256, 2))
    out.append(Phase("qa", 2, KD * 256, 2))
    out.append(Phase("om", 2, KD * 256, 2))
    out.append(Phase("out0", 4, KD * 256, 2))
    ffn(0, True)
    out.append(Phase("ada1", 24, KD * 256, 1, counted=False))
    out.append(Phase("in1", 12, KD * 256, 2))
    out.append(Phase("vr", 2, KD * 256, TT))
    out.append(Phase("dt", 1, KD * 16, TT))
    out.append(Phase("out1", 4, KD * 256, 2))
    ffn(1, True)
    out.append(Phase("ada2", 24, KD * 256, 1, counted=False))
    out.append(Phase("cq", 3, KD * 256, 2))
    out.append(Phase("ckv", 1, KD * 256, 2))
    out.append(Phase("kpe", 1, KD * LR, 1))
    out.append(Phase("uq", 8, 6 * 2 * LQ, 1))
    out.append(Phase("uk", 2, 2 * 512, 8))
    out.append(Phase("uv", 2, 2 * 512, TT))
    out.append(Phase("out2", 4, KD * 256, 2))
    ffn(2, True)
    unit = product = taken = 0
    for f in out:
        f.first_unit, f.first_product, f.first_taken = unit, product, taken
        unit += f.units
        product += f.units * f.products
        taken += f.units * f.products * f.counted
    return {f.name: f for f in out}


class Chain:

    def __init__(self, engine, sem):
        self.engine, self.sem, self.n, self.moving = engine, sem, 0, 0

    def then(self, instruction):
        self.n += 1
        instruction.then_inc(self.sem, 1)
        self.engine.wait_ge(self.sem, self.moving + self.n)


def unit_rounds(engine, phase, body, chain=None, links=0):
    rounds, left = divmod(phase.units, SLOTS)
    if rounds > 1:
        n0 = chain.n if chain else 0
        with engine.Fori(0, rounds) as r:
            if chain:
                chain.moving = r * (links * SLOTS)
            for j in range(SLOTS):
                body(r * SLOTS + j, j)
        if chain:
            assert chain.n == n0 + links * SLOTS, (phase.name, chain.n - n0)
            chain.moving, chain.n = 0, n0 + rounds * links * SLOTS
    else:
        for j in range(rounds * SLOTS):
            body(j, j)
    for j in range(left):
        body(rounds * SLOTS + j, j)


def build(nc, dram, small_at, const_at, layers=3):
    ph = weight_phases()
    run = [n for n in ph]
    if layers < 3:
        run = run[:run.index("ada%d" % layers)]
    with ExitStack() as stack:
        def sb(name, shape):
            return stack.enter_context(nc.sbuf_tensor(name, shape, F32))

        def sem(name):
            return stack.enter_context(nc.semaphore(name))

        ring = sb("ring", [P, SLOTS, SLOT])
        X = sb("X", [P, KD, TOK])
        H = sb("H", [P, KD, TOK])
        small = sb("small", [P, max(b for _, b in small_at.values())])
        const = sb("const", [P, max(b for _, b in const_at.values())])
        mod = sb("mod", [P, 48, 2])
        gain = sb("gain", [P, 2, KD, 2])
        silu_c = sb("silu_c", [P, 2, KD, 2])
        std = sb("std", [P, TOK])
        inv = sb("inv", [P, TOK])
        arena = sb("arena", [P, 25280])
        bank = [stack.enter_context(nc.psum_tensor(f"bank{i}", [P, 512], F32)) for i in range(8)]

        def S(name, *dims):
            a, b = small_at[name]
            v = small[:, a:b]
            if dims:
                return v.rearrange("p (a b) -> p a b", a=dims[0])
            return v

        def C(name, a=None, parts=P):
            x, y = const_at[name]
            v = const[0:parts, x:y]
            return v.rearrange("p (a b) -> p a b", a=a) if a else v

        ident, ones = C("ident"), C("ones")

        class Carve:
            def __init__(self, at=0):
                self.at = at

            def __call__(self, *dims):
                n = int(np.prod(dims))
                v = arena[:, self.at:self.at + n]
                self.at += n
                assert self.at <= 25280, self.at
                if len(dims) == 2:
                    return v.rearrange("p (a b) -> p a b", a=dims[0])
                if len(dims) == 3:
                    return v.rearrange("p (a b c) -> p a b c", a=dims[0], b=dims[1])
                return v

        c = Carve()
        qm, km = c(MH, LAT), c(MH, TOK)
        vm, va, gates = c(TT, 512), c(TT, P), c(TT, 16)
        om, qa, ka = c(MH, LAT), c(4, LAT), c(2, TOK)
        att_at = c.at
        lf, gtmp = c(TT, 16), c(TT, 16)
        g_cum, g_bias = c(2, TT, MH), c(2, TT, MH)
        rows, run_max, top = c(4, LAT), c(2 * 512), c(2)
        conv = c(2, TOK)
        narg, ex = c(2, 3, LAT), c(2, TT, LAT)
        prob_m, den_a, den_e, hid = c(8, LAT), c(512), c(512), c(512)
        hm = c(MH, LAT)
        sq_m, sig = c(MH, LAT), c(MH, LAT)
        c = Carve()
        hidden = c(KF, TOK)
        up_tmp = c(4, TOK)
        c = Carve()
        t1 = c(24, TOK)
        vr, xt = c(TT, 512), c(TT, 512)
        dt, dtmp, la = c(TT, 16), c(TT, 16), c(TT, 16)
        gs, ngs = c(2, TT, RH), c(2, TT, RH)
        log_r, nega = c(16), c(16)
        grow = c(2, TOK)
        scr = c.at
        swap_r = c(KD, LAT)
        conv1 = c(2, TOK)
        c = Carve(scr)
        ea, eb = c(3, 512), c(3, 512)
        pr = [c(3, 512)]
        arg1 = c(512)
        c = Carve(scr)
        y_sq, y_sg = c(4, 512), c(4, 512)
        c = Carve()
        qh = c(LH, LAT)
        kh = c(LH, TOK)
        att2_at = c.at
        cq, ckv, kpe = c(6, LAT), c(2, TOK), c(TOK)
        kswap = c(2, 2 * LAT)
        sq_l = c(2, TOK)
        vl = c(TT, 1024)

        def attention_scratch(at):
            c = Carve(at)
            return dict(masked=[c(512), c(512)], prob=[c(512), c(512)],
                        turned=[c(4, LAT), c(4, LAT)],
                        peak=c(32), nmax=c(32), total=c(32), esink=c(32), nsink=c(8))

        att_s = {0: attention_scratch(att_at), 2: attention_scratch(att2_at)}

        names = ["small_in", "consts_in", "x_in", "ctx2_in", "out_done", "products", "taken", "silu_ready",
                 "mod_ready", "sq_ready", "sum_ready", "std_ready", "scaled", "h_ready", "x_ready",
                 "vector_order", "scalar_order", "pool_order", "tensor_order",
                 "conv_ready", "conv_act", "lf_in", "lf_exp", "lf_ready", "cum_ready", "cum_taken",
                 "rows_ready", "rows_taken", "ml_bcast", "ml_s", "ml_arg", "ml_e", "ml_p", "ml_num",
                 "ml_h", "ml_sq", "ml_sum", "ml_std", "y_ready", "rope_ready",
                 "att_s", "att_m", "att_e", "att_p", "att_t", "att_pt", "att_o", "att_y",
                 "up_act", "up_conv", "rt_s", "rt_arg", "rt_e", "rt_p", "rt_o", "rt_y",
                 "gn_in", "gn_sum", "gn_std", "gn_done", "gn_act", "swap_done",
                 "sd_t", "sd_tt", "sd_b", "sd_s", "sd_arg", "sd_e", "sd_p", "sd_o", "sd_y",
                 "sn_in", "sn_sum", "sn_std", "x_loaded", "kpe_in", "kpe_done", "lt_ready",
                 "lq_in", "lq_sum", "lq_std", "lq_done"]
        s = {n: sem(n) for n in names}
        full = [sem(f"slot_full{i}") for i in range(SLOTS)]

        def loaded(engine, f, u, j):
            g = f.first_unit + j
            engine.wait_ge(full[g % SLOTS], (u - j) * (16 // SLOTS) + 16 * (g // SLOTS + 1))

        def slot(f, j, k):
            v = ring[:, (f.first_unit + j) % SLOTS, 0:f.width]
            return v.rearrange("p (k n) -> p k n", k=k)

        def bank_of(f, j, i):
            return bank[(f.first_taken + j * f.products + i) % BANKS]

        def product_in(engine, f, u, j, i):
            engine.wait_ge(s["products"], u * f.products + (f.first_product + i + 1))

        block = stack.enter_context(nc.Block())

        @block.sync
        def _(sp):
            sp.dma_start(small[:, :], dram["small"]).then_inc(s["small_in"], 16)
            done = []
            for name in run:
                f = ph[name]
                for u in range(min(f.units, SLOTS)):
                    g = f.first_unit + u
                    if g >= SLOTS:
                        sp.wait_ge(s["products"], done[g - SLOTS])
                    sp.dma_start(ring[:, g % SLOTS, 0:f.width], dram[name][u]).then_inc(full[g % SLOTS], 16)
                    if g == 0:
                        sp.dma_start(const[:, :], dram["const"]).then_inc(s["consts_in"], 16)
                        sp.dma_start(X[:, :, L0:L1], dram["x"]).then_inc(s["x_in"], 16)
                        sp.dma_start(X[:, :, 0:L0], dram["ctx"]).then_inc(s["x_in"], 16)
                    done.append(f.first_product + (u + 1) * f.products)
                more = Phase(f.name, f.units - SLOTS, f.width, f.products)

                def load(u, j, f=f):
                    g = f.first_unit + j
                    sp.wait_ge(s["products"], u * f.products + (f.first_product + f.products))
                    sp.dma_start(ring[:, g % SLOTS, 0:f.width],
                                 dram[f.name][u + SLOTS]).then_inc(full[g % SLOTS], 16)

                if more.units > 0:
                    unit_rounds(sp, more, load)
                    done += [f.first_product + (u + 1) * f.products for u in range(SLOTS, f.units)]
            sp.wait_ge(s["x_ready"], 2 if layers == 3 else 1)
            if layers == 2:
                sp.wait_ge(s["taken"], ph["ada2"].first_taken)
            sp.dma_start(dram["out"], X[:, :, L0:L1]).then_inc(s["out_done"], 16)
            sp.wait_ge(s["out_done"], 16)

        @block.tensor
        def _(pe):
            norms = [0]

            def room(f, u, j, i):
                t = f.first_taken + i - BANKS + 1
                if t + j * f.products > 0:
                    pe.wait_ge(s["taken"], u * f.products + t)

            def peeled(f, body):
                unit_rounds(pe, f, body)

            def adaln(n):
                f = ph[f"ada{n}"]
                if n:
                    pe.wait_ge(s["mod_ready"], n)
                else:
                    pe.wait_ge(s["silu_ready"], 2)

                def body(u, j):
                    loaded(pe, f, u, j)
                    w = slot(f, j, KD)
                    for i in range(2):
                        for k in range(KD):
                            last = pe.matmul(bank[7][:, bass.ds(u * 4 + 2 * i, 2)],
                                             w[:, k, i * P:(i + 1) * P], silu_c[:, min(n, 1), k, :],
                                             start=(k == 0), stop=(k == KD - 1))
                    last.then_inc(s["products"], 1)

                unit_rounds(pe, f, body)

            def feature_sums(t0, t1):
                n = norms[0]
                norms[0] += 1
                if n == 0:
                    pe.wait_ge(s["consts_in"], 16)
                for k in range(KD):
                    pe.wait_ge(s["sq_ready"], n * KD + k + 1)
                    last = pe.matmul(bank[6][:, t0:t1], ones, H[:, k, t0:t1], start=(k == 0), stop=(k == KD - 1))
                last.then_inc(s["sum_ready"], 1)

            def linear(name, t0, t1, K=KD, src=None, M=P, per=1):
                f = ph[name]
                src = H if src is None else src

                def body(u, j):
                    loaded(pe, f, u, j)
                    w = slot(f, j, K)
                    for i in range(f.products):
                        room(f, u, j, i)
                        b = bank_of(f, j, i)
                        for q in range(per):
                            m = i * per + q
                            for k in range(K):
                                last = pe.matmul(b[0:M, q * (t1 - t0):(q + 1) * (t1 - t0)],
                                                 w[:, k, m * M:(m + 1) * M], src[:, k, t0:t1],
                                                 start=(k == 0), stop=(k == K - 1))
                        last.then_inc(s["products"], 1)

                unit_rounds(pe, f, body)

            def token_linear(name, K=KD, src=None):
                f = ph[name]
                src = H if src is None else src
                for u in range(f.units):
                    loaded(pe, f, u, u)
                    w = slot(f, u, K)
                    for i in range(TT):
                        room(f, u, u, i)
                        b = bank_of(f, u, i)
                        for k in range(K):
                            last = pe.matmul(b[:, 0:f.width // K], src[:, k, i * P:(i + 1) * P],
                                             w[:, k, :], start=(k == 0), stop=(k == K - 1))
                        last.then_inc(s["products"], 1)

            def cumulate(src, off, heads, b):
                for d in range(2):
                    order = (0, 1, 2, 3) if d == 0 else (1, 0, 3, 2)
                    for n, i in enumerate(order):
                        col = (d * TT + i) * heads
                        out = b[:, col:col + heads]
                        for e in range(n):
                            pe.matmul(out, ones, src[:, order[e], off[d]:off[d] + heads],
                                      start=(e == 0), stop=False)
                        last = pe.matmul(out, C("upto" if d == 0 else "from"),
                                         src[:, i, off[d]:off[d] + heads], start=(n == 0), stop=True)
                return last

            def mlstm():
                pe.wait_ge(s["lf_ready"], 1)
                cumulate(lf, (4, 12), MH, bank[6]).then_inc(s["cum_ready"], 1)
                pe.wait_ge(s["cum_taken"], 1)
                for d in range(2):
                    for i in range(TT):
                        pe.matmul(bank[d][0:MH, i * P:(i + 1) * P], g_bias[:, d, i, :], ident,
                                  start=True, stop=True)
                for d in range(2):
                    for i in range(2):
                        last = pe.matmul(bank[2][0:MH, d * LAT + i * P:d * LAT + (i + 1) * P],
                                         g_cum[:, d, 2 + i, :], ident, start=True, stop=True)
                last.then_inc(s["rows_ready"], 1)
                pe.wait_ge(s["rows_taken"], 1)

                def before(h):
                    pick = ident[0:MH, h:h + 1].to_broadcast([MH, P])
                    if h:
                        pe.wait_ge(s["ml_e"], 2 * h)
                        pe.wait_ge(s["ml_arg"], h)
                    for i in range(2):
                        last = pe.matmul(bank[i][:, :], pick, rows[0:MH, 2 * i:2 * i + 2, :],
                                         start=True, stop=True)
                    last.then_inc(s["ml_bcast"], 1)
                    if h:
                        pe.wait_ge(s["ml_p"], h)
                    for i in range(TT):
                        last = pe.matmul(bank[2 + i // 2][:, (i % 2) * LAT:(i % 2 + 1) * LAT],
                                         km[:, h, i * P:(i + 1) * P], qm[:, h, :], start=True, stop=True)
                    last.then_inc(s["ml_s"], 1)

                def sums(h):
                    pe.wait_ge(s["ml_p"], h + 1)
                    if h:
                        pe.wait_ge(s["ml_h"], h)
                    for d in range(2):
                        for i in range(TT):
                            pe.matmul(bank[4][:, d * LAT:(d + 1) * LAT], vm[:, i, h * MD:(h + 1) * MD],
                                      prob_m[:, d * TT + i, :], start=(i == 0), stop=(i == TT - 1))
                    for d in range(2):
                        for i in range(TT):
                            last = pe.matmul(bank[5][:, d * LAT:(d + 1) * LAT], ones,
                                             prob_m[:, d * TT + i, :], start=(i == 0), stop=(i == TT - 1))
                    last.then_inc(s["ml_num"], 1)

                for h in range(MH):
                    before(h)
                    sums(h)
                pe.wait_ge(s["ml_sq"], 1)
                for i in range(2):
                    last = pe.matmul(bank[i][:, :], ones, sq_m[:, 2 * i:2 * i + 2, :], start=True, stop=True)
                last.then_inc(s["ml_sum"], 1)

            def attention(n, a0, heads, q, k, v):
                count = 2 * heads

                def scores(a):
                    h, t = divmod(a, 2)
                    if a >= 2:
                        pe.wait_ge(s["att_e"], a0 + a - 1)
                    pe.matmul(bank[a % 2][:, :], q(h)[:, t * P:(t + 1) * P], k(h),
                              start=True, stop=True).then_inc(s["att_s"], 1)

                def turn(a):
                    pe.wait_ge(s["att_p"], a0 + a + 1)
                    if a >= 2:
                        pe.wait_ge(s["att_pt"], a0 + a - 1)
                    for i in range(TT):
                        last = pe.transpose(bank[2 + a % 2][:, i * P:(i + 1) * P],
                                            att_s[n]["prob"][a % 2][:, i * P:(i + 1) * P], ident)
                    last.then_inc(s["att_t"], 1)

                def values(h):
                    pe.wait_ge(s["att_pt"], a0 + 2 * h + 2)
                    if h >= 4 and h % 2 == 0:
                        pe.wait_ge(s["att_y"], a0 // 4 + h // 2 - 1)
                    for i in range(TT):
                        last = pe.matmul(bank[4 + (h // 2) % 2][64 * (h % 2):64 * (h % 2) + 64, 0:LAT],
                                         v(h, i), att_s[n]["turned"][h % 2][:, i, :],
                                         start=(i == 0), stop=(i == TT - 1))
                    last.then_inc(s["att_o"], 1)

                scores(0)
                scores(1)
                for a in range(count):
                    turn(a)
                    if a + 2 < count:
                        scores(a + 2)
                    if a % 2 and a > 2:
                        values(a // 2 - 1)
                values(heads - 1)

            def mixer1():
                def ret_scores(h):
                    t, p0, b = h // 2, 64 * (h % 2), 3 * (h % 2)
                    if h >= 2:
                        pe.wait_ge(s["rt_p"], h - 1)
                    for i in range(2):
                        pe.matmul(bank[b + i][:, :], t1[p0:p0 + 64, 4 + t, i * P:(i + 1) * P],
                                  t1[p0:p0 + 64, t, :], start=True, stop=True)
                    for i in range(2, TT):
                        last = pe.matmul(bank[b + 2][:, (i - 2) * LAT:(i - 1) * LAT],
                                         t1[p0:p0 + 64, 4 + t, i * P:(i + 1) * P],
                                         t1[p0:p0 + 64, t, L0:L1], start=True, stop=True)
                    last.then_inc(s["rt_s"], 1)

                def weighted(h, v, ready, taken, out, done):
                    t, p0 = h // 2, 64 * (h % 2)
                    pe.wait_ge(ready, h + 1)
                    if t >= 2 and h % 2 == 0:
                        pe.wait_ge(taken, t - 1)
                    b = bank[out + t % 2]
                    for i in range(TT):
                        lat = i >= 2
                        last = pe.matmul(b[p0:p0 + 64, L0 if lat else 0:L1], v[:, i, h * 64:(h + 1) * 64],
                                         pr[0][:, 2, (i - 2) * LAT:(i - 1) * LAT] if lat else pr[0][:, i, :],
                                         start=(i == 0), stop=(i == TT - 1))
                    last.then_inc(done, 1)

                pe.wait_ge(s["rope_ready"], 2)
                ret_scores(0)
                for h in range(RH):
                    if h + 1 < RH:
                        ret_scores(h + 1)
                    weighted(h, vr, s["rt_p"], s["rt_y"], 6, s["rt_o"])
                for r in range(2):
                    for i in range(4):
                        if r == 0:
                            pe.wait_ge(s["rt_y"], 4)
                        else:
                            pe.wait_ge(s["gn_in"], i + 1)
                        src = H[:, i, :] if r == 0 else y_sq[:, i, :]
                        pe.matmul(bank[i][:, :], C("half_mean"), src, start=True, stop=True)\
                          .then_inc(s["gn_sum"], 1)
                for i in range(TT):
                    pe.wait_ge(s["conv_act"], 8 + 8)
                    if i == 0:
                        pe.wait_ge(s["gn_done"], 1)
                    for j in range(4):
                        last = pe.transpose(bank[i][:, j * P:(j + 1) * P], t1[:, 16 + j, i * P:(i + 1) * P], ident)
                    last.then_inc(s["sd_t"], 1)
                pe.wait_ge(s["lf_ready"], 2)
                cumulate(la, (0, 8), RH, bank[7]).then_inc(s["cum_ready"], 1)
                pe.wait_ge(s["cum_taken"], 2)
                for d in range(2):
                    for i in range(TT):
                        last = pe.matmul(bank[5 + d][0:RH, i * P:(i + 1) * P], gs[:, d, i, :], ident,
                                         start=True, stop=True)
                last.then_inc(s["rows_ready"], 1)
                pe.wait_ge(s["rows_taken"], 2)
                pe.wait_ge(s["sd_tt"], TT)

                def ssd_scores(g):
                    if g:
                        pe.wait_ge(s["sd_p"], 4)
                    for i in range(2):
                        pe.matmul(bank[i][:, :], t1[:, 20 + g, i * P:(i + 1) * P], t1[:, 22 + g, :],
                                  start=True, stop=True)
                    for i in range(2, TT):
                        last = pe.matmul(bank[2][:, (i - 2) * LAT:(i - 1) * LAT],
                                         t1[:, 20 + g, i * P:(i + 1) * P], t1[:, 22 + g, L0:L1],
                                         start=True, stop=True)
                    last.then_inc(s["sd_s"], 1)

                def spread(h):
                    pick = ident[0:RH, h:h + 1].to_broadcast([RH, P])
                    if h:
                        pe.wait_ge(s["sd_arg"], 2 * h)
                    for d in range(2):
                        pe.matmul(bank[3 + d][:, :], pick, grow[0:RH, d, :], start=True, stop=True)\
                          .then_inc(s["sd_b"], 1)

                ssd_scores(0)
                spread(0)
                for h in range(RH):
                    if h + 1 < RH:
                        spread(h + 1)
                    weighted(h, xt, s["sd_p"], s["sd_y"], 5, s["sd_o"])
                    if h == 3:
                        ssd_scores(1)
                for i in range(4):
                    pe.wait_ge(s["sn_in"], i + 1)
                    last = pe.matmul(bank[7][:, :], ones, y_sq[:, i, :], start=(i == 0), stop=(i == 3))
                last.then_inc(s["sn_sum"], 1)

            def latent_norms():
                for i in range(6):
                    pe.wait_ge(s["lq_in"], i + 1)
                    last = pe.matmul(bank[6][:, 0:LAT], ones, H[:, i, L0:L1], start=(i == 0), stop=(i == 5))
                last.then_inc(s["lq_sum"], 1)
                for i in range(2):
                    pe.wait_ge(s["lq_in"], 7 + i)
                    last = pe.matmul(bank[7][:, :], ones, sq_l[:, i, :], start=(i == 0), stop=(i == 1))
                last.then_inc(s["lq_sum"], 1)
                pe.wait_ge(s["lq_done"], 1)

            def ffn(n, t0, t1):
                feature_sums(t0, t1)
                pe.wait_ge(s["h_ready"], norms_done())
                linear(f"up{n}", t0, t1)
                pe.wait_ge(s["taken"], ph[f"down{n}"].first_taken)
                linear(f"down{n}", t0, t1, K=KF, src=hidden)

            heads_ready = [0]

            def norms_done():
                heads_ready[0] += KD
                return heads_ready[0]

            adaln(0)
            feature_sums(0, TOK)
            pe.wait_ge(s["h_ready"], norms_done())
            token_linear("vm")
            token_linear("va_gates")
            linear("km", 0, TOK)
            linear("qm", L0, L1)
            linear("ka", 0, TOK)
            linear("qa", L0, L1)
            linear("om", L0, L1)
            mlstm()
            pe.wait_ge(s["rope_ready"], 1)
            pe.wait_ge(s["ml_std"], 1)
            attention(0, 0, AH,
                      lambda h: qa[64 * (h % 2):64 * (h % 2) + 64, h // 2, :],
                      lambda h: ka[64 * (h % 2):64 * (h % 2) + 64, h // 4, :],
                      lambda h, i: va[:, i, (h // 4) * 64:(h // 4) * 64 + 64])
            pe.wait_ge(s["att_y"], AH // 2)
            linear("out0", L0, L1)
            ffn(0, L0, L1)
            feature_sums(L0, L1)
            if layers == 1:
                return
            adaln(1)
            feature_sums(0, TOK)
            pe.wait_ge(s["h_ready"], norms_done())
            linear("in1", 0, TOK)
            token_linear("vr")
            token_linear("dt")
            mixer1()
            pe.wait_ge(s["y_ready"], 1)
            linear("out1", 0, TOK)
            ffn(1, 0, TOK)
            if layers == 2:
                return
            adaln(2)
            feature_sums(0, TOK)
            pe.wait_ge(s["h_ready"], norms_done())
            linear("cq", L0, L1)
            linear("ckv", 0, TOK)
            f = ph["kpe"]
            loaded(pe, f, 0, 0)
            room(f, 0, 0, 0)
            for k in range(KD):
                last = pe.matmul(bank_of(f, 0, 0)[LN:LQ, :], slot(f, 0, KD)[:, k, :], H[:, k, :],
                                 start=(k == 0), stop=(k == KD - 1))
            last.then_inc(s["products"], 1)
            latent_norms()
            linear("uq", 0, LAT, K=6, src=cq, M=LQ, per=2)
            pe.wait_ge(s["lq_done"], 2)
            linear("uk", 0, TOK, K=2, src=ckv, M=LN)
            token_linear("uv", K=2, src=ckv)
            pe.wait_ge(s["taken"], ph["out2"].first_taken)
            pe.wait_ge(s["kpe_done"], 1)
            attention(2, 2 * AH, LH, lambda h: qh[0:LQ, h, :], lambda h: kh[0:LQ, h, :],
                      lambda h, i: vl[:, i, h * LV:(h + 1) * LV])
            pe.wait_ge(s["att_y"], AH // 2 + LH // 2)
            linear("out2", L0, L1)
            ffn(2, L0, L1)
            feature_sums(L0, L1)

        @block.scalar
        def _(act):
            chain = Chain(act, s["scalar_order"])
            norms = [0]
            scaled = [0]

            def rms_std():
                norms[0] += 1
                t0, t1 = norm_tokens[norms[0] - 1]
                act.wait_ge(s["sum_ready"], norms[0])
                act.activation(std[:, t0:t1], bank[6][:, t0:t1], ACT.Sqrt, scale=1.0 / D, bias=EPS)\
                   .then_inc(s["std_ready"], 1)

            def modulate(which, both):
                for k in range(KD):
                    scaled[0] += 1
                    act.wait_ge(s["scaled"], scaled[0])
                    for t0, t1, m in ([(0, L0, 1)] if both else []) + [(L0, L1, 0)]:
                        last = act.activation(H[:, k, t0:t1], H[:, k, t0:t1], ACT.Identity,
                                              scale=gain[:, which, k, m:m + 1],
                                              bias=mod[:, 24 * which + k, m:m + 1])
                    last.then_inc(s["h_ready"], 1)

            norm_tokens = [(0, TOK), (L0, L1), (L0, L1), (0, TOK), (0, TOK), (0, TOK), (L0, L1), (L0, L1)]

            def log_sigmoid_parts(src_ready, x, cols):
                act.wait_ge(s["lf_in"], src_ready)
                chain.then(act.activation(x, x, ACT.Exp))
                act.activation(x, x, ACT.Ln, bias=1.0).then_inc(s["lf_exp"], 1)

            def attention(n, a0, heads, scale, sinks):
                m = att_s[n]

                def exps(a):
                    act.wait_ge(s["att_m"], a0 + a + 1)
                    if a >= 2:
                        act.wait_ge(s["att_t"], a0 + a - 1)
                    src = m["masked"][a % 2] if sinks else bank[a % 2][:, :]
                    e = act.activation(m["prob"][a % 2], src, ACT.Exp, bias=m["nmax"][:, a:a + 1],
                                       scale=scale, accum_out=m["total"][:, a:a + 1])
                    if sinks:
                        e = act.activation(m["esink"][:, a:a + 1], S("sink")[:, a // 2:a // 2 + 1],
                                           ACT.Exp, bias=m["nmax"][:, a:a + 1])
                    e.then_inc(s["att_e"], 1)

                def keep(a):
                    h, t = divmod(a, 2)
                    act.wait_ge(s["att_t"], a0 + a + 1)
                    if h >= 2:
                        act.wait_ge(s["att_o"], a0 // 2 + h - 1)
                    act.activation(m["turned"][h % 2][:, :, t * P:(t + 1) * P],
                                   bank[2 + a % 2][:, :].rearrange("p (k q) -> p k q", k=TT),
                                   ACT.Copy).then_inc(s["att_pt"], 1)

                exps(0)
                for a in range(2 * heads):
                    if a + 1 < 2 * heads:
                        exps(a + 1)
                    keep(a)

            act.wait_ge(s["small_in"], 16)
            for n in range(2):
                act.activation(silu_c[:, n, :, :], S(f"c{n}", KD), ACT.Silu).then_inc(s["silu_ready"], 1)
            rms_std()
            modulate(0, True)
            for i in range(8):
                act.wait_ge(s["taken"], ph["km"].first_taken + i + 1)
                if i < 4:
                    act.activation(km[:, i, :], conv[:, i % 2, :], ACT.Silu).then_inc(s["conv_act"], 1)
                else:
                    act.activation(qm[:, i - 4, :], conv[:, i % 2, 0:LAT], ACT.Silu).then_inc(s["conv_act"], 1)
            log_sigmoid_parts(1, gtmp, 64)
            for h in range(MH):
                act.wait_ge(s["ml_arg"], h + 1)
                if h:
                    act.wait_ge(s["ml_p"], h)
                for d in range(2):
                    for i in range(TT):
                        src = narg[:, d, 0, :] if i < 2 else narg[:, d, i - 1, :]
                        last = act.activation(ex[:, d, i, :], src, ACT.Exp, bias=g_bias[:, d, i, h:h + 1])
                last.then_inc(s["ml_e"], 1)
                if h:
                    act.wait_ge(s["ml_h"], h)
                act.activation(den_e, bank[1][:, :], ACT.Exp, scale=-1.0).then_inc(s["ml_e"], 1)
            act.wait_ge(s["ml_sum"], 1)
            for i in range(2):
                act.activation(sq_m[:, 2 * i:2 * i + 2, :], bank[i][:, :].rearrange("p (a b) -> p a b", a=2),
                               ACT.Sqrt, scale=1.0 / MD, bias=EPS)
            act.activation(sig, om, ACT.Sigmoid).then_inc(s["ml_std"], 1)
            attention(0, 0, AH, AD ** -0.5, True)
            rms_std()
            modulate(1, False)
            f = ph["up0"]

            def gelu(u, j):
                act.wait_ge(s["up_conv"], u + 1)
                act.activation(up_tmp[:, 2 + j % 2, 0:LAT], up_tmp[:, j % 2, 0:LAT], ACT.Gelu_apprx_tanh)\
                   .then_inc(s["up_act"], 1)

            unit_rounds(act, f, gelu)
            rms_std()
            if layers == 1:
                return

            def silu_gates(name, before, t0, t1):
                f = ph[name]

                def body(u, j):
                    product_in(act, f, u, j, 0)
                    act.wait_ge(s["taken"], u * 2 + (f.first_taken - 2))
                    act.activation(up_tmp[:, j % 2, t0:t1], bank_of(f, j, 0)[:, 0:t1 - t0], ACT.Silu)\
                       .then_inc(s["up_act"], 1)

                unit_rounds(act, f, body)

            rms_std()
            modulate(0, True)
            log_sigmoid_parts(2, dtmp[:, 0, :], 16)
            act.wait_ge(s["lf_in"], 3)
            chain.then(act.activation(dtmp, dtmp, ACT.Exp))
            act.activation(dtmp, dtmp, ACT.Ln, bias=1.0).then_inc(s["lf_exp"], 1)
            act.activation(nega, S("a_log"), ACT.Exp).then_inc(s["lf_exp"], 1)
            for i in range(8):
                act.wait_ge(s["conv_ready"], i + 1)
                act.activation(t1[:, 16 + i, :], conv1[:, i % 2, :], ACT.Silu).then_inc(s["conv_act"], 1)
            for h in range(RH):
                act.wait_ge(s["rt_arg"], h + 1)
                if h:
                    act.wait_ge(s["rt_p"], h)
                act.activation(ea[:, 0:2, 0:LAT], ea[:, 2, :].rearrange("p (a b) -> p a b", a=2), ACT.Exp)
                for d, dst in ((0, ea), (1, eb)):
                    last = act.activation(dst[:, 0:2, L0:L1], C("far_f" if d == 0 else "far_b", 2), ACT.Exp,
                                          scale=log_r[:, d * RH + h:d * RH + h + 1])
                last.then_inc(s["rt_e"], 1)
            for i in range(4):
                act.wait_ge(s["gn_sum"], 4 + i + 1)
                last = act.activation(y_sq[:, i, :], bank[i][:, :], ACT.Sqrt, bias=EPS)
            last.then_inc(s["gn_std"], 1)
            for i in range(4):
                act.activation(t1[:, 8 + i, :], t1[:, 8 + i, :], ACT.Silu)
                last = act.activation(t1[:, 12 + i, :], t1[:, 12 + i, :], ACT.Silu)
            last.then_inc(s["gn_act"], 1)
            for i in range(TT):
                act.wait_ge(s["sd_t"], i + 1)
                act.activation(xt[:, i, :], bank[i][:, :], ACT.Copy).then_inc(s["sd_tt"], 1)
            for h in range(RH):
                for d, e in ((0, ea), (1, eb)):
                    act.wait_ge(s["sd_arg"], 2 * h + d + 1)
                    for i in range(2):
                        act.activation(e[:, i, :], e[:, i, :], ACT.Exp, bias=ngs[:, d, i, h:h + 1])
                    for i in range(2, TT):
                        part = e[:, 2, (i - 2) * LAT:(i - 1) * LAT]
                        last = act.activation(part, part, ACT.Exp, bias=ngs[:, d, i, h:h + 1])
                    last.then_inc(s["sd_e"], 1)
            act.wait_ge(s["sn_sum"], 1)
            act.activation(std[:, :], bank[7][:, :], ACT.Sqrt, scale=1.0 / 512, bias=EPS).then_inc(s["sn_std"], 1)
            rms_std()
            modulate(1, True)
            silu_gates("up1", 0, 0, TOK)
            if layers == 2:
                return
            rms_std()
            modulate(0, True)
            act.wait_ge(s["lq_sum"], 1)
            act.activation(std[:, L0:L1], bank[6][:, 0:LAT], ACT.Sqrt, scale=1.0 / 768, bias=EPS)\
               .then_inc(s["lq_std"], 1)
            act.wait_ge(s["lq_sum"], 2)
            act.wait_ge(s["lq_done"], 1)
            act.activation(std[:, :], bank[7][:, :], ACT.Sqrt, scale=1.0 / 256, bias=EPS)\
               .then_inc(s["lq_std"], 1)
            act.wait_ge(s["kpe_in"], 1)
            act.activation(kh[LN:LQ, :, :], kpe[LN:LQ, :].unsqueeze(1).to_broadcast([LR, LH, TOK]),
                           ACT.Copy).then_inc(s["kpe_done"], 1)
            attention(2, 2 * AH, LH, LQ ** -0.5, False)
            rms_std()
            modulate(1, False)
            silu_gates("up2", 0, L0, L1)
            rms_std()

        @block.gpsimd
        def _(pool):
            if layers == 1:
                return
            pool.wait_ge(s["x_ready"], 1)
            pool.dma_start(X[:, :, 0:L0], dram["ctx_2"]).then_inc(s["ctx2_in"], 16)
            pool.wait_ge(s["taken"], ph["vr"].first_taken)
            for q in range(4):
                src = t1[32 * (q ^ 1):32 * (q ^ 1) + 32, 0:8, L0:L1]
                last = pool.tensor_copy(swap_r[32 * q:32 * q + 32, :, :], src)
            last.then_inc(s["swap_done"], 1)

        @block.vector
        def _(dve):
            chain = Chain(dve, s["vector_order"])
            then = chain.then
            norms = [0]
            scaled = [0]

            def adaln(n):
                f = ph[f"ada{n}"]
                dve.wait_ge(s["products"], f.first_product + f.units)
                bias = S(f"b_ada{n}")
                then(dve.tensor_tensor(mod[:, :, :], bank[7][:, 0:96].rearrange("p (a b) -> p a b", b=2),
                                       bias.unsqueeze(2).to_broadcast([P, 48, 2]), ALU.add))
                for w in range(2):
                    sc = mod[:, 24 * w + 8:24 * w + 16, :]
                    if n == 0:
                        g = S("norm_mix" if w == 0 else "norm_ffn").unsqueeze(2).to_broadcast([P, KD, 2])
                        last = dve.scalar_tensor_tensor(out=gain[:, w, :, :], in0=sc, scalar=1.0, in1=g,
                                                        op0=ALU.add, op1=ALU.mult)
                    else:
                        last = dve.tensor_scalar(gain[:, w, :, :], sc, 1.0, None, ALU.add)
                last.then_inc(s["mod_ready"], 1)
                dve.wait_ge(s["mod_ready"], n + 1)

            def inverse_rms(t0, t1):
                for k in range(KD):
                    dve.tensor_tensor(H[:, k, t0:t1], X[:, k, t0:t1], X[:, k, t0:t1], ALU.mult)\
                       .then_inc(s["sq_ready"], 1)
                norms[0] += 1
                dve.wait_ge(s["std_ready"], norms[0])
                then(dve.reciprocal(inv[:, t0:t1], std[:, t0:t1]))

            def norm(t0, t1):
                inverse_rms(t0, t1)
                for k in range(KD):
                    dve.tensor_tensor(H[:, k, t0:t1], X[:, k, t0:t1], inv[:, t0:t1], ALU.mult)\
                       .then_inc(s["scaled"], 1)

            def each_product(name, body, links=0):
                f = ph[name]

                def unit(u, j):
                    for i in range(f.products):
                        product_in(dve, f, u, j, i)
                        body(u, j, i, bank_of(f, j, i)).then_inc(s["taken"], 1)

                unit_rounds(dve, f, unit, chain, links)

            def copy(out, in_):
                return dve.tensor_scalar(out, in_, 1.0, None, ALU.mult)

            def conv_taps(dst, src, taps, bias, segs):
                half = len(taps) // 2
                d, x = (v.rearrange("p (a b) -> p a b", a=segs) for v in (dst, src))
                w = d.shape[2]
                then(dve.tensor_scalar(dst, src, taps[half], bias, ALU.mult, ALU.add))
                last = None
                for n, tap in enumerate(taps):
                    o = n - half
                    if o == 0:
                        continue
                    if last is not None:
                        then(last)
                    lo, hi = max(0, -o), w - max(0, o)
                    last = dve.scalar_tensor_tensor(out=d[:, :, lo:hi], in0=x[:, :, lo + o:hi + o],
                                                    scalar=tap, in1=d[:, :, lo:hi], op0=ALU.mult, op1=ALU.add)
                return last

            def log_sigmoid_arg(dst, x):
                dve.scalar_tensor_tensor(out=dst, in0=x, scalar=-1.0, in1=x, op0=ALU.mult, op1=ALU.min)\
                   .then_inc(s["lf_in"], 1)

            def mlstm():
                log_sigmoid_arg(gtmp, gates)
                dve.wait_ge(s["lf_exp"], 1)
                dve.scalar_tensor_tensor(out=lf, in0=gates, scalar=0.0, in1=gtmp, op0=ALU.min,
                                         op1=ALU.subtract).then_inc(s["lf_ready"], 1)
                dve.wait_ge(s["cum_ready"], 1)
                then(copy(g_cum, bank[6][:, 0:2 * TT * MH].rearrange("p (d i h) -> p d i h", d=2, i=TT)))
                for d in range(2):
                    last = dve.tensor_tensor(g_bias[:, d, :, :], gates[:, :, 8 * d:8 * d + 4], g_cum[:, d, :, :],
                                             ALU.subtract)
                last.then_inc(s["cum_taken"], 1)
                dve.wait_ge(s["rows_ready"], 1)
                then(copy(run_max[0:MH, 0:512], bank[0][0:MH, :]))
                then(copy(run_max[0:MH, 512:1024], bank[1][0:MH, :]))
                for d in range(2):
                    then(dve.reduce_max(top[0:MH, d:d + 1], run_max[0:MH, d * 512:d * 512 + L0], AX_X))
                then(dve.tensor_scalar(top[0:MH, :], top[0:MH, :], 0.0, None, ALU.max))
                b = run_max[0:MH, L0:L1]
                dve.tensor_tensor_scan(rows[0:MH, 0, :], b, b, top[0:MH, 0:1], ALU.max, ALU.max)
                b = run_max[0:MH, 1023:767:-1]
                then(dve.tensor_tensor_scan(rows[0:MH, 1, ::-1], b, b, top[0:MH, 1:2], ALU.max, ALU.max))
                dve.tensor_tensor(rows[0:MH, 2:4, :], rows[0:MH, 0:2, :],
                                  bank[2][0:MH, :].rearrange("p (a b) -> p a b", a=2), ALU.add)\
                   .then_inc(s["rows_taken"], 1)
                for h in range(MH):
                    dve.wait_ge(s["ml_bcast"], h + 1)
                    if h:
                        dve.wait_ge(s["ml_e"], 2 * h)
                    for d in range(2):
                        m = bank[0][:, d * LAT:(d + 1) * LAT]
                        dve.tensor_scalar(narg[:, d, 0, :], m, -1.0, None, ALU.mult)
                        last = dve.scalar_tensor_tensor(
                            out=narg[:, d, 1:3, :], in0=m.unsqueeze(1).to_broadcast([P, 2, LAT]), scalar=-1.0,
                            in1=C("after" if d == 0 else "before", 2), op0=ALU.mult, op1=ALU.add)
                    last.then_inc(s["ml_arg"], 1)
                    dve.wait_ge(s["ml_s"], h + 1)
                    dve.wait_ge(s["ml_e"], 2 * h + 1)
                    if h:
                        dve.wait_ge(s["ml_num"], h)
                    for d in range(2):
                        for i in range(2):
                            last = dve.scalar_tensor_tensor(
                                out=prob_m[:, d * TT + 2 * i:d * TT + 2 * i + 2, :],
                                in0=bank[2 + i][:, :].rearrange("p (a b) -> p a b", a=2), scalar=MD ** -0.5,
                                in1=ex[:, d, 2 * i:2 * i + 2, :], op0=ALU.mult, op1=ALU.mult)
                    last.then_inc(s["ml_p"], 1)
                    dve.wait_ge(s["ml_num"], h + 1)
                    then(dve.tensor_scalar(den_a, bank[5][:, :], -1.0, None, ALU.mult))
                    then(dve.tensor_tensor(den_a, den_a, bank[5][:, :], ALU.max))
                    dve.wait_ge(s["ml_e"], 2 * h + 2)
                    then(dve.tensor_tensor(den_a, den_a, den_e, ALU.max))
                    then(dve.reciprocal(den_a, den_a))
                    then(dve.tensor_tensor(hid, den_a, bank[4][:, :], ALU.mult))
                    dve.tensor_tensor(hm[:, h, :], hid[:, 0:LAT], hid[:, LAT:2 * LAT], ALU.add)\
                       .then_inc(s["ml_h"], 1)
                dve.wait_ge(s["ml_h"], MH)
                dve.tensor_tensor(sq_m, hm, hm, ALU.mult).then_inc(s["ml_sq"], 1)
                dve.wait_ge(s["ml_std"], 1)
                then(dve.reciprocal(sq_m, sq_m))
                then(dve.tensor_tensor(sig, sig, sq_m, ALU.mult))
                for h in range(MH):
                    last = dve.scalar_tensor_tensor(out=H[:, h, L0:L1], in0=hm[:, h, :],
                                                    scalar=S("mlstm_norm")[:, h:h + 1], in1=sig[:, h, :],
                                                    op0=ALU.mult, op1=ALU.mult)
                then(last)

            swap16 = list(range(16, 32)) + list(range(16))

            def attention(n, a0, heads, scale, sinks, tile0):
                m = att_s[n]
                if sinks:
                    then(dve.tensor_scalar(m["nsink"], S("sink"), -1.0, None, ALU.mult))

                def peaks(a):
                    h, t = divmod(a, 2)
                    dve.wait_ge(s["att_s"], a0 + a + 1)
                    if sinks:
                        if a >= 2:
                            dve.wait_ge(s["att_e"], a0 + a - 1)
                        then(dve.tensor_tensor_reduce(m["masked"][a % 2], bank[a % 2][:, :],
                                                      C("window", 2)[:, t, :], 1.0, -3e38, ALU.add, ALU.max,
                                                      m["peak"][:, a:a + 1]))
                        dve.tensor_scalar(m["nmax"][:, a:a + 1], m["peak"][:, a:a + 1], -scale,
                                          m["nsink"][:, h:h + 1], ALU.mult, ALU.min).then_inc(s["att_m"], 1)
                    else:
                        then(dve.reduce_max(m["peak"][:, a:a + 1], bank[a % 2][:, :], AX_X))
                        dve.tensor_scalar(m["nmax"][:, a:a + 1], m["peak"][:, a:a + 1], -scale, None,
                                          ALU.mult).then_inc(s["att_m"], 1)

                def divide(a):
                    dve.wait_ge(s["att_e"], a0 + a + 1)
                    one = m["total"][:, a:a + 1]
                    if sinks:
                        then(dve.tensor_tensor(one, one, m["esink"][:, a:a + 1], ALU.add))
                    then(dve.reciprocal(one, one))
                    dve.tensor_scalar(m["prob"][a % 2], m["prob"][a % 2], one, None, ALU.mult)\
                       .then_inc(s["att_p"], 1)

                def outputs(t):
                    dve.wait_ge(s["att_o"], a0 // 2 + 2 * t + 2)
                    copy(H[:, tile0 + t, L0:L1], bank[4 + t % 2][:, 0:LAT]).then_inc(s["att_y"], 1)

                peaks(0)
                for a in range(2 * heads):
                    if a + 1 < 2 * heads:
                        peaks(a + 1)
                    divide(a)
                    if a >= 7 and (a - 7) % 4 == 0:
                        outputs((a - 7) // 4)
                outputs(heads // 2 - 1)
                dve.wait_ge(s["att_y"], a0 // 4 + heads // 2)

            def residual(name, chunk, both):
                def body(u, j, i, b):
                    k = u * ph[name].products + i
                    for t0, t1, m in ([(0, L0, 1)] if both else []) + [(L0, L1, 0)]:
                        at = t0 if both else 0
                        g = mod[:, bass.ds(8 * chunk + k, 1), m]
                        x = X[:, bass.ds(k, 1), t0:t1].rearrange("p a b -> p (a b)")
                        last = dve.scalar_tensor_tensor(out=x, in0=b[:, at:at + t1 - t0], scalar=g,
                                                        in1=x, op0=ALU.mult, op1=ALU.add)
                    return last
                each_product(name, body)
                f = ph[name]
                dve.wait_ge(s["taken"], f.first_taken + f.units * f.products)

            def ffn0():
                norm(L0, L1)
                w, b = S("ffn_conv_w", 3), S("ffn_conv_b")
                f = ph["up0"]

                def unit(u, j):
                    product_in(dve, f, u, j, 0)
                    dst = up_tmp[:, j % 2, 0:LAT]
                    last = conv_taps(dst, bank_of(f, j, 0)[:, 0:LAT],
                                     [w[:, q, bass.ds(u, 1)] for q in range(3)], b[:, bass.ds(u, 1)], 1)
                    last.then_inc(s["up_conv"], 1)
                    dve.wait_ge(s["up_act"], u + 1)
                    product_in(dve, f, u, j, 1)
                    dve.tensor_tensor(hidden[:, bass.ds(u, 1), L0:L1].rearrange("p a b -> p (a b)"),
                                      up_tmp[:, 2 + j % 2, 0:LAT], bank_of(f, j, 1)[:, 0:LAT], ALU.mult)\
                       .then_inc(s["taken"], 2)

                unit_rounds(dve, f, unit, chain, 2)
                dve.wait_ge(s["taken"], f.first_taken + 2 * f.units)
                residual("down0", 5, False)

            def swiglu(n, t0, t1):
                norm(t0, t1)
                f = ph[f"up{n}"]

                def unit(u, j):
                    dve.wait_ge(s["up_act"], u + (KF * n + 1))
                    product_in(dve, f, u, j, 1)
                    dve.tensor_tensor(hidden[:, bass.ds(u, 1), t0:t1].rearrange("p a b -> p (a b)"),
                                      up_tmp[:, j % 2, t0:t1], bank_of(f, j, 1)[:, 0:t1 - t0], ALU.mult)\
                       .then_inc(s["taken"], 2)

                unit_rounds(dve, f, unit)
                dve.wait_ge(s["taken"], f.first_taken + 2 * f.units)
                residual(f"down{n}", 5, n == 1)

            def log_decays_r():
                lg = S("decay_logit")
                log_sigmoid_arg(dtmp[:, 0, :], lg)
                dve.wait_ge(s["lf_exp"], 2)
                then(dve.scalar_tensor_tensor(out=log_r, in0=lg, scalar=0.0, in1=dtmp[:, 0, :], op0=ALU.min,
                                              op1=ALU.subtract))

            def mixer1():
                each_product("in1", lambda u, j, i, b: copy(
                    t1[:, bass.ds(u * 2 + i, 1), :].rearrange("p a b -> p (a b)"), b[:, :]))
                dve.wait_ge(s["taken"], ph["vr"].first_taken)
                each_product("vr", lambda u, j, i, b: copy(vr[:, i, u * 256:(u + 1) * 256], b[:, 0:256]))
                each_product("dt", lambda u, j, i, b: dve.tensor_tensor(dt[:, i, :], b[:, 0:16], S("dt_bias"),
                                                                        ALU.add))
                dve.wait_ge(s["taken"], ph["out1"].first_taken)
                log_decays_r()
                log_sigmoid_arg(dtmp, dt)
                dve.wait_ge(s["lf_exp"], 4)
                then(dve.scalar_tensor_tensor(out=dt, in0=dt, scalar=0.0, in1=dtmp, op0=ALU.max, op1=ALU.add))
                dve.scalar_tensor_tensor(out=la, in0=dt, scalar=-1.0,
                                         in1=nega.unsqueeze(1).to_broadcast([P, TT, 16]),
                                         op0=ALU.mult, op1=ALU.mult).then_inc(s["lf_ready"], 1)
                w, b = S("ssd_conv_w", 5), S("ssd_conv_b")
                for i in range(8):
                    if i >= 2:
                        dve.wait_ge(s["conv_act"], 8 + i - 1)
                    conv_taps(conv1[:, i % 2, :], t1[:, 16 + i, :], [w[:, q, i:i + 1] for q in range(5)],
                              b[:, i:i + 1], 2).then_inc(s["conv_ready"], 1)
                dve.wait_ge(s["swap_done"], 1)
                lat = t1[:, 0:8, L0:L1]
                cs, sn = (C(x).unsqueeze(1).to_broadcast([P, KD, LAT]) for x in ("cos_r", "sin_r"))
                dve.tensor_tensor(swap_r, swap_r, sn, ALU.mult)
                then(dve.tensor_tensor(lat, lat, cs, ALU.mult))
                dve.tensor_tensor(lat, lat, swap_r, ALU.add).then_inc(s["rope_ready"], 1)
                dve.wait_ge(s["rope_ready"], 2)
                dve.wait_ge(s["conv_act"], 16)
                for h in range(RH):
                    if h:
                        dve.wait_ge(s["rt_e"], h)
                    rf, rb = log_r[:, h:h + 1], log_r[:, RH + h:RH + h + 1]
                    arg = ea[:, 2, :]
                    then(dve.tensor_scalar(arg, C("dist_b"), rb, None, ALU.mult))
                    dve.scalar_tensor_tensor(out=arg, in0=C("dist_f"), scalar=rf, in1=arg, op0=ALU.mult,
                                             op1=ALU.add).then_inc(s["rt_arg"], 1)
                    dve.wait_ge(s["rt_e"], h + 1)
                    then(dve.tensor_tensor(ea[:, 0:2, L0:L1], ea[:, 0:2, L0:L1], eb[:, 0:2, L0:L1], ALU.add))
                    dve.wait_ge(s["rt_s"], h + 1)
                    if h:
                        dve.wait_ge(s["rt_o"], h)
                    sb0 = 3 * (h % 2)
                    for i in range(2):
                        dve.scalar_tensor_tensor(out=pr[0][:, i, :], in0=bank[sb0 + i][:, :], scalar=0.125,
                                                 in1=ea[:, i, :], op0=ALU.mult, op1=ALU.mult)
                    dve.scalar_tensor_tensor(
                        out=pr[0][:, 2, :].rearrange("p (a b) -> p a b", a=2),
                        in0=bank[sb0 + 2][:, :].rearrange("p (a b) -> p a b", a=2), scalar=0.125,
                        in1=ea[:, 0:2, 0:LAT], op0=ALU.mult, op1=ALU.mult).then_inc(s["rt_p"], 1)
                    if h % 2 and h > 1:
                        dve.wait_ge(s["rt_o"], h - 1)
                        copy(H[:, h // 2 - 1, :], bank[6 + (h // 2 - 1) % 2][:, :]).then_inc(s["rt_y"], 1)
                dve.wait_ge(s["rt_o"], RH)
                copy(H[:, 3, :], bank[7][:, :]).then_inc(s["rt_y"], 1)
                dve.wait_ge(s["rt_y"], 4)
                for i in range(4):
                    dve.wait_ge(s["gn_sum"], i + 1)
                    then(dve.tensor_tensor(H[:, i, :], H[:, i, :], bank[i][:, :], ALU.subtract))
                    dve.tensor_tensor(y_sq[:, i, :], H[:, i, :], H[:, i, :], ALU.mult).then_inc(s["gn_in"], 1)
                dve.wait_ge(s["gn_std"], 1)
                then(dve.reciprocal(y_sq, y_sq))
                for i in range(4):
                    last = dve.scalar_tensor_tensor(out=y_sq[:, i, :], in0=y_sq[:, i, :],
                                                    scalar=S("gn_w")[:, i:i + 1], in1=H[:, i, :],
                                                    op0=ALU.mult, op1=ALU.mult)
                then(last)
                dve.wait_ge(s["gn_act"], 1)
                dve.tensor_tensor(H[:, 0:4, :], y_sq, t1[:, 8:12, :], ALU.mult).then_inc(s["gn_done"], 1)
                dve.wait_ge(s["gn_done"], 1)
                dve.wait_ge(s["cum_ready"], 2)
                cum = bank[7][:, 0:2 * TT * RH].rearrange("p (d i h) -> p d i h", d=2, i=TT)
                dve.tensor_scalar(ngs, cum, -1.0, None, ALU.mult)
                copy(gs, cum).then_inc(s["cum_taken"], 1)
                dve.wait_ge(s["rows_ready"], 2)
                copy(grow[0:RH, 0, :], bank[5][0:RH, :])
                copy(grow[0:RH, 1, :], bank[6][0:RH, :]).then_inc(s["rows_taken"], 1)
                for h in range(RH):
                    for d, e in ((0, ea), (1, eb)):
                        dve.wait_ge(s["sd_b"], 2 * h + d + 1)
                        g = bank[3 + d][:, :]
                        mask = C("after" if d == 0 else "before_strict", 2)
                        gl = g[:, L0:L1].unsqueeze(1).to_broadcast([P, 2, LAT])
                        gc = g[:, 0:L0].unsqueeze(1).to_broadcast([P, 2, LAT])
                        dve.tensor_tensor(e[:, 0:2, 0:L0], gc, mask, ALU.add)
                        copy(e[:, 0:2, L0:L1], gl)
                        dve.tensor_tensor(e[:, 2, :].rearrange("p (a b) -> p a b", a=2), gl, mask, ALU.add)\
                           .then_inc(s["sd_arg"], 1)

                    def parts(v, i):
                        return v[:, i, :] if i < 2 else v[:, 2, (i - 2) * LAT:(i - 1) * LAT]

                    dve.wait_ge(s["sd_e"], 2 * h + 1)
                    for i in range(TT):
                        last = dve.tensor_scalar(parts(ea, i), parts(ea, i), dt[:, i, h:h + 1], None, ALU.mult)
                    then(last)
                    dve.wait_ge(s["sd_e"], 2 * h + 2)
                    for i in range(TT):
                        last = dve.scalar_tensor_tensor(out=parts(eb, i), in0=parts(eb, i),
                                                        scalar=dt[:, i, RH + h:RH + h + 1], in1=parts(ea, i),
                                                        op0=ALU.mult, op1=ALU.add)
                    then(last)
                    dve.wait_ge(s["sd_s"], h // 4 + 1)
                    if h:
                        dve.wait_ge(s["sd_o"], h)
                    for i in range(3):
                        last = dve.tensor_tensor(pr[0][:, i, :], eb[:, i, :], bank[i][:, :], ALU.mult)
                    last.then_inc(s["sd_p"], 1)
                    dve.wait_ge(s["sd_p"], h + 1)
                    if h % 2 and h > 1:
                        dve.wait_ge(s["sd_o"], h - 1)
                        copy(H[:, 4 + h // 2 - 1, :], bank[5 + (h // 2 - 1) % 2][:, :]).then_inc(s["sd_y"], 1)
                dve.wait_ge(s["sd_o"], RH)
                copy(H[:, 7, :], bank[6][:, :]).then_inc(s["sd_y"], 1)
                dve.wait_ge(s["sd_y"], 4)
                for i in range(4):
                    y = H[:, 4 + i, :]
                    then(dve.scalar_tensor_tensor(out=y, in0=t1[:, 16 + i, :], scalar=S("ssd_d")[:, i:i + 1],
                                                  in1=y, op0=ALU.mult, op1=ALU.add))
                    then(dve.tensor_tensor(y, y, t1[:, 12 + i, :], ALU.mult))
                    dve.tensor_tensor(y_sq[:, i, :], y, y, ALU.mult).then_inc(s["sn_in"], 1)
                dve.wait_ge(s["sn_std"], 1)
                then(dve.reciprocal(inv[:, :], std[:, :]))
                for i in range(4):
                    y = H[:, 4 + i, :]
                    last = dve.scalar_tensor_tensor(out=y, in0=y, scalar=S("ssd_norm")[:, i:i + 1],
                                                    in1=inv[:, :], op0=ALU.mult, op1=ALU.mult)
                last.then_inc(s["y_ready"], 1)

            def mixer2():
                each_product("cq", lambda u, j, i, b: copy(cq[:, 2 * u + i, :], b[:, 0:LAT]))
                each_product("ckv", lambda u, j, i, b: copy(ckv[:, i, :], b[:, :]))
                each_product("kpe", lambda u, j, i, b: copy(kpe[LN:LQ, :], b[LN:LQ, :]))
                dve.wait_ge(s["taken"], ph["uq"].first_taken)
                for i in range(6):
                    dve.tensor_tensor(H[:, i, L0:L1], cq[:, i, :], cq[:, i, :], ALU.mult).then_inc(s["lq_in"], 1)
                for i in range(2):
                    dve.tensor_tensor(sq_l[:, i, :], ckv[:, i, :], ckv[:, i, :], ALU.mult).then_inc(s["lq_in"], 1)
                dve.wait_ge(s["lq_std"], 1)
                then(dve.reciprocal(inv[:, L0:L1], std[:, L0:L1]))
                for i in range(6):
                    last = dve.scalar_tensor_tensor(out=cq[:, i, :], in0=cq[:, i, :], scalar=S("q_norm")[:, i:i + 1],
                                                    in1=inv[:, L0:L1], op0=ALU.mult, op1=ALU.mult)
                last.then_inc(s["lq_done"], 1)
                dve.wait_ge(s["lq_std"], 2)
                dve.wait_ge(s["lq_done"], 1)
                then(dve.reciprocal(inv[:, :], std[:, :]))
                for i in range(2):
                    last = dve.scalar_tensor_tensor(out=ckv[:, i, :], in0=ckv[:, i, :],
                                                    scalar=S("kv_norm")[:, i:i + 1], in1=inv[:, :],
                                                    op0=ALU.mult, op1=ALU.mult)
                last.then_inc(s["lq_done"], 1)
                cs, sn = (C(x)[LN:LQ, :] for x in ("cos_l", "sin_l"))

                def rotate(v, sw, n):
                    c3, s3 = (x.unsqueeze(1).to_broadcast([LR, n, LAT]) for x in (cs, sn))
                    then(dve.stream_shuffle(sw, v, swap16))
                    dve.tensor_tensor(v, v, c3, ALU.mult)
                    then(dve.tensor_tensor(sw, sw, s3, ALU.mult))
                    return dve.tensor_tensor(v, v, sw, ALU.add)

                rotate(kpe[LN:LQ, L0:L1].unsqueeze(1), kswap[LN:LQ, 0, 0:LAT].unsqueeze(1), 1)\
                    .then_inc(s["kpe_in"], 1)

                f = ph["uq"]

                def q_unit(u, j):
                    product_in(dve, f, u, j, 0)
                    dst = qh[0:LQ, bass.ds(2 * u, 2), :].rearrange("p a b -> p (a b)")
                    copy(dst, bank_of(f, j, 0)[0:LQ, :]).then_inc(s["taken"], 1)

                unit_rounds(dve, f, q_unit)
                dve.wait_ge(s["taken"], f.first_taken + f.units)
                dve.wait_ge(s["kpe_in"], 1)
                for u in range(LH // 2):
                    then(rotate(qh[LN:LQ, 2 * u:2 * u + 2, :],
                                kswap[LN:LQ, u % 2, :].rearrange("p (a b) -> p a b", a=2), 2))
                each_product("uk", lambda u, j, i, b: copy(kh[0:LN, u * 8 + i, :], b[0:LN, :]))
                each_product("uv", lambda u, j, i, b: copy(vl[:, i, u * 512:(u + 1) * 512], b[:, :]))
                dve.wait_ge(s["taken"], ph["out2"].first_taken)
                attention(2, 2 * AH, LH, LQ ** -0.5, False, 0)

            dve.wait_ge(s["small_in"], 16)
            dve.wait_ge(s["consts_in"], 16)
            adaln(0)
            dve.wait_ge(s["x_in"], 32)
            norm(0, TOK)
            each_product("vm", lambda u, j, i, b: copy(vm[:, i, u * 256:(u + 1) * 256], b[:, 0:256]))

            def va_gates(u, j, i, b):
                copy(va[:, i, :], b[:, 0:P])
                return dve.tensor_tensor(gates[:, i, :], b[:, P:P + 16], S("gate_b"), ALU.add)

            each_product("va_gates", va_gates)
            w, cb = S("qk_conv_w", 3), S("qk_conv_b")
            for name, first, n in (("km", 4, TOK), ("qm", 0, LAT)):
                def convolve(u, j, i, b, first=first, n=n):
                    t = 2 * u + i
                    done = t if first else 4 + t
                    if done >= 2:
                        dve.wait_ge(s["conv_act"], done - 1)
                    return conv_taps(conv[:, done % 2, 0:n], b[:, 0:n],
                                     [w[:, q, first + t:first + t + 1] for q in range(3)],
                                     cb[:, first + t:first + t + 1], n // 256)
                each_product(name, convolve)
            each_product("ka", lambda u, j, i, b: copy(ka[:, i, :], b[:, :]))
            each_product("qa", lambda u, j, i, b: copy(qa[:, 2 * u + i, :], b[:, 0:LAT]))
            each_product("om", lambda u, j, i, b: copy(om[:, 2 * u + i, :], b[:, 0:LAT]))
            dve.wait_ge(s["taken"], ph["out0"].first_taken)
            swq, swk = hm, sq_m
            cs, sn = (C(x).unsqueeze(1) for x in ("cos_a", "sin_a"))
            for v, sw, n in ((qa, swq, 4), (ka[:, :, L0:L1], swk[:, 0:2, :], 2)):
                c3, s3 = cs.to_broadcast([P, n, LAT]), sn.to_broadcast([P, n, LAT])
                then(dve.stream_shuffle(sw, v, swap16))
                dve.tensor_tensor(v, v, c3, ALU.mult)
                then(dve.tensor_tensor(sw, sw, s3, ALU.mult))
                last = dve.tensor_tensor(v, v, sw, ALU.add)
            last.then_inc(s["rope_ready"], 1)
            dve.wait_ge(s["rope_ready"], 1)
            mlstm()
            attention(0, 0, AH, AD ** -0.5, True, 4)
            residual("out0", 2, False)
            ffn0()
            inverse_rms(L0, L1)
            for k in range(KD):
                x = X[:, k, L0:L1]
                last = dve.scalar_tensor_tensor(out=x, in0=x, scalar=S("final_norm")[:, k:k + 1],
                                                in1=inv[:, L0:L1], op0=ALU.mult, op1=ALU.mult)
            last.then_inc(s["x_ready"], 1)
            if layers > 1:
                adaln(1)
                dve.wait_ge(s["x_ready"], 1)
                dve.wait_ge(s["ctx2_in"], 16)
                norm(0, TOK)
                mixer1()
                residual("out1", 2, True)
                swiglu(1, 0, TOK)
            if layers > 2:
                adaln(2)
                norm(0, TOK)
                mixer2()
                residual("out2", 2, False)
                swiglu(2, L0, L1)
                inverse_rms(L0, L1)
                for k in range(KD):
                    x = X[:, k, L0:L1]
                    last = dve.scalar_tensor_tensor(out=x, in0=x, scalar=S("final_norm_2")[:, k:k + 1],
                                                    in1=inv[:, L0:L1], op0=ALU.mult, op1=ALU.mult)
                last.then_inc(s["x_ready"], 1)



def _columns(v):
    v = np.asarray(v)
    return v.reshape(-1, P).T


def _rows(v):
    return np.broadcast_to(np.asarray(v).reshape(1, -1), (P, np.asarray(v).size))


def _units(w, cols):
    w = np.asarray(w)
    k, n = w.shape
    return w.reshape(k // P, P, n // cols, cols).transpose(2, 1, 0, 3).reshape(n // cols, P, -1)


def _pairs(a, b):
    a, b = np.asarray(a), np.asarray(b)
    return np.concatenate([a.reshape(D, -1, P), b.reshape(D, -1, P)], axis=2).reshape(D, -1)


def _tokens(x):
    return np.asarray(x)[0].T.reshape(KD, P, -1).transpose(1, 0, 2)


def _layout(i):
    small = {
        "c0": np.stack([_columns(i["c"][0]), _columns(i["c_ctx"])], 2).reshape(P, -1),
        "c1": np.stack([_columns(i["c_2"][0]), _columns(i["c_ctx_2"])], 2).reshape(P, -1),
        "b_ada0": _columns(i["b_ada"][0]), "b_ada1": _columns(i["b_ada_2"][0]),
        "b_ada2": _columns(i["b_ada_2"][1]),
        "norm_mix": _columns(i["norm_mix"][0]), "norm_ffn": _columns(i["norm_ffn"][0]),
        "gate_b": _rows(i["gate_b"][0]),
        "qk_conv_w": np.concatenate([_columns(t) for t in i["qk_conv_w"][0]], 1),
        "qk_conv_b": _columns(i["qk_conv_b"][0]), "mlstm_norm": _columns(i["mlstm_norm"][0]),
        "sink": _rows(i["attn_sink"][0]),
        "ffn_conv_w": np.concatenate([_columns(t) for t in i["ffn_conv_w"][0]], 1),
        "ffn_conv_b": _columns(i["ffn_conv_b"][0]), "final_norm": _columns(i["final_norm"]),
        "ssd_conv_w": np.concatenate([_columns(t) for t in i["ssd_conv_w_2"][0]], 1),
        "ssd_conv_b": _columns(i["ssd_conv_b_2"][0]), "dt_bias": _rows(i["ssd_dt_bias_2"][0]),
        "a_log": _rows(i["ssd_a_log_2"][0]), "ssd_d": _columns(np.repeat(i["ssd_d_2"][0], 64)),
        "ssd_norm": _columns(i["ssd_norm_w_2"][0]), "decay_logit": _rows(i["ret_decay_logit_2"][0]),
        "gn_w": _columns(i["ret_gn_w_2"][0]), "q_norm": _columns(i["mla_q_norm_w_2"][0]),
        "kv_norm": _columns(i["mla_kv_norm_w_2"][0]), "final_norm_2": _columns(i["final_norm_w_2"]),
    }
    const = constant_tables()
    w0, w1, w2 = (np.asarray(i[n][0]) for n in ("w_in", "ret_ssd_w_in_2", "mla_w_in_2"))
    m = MH * MD
    q0, k0, v0, o0, g0, qa0, ka0, va0 = np.split(w0, np.cumsum([m, m, m, m, 16, 512, 128]), axis=1)
    arrays = {"x": _tokens(i["x"]), "ctx": _tokens(i["ctx"]), "ctx_2": _tokens(i["ctx_2"]),
              "ada0": _units(i["w_ada"][0], 256), "ada1": _units(i["w_ada_2"][0], 256),
              "ada2": _units(i["w_ada_2"][1], 256),
              "vm": _units(v0, 256), "va_gates": _units(np.concatenate([va0, g0], 1), 144),
              "km": _units(k0, 256), "qm": _units(q0, 256),
              "ka": _units(np.concatenate([ka0[:, :64], ka0[:, :64], ka0[:, 64:], ka0[:, 64:]], 1), 256),
              "qa": _units(qa0, 256), "om": _units(o0, 256), "out0": _units(i["w_out"][0], 256)}
    up = np.asarray(i["w_up"][0])
    arrays["up0"] = _units(_pairs(up[:, :FF], up[:, FF:]), 256)
    arrays["down0"] = _units(i["w_down"][0], P)
    q1, k1, v1, g1, z1, xbc1, dt1 = np.split(w1, np.cumsum([512] * 5 + [1024]), axis=1)
    arrays["in1"] = _units(np.concatenate([q1, k1, g1, z1, xbc1], 1), 256)
    arrays["vr"] = _units(v1, 256)
    arrays["dt"] = _units(dt1, 16)
    arrays["out1"] = _units(i["ret_ssd_w_out_2"][0], 256)
    for n in range(2):
        arrays[f"up{n + 1}"] = _units(_pairs(i["w_ffn_gate_2"][n], i["w_ffn_up_2"][n]), 256)
        arrays[f"down{n + 1}"] = _units(i["w_ffn_down_2"][n], P)
    arrays["cq"] = _units(w2[:, :768], 256)
    arrays["ckv"] = _units(w2[:, 768:1024], 256)
    arrays["kpe"] = _units(w2[:, 1024:], LR)
    arrays["uq"] = _units(i["mla_w_uq_2"][0], 2 * LQ)
    ukv = np.asarray(i["mla_w_ukv_2"][0]).reshape(256, LH, LN + LV)
    arrays["uk"] = _units(ukv[:, :, :LN].reshape(256, -1), 512)
    arrays["uv"] = _units(ukv[:, :, LN:].reshape(256, -1), 512)
    arrays["out2"] = _units(i["mla_w_out_2"][0], 256)
    arrays["small"] = np.concatenate(list(small.values()), 1)
    arrays["const"] = np.concatenate(list(const.values()), 1)
    return arrays, packed(small)[0], packed(const)[0]


def kernel(**inputs):
    import concourse.bacc as bacc
    from concourse.bass_utils import run_bass_kernel_spmd

    arrays, small_at, const_at = _layout({k: np.asarray(v) for k, v in inputs.items()})
    nc = bacc.Bacc("TRN2", target_bir_lowering=False, num_devices=1)
    dram, feed = {}, {}
    for name, a in arrays.items():
        a = np.ascontiguousarray(a)
        feed[f"in_{name}"] = a
        dram[name] = nc.dram_tensor(f"in_{name}", a.shape, mybir.dt.from_np(a.dtype), kind="ExternalInput").ap()
    dram["out"] = nc.dram_tensor("out", (P, KD, LAT), F32, kind="ExternalOutput").ap()
    build(nc, dram, small_at, const_at)
    r = run_bass_kernel_spmd(nc, [feed], core_ids=[0])
    y = np.asarray(r.results[0]["out"])
    return y.transpose(2, 1, 0).reshape(1, LAT, D)
```

```python
from contextlib import ExitStack

import numpy as np

import concourse.bass as bass
from concourse import mybir
from concourse.alu_op_type import AluOpType as ALU

ACT = mybir.ActivationFunctionType
F32 = mybir.dt.float32
F32R = mybir.dt.float32r
AX_X = mybir.AxisListType.X

P = 128
D = 1024
KD = D // P
CTX = LAT = 256
TOK = CTX + LAT
TT = TOK // P
L0, L1 = CTX, TOK
EPS = 1e-6
NEG = -1e30
FF = 2816
KF = FF // P
SLOTS = 3
SLOT = KF // 2 * P
BANKS = 3
ROUND = 6
ARENA = 24064
AHEAD = 2

MH, MD = 4, 128
AH, AD = 8, 64
RH = 8
LH, LN, LR, LV = 16, 64, 32, 64
LQ = LN + LR



def constant_tables():
    p = np.arange(P)
    s = np.arange(2)[None, :, None] * P + p[:, None, None]
    t = np.arange(256)[None, None, :]
    upto, since = p[:, None] <= p[None, :], p[:, None] >= p[None, :]
    after = np.where(s <= t, 0.0, NEG)
    window = np.where(np.abs(s - t) <= 128, 0.0, NEG)
    row, col = np.arange(LAT) // 64, np.arange(LAT) % 64

    def rope(axes, pairs, signs):
        inv = np.float32(10000.0) ** (-np.arange(pairs, dtype=np.float32) / np.float32(pairs))
        ang = np.stack([np.float32(np.where(a, col, row)) * inv[x % pairs] for x, a in enumerate(axes)])
        return np.cos(ang), np.sin(ang) * signs[:, None]

    cos_a, sin_a = rope(p % 64 // 32, 16, np.where(p % 32 < 16, -1.0, 1.0))
    cos_r, sin_r = rope(p % 32 // 16, 16, np.where(p % 64 < 32, -1.0, 1.0))
    cos_l, sin_l = rope(p % 16 // 8, 8, np.where(p % 32 < 16, -1.0, 1.0))
    tables = (
        {"upto": upto, "since": since, "after": after, "before": np.where(s >= t, 0.0, NEG),
         "window": np.concatenate([np.zeros((P, 2, CTX)), window], axis=2),
         "cos": cos_a, "sin": sin_a},
        {"upto": upto, "since": since, "half_mean": (p[:, None] // 64 == p[None, :] // 64) / 64.0,
         "after": after, "before": np.where(s > t, 0.0, NEG),
         "dist_f": np.maximum(t - s, 0), "dist_b": np.maximum(s - t, 0),
         "far_f": CTX + t - s, "far_b": CTX + s - t, "cos": cos_r, "sin": sin_r},
        {"cos": cos_l, "sin": sin_l},
        {"ident": np.eye(P), "ones": np.ones((P, P))},
    )
    return [{k: np.asarray(v, np.float32).reshape(P, -1) for k, v in x.items()} for x in tables]


def packed(parts):
    at, n = {}, 0
    for name, a in parts.items():
        at[name] = (n, n + a.shape[1])
        n += a.shape[1]
    return at, n



class Phase:

    def __init__(self, name, units, width, steps=1, takes=1, split=True):
        self.name, self.units, self.width = name, units, width
        self.steps, self.takes, self.split = steps, takes, split

    def steps_after(self, u):
        if self.name in ("vm", "vr"):
            u = u // 2 * 2 + 1
        return self.first_step + (u + 1) * self.steps


def weight_phases():
    out = []

    def ffn(n):
        out.append(Phase(f"up{n}", 2 * KF, KD * P))
        out.append(Phase(f"down{n}", 2 * KD, SLOT, takes=0.5))

    def ada(n):
        out.append(Phase(f"ada{n}", 48, KD * P, takes=0, split=False))

    ada(0)
    out.append(Phase("va_gates", 1, KD * 144, TT, TT))
    out.append(Phase("vm", 4, KD * P, 2, 2))
    out.append(Phase("km", 4, KD * P))
    out.append(Phase("qm", 4, KD * P))
    out.append(Phase("ka", 2, KD * P))
    out.append(Phase("qa", 4, KD * P))
    out.append(Phase("om", 4, KD * P))
    out.append(Phase("out0", 8, KD * P))
    ffn(0)
    ada(1)
    out.append(Phase("in1", 24, KD * P))
    out.append(Phase("vr", 4, KD * P, 2, 2))
    out.append(Phase("dt", 1, KD * 16, TT, TT))
    out.append(Phase("out1", 8, KD * P))
    ffn(1)
    ada(2)
    out.append(Phase("cq", 6, KD * P))
    out.append(Phase("ckv", 2, KD * P))
    out.append(Phase("kpe", 1, KD * P))
    out.append(Phase("uq", 8, 6 * 2 * LQ))
    out.append(Phase("uk", 2, 2 * 512, 4, 4))
    out.append(Phase("uv", 2, 2 * 512, TT, TT))
    out.append(Phase("out2", 8, KD * P))
    ffn(2)
    unit = step = taken = split = 0
    for f in out:
        f.first_unit, f.first_step, f.first_taken, f.first_split = unit, step, int(taken), split
        unit += f.units
        step += f.units * f.steps
        taken += f.units * f.takes
        split += f.units * f.split
    return {f.name: f for f in out}


class Chain:

    def __init__(self, engine, sem):
        self.engine, self.sem, self.n, self.moving = engine, sem, 0, 0

    def then(self, instruction):
        self.n += 1
        instruction.then_inc(self.sem, 1)
        self.engine.wait_ge(self.sem, self.moving + self.n)


def unit_rounds(engine, start, stop, body, chain=None, links=0):
    rounds, left = divmod(stop - start, ROUND)
    if rounds > 1:
        n0 = chain.n if chain else 0
        with engine.Fori(0, rounds) as r:
            if chain:
                chain.moving = r * links
            for j in range(start, start + ROUND):
                body(r * ROUND + j, j, r)
        if chain:
            assert chain.n == n0 + links, chain.n - n0
            chain.moving, chain.n = 0, n0 + rounds * links
    else:
        for u in range(start, start + rounds * ROUND):
            body(u, u, 0)
    for u in range(start + rounds * ROUND, stop):
        body(u, u, 0)


def build(nc, dram, small_at, tables_at, layers=3):
    ph = weight_phases()
    run = [n for n in ph]
    if layers < 3:
        run = run[:run.index("ada%d" % layers)]
    with ExitStack() as stack:
        def sb(name, shape):
            return stack.enter_context(nc.sbuf_tensor(name, shape, F32))

        def sbr(name, shape):
            return stack.enter_context(nc.sbuf_tensor(name, shape, F32R))

        def sem(name):
            return stack.enter_context(nc.semaphore(name))

        raw = sb("raw", [P, SLOTS, SLOT])
        w_hi = sbr("w_hi", [P, SLOTS, SLOT])
        w_lo = sbr("w_lo", [P, SLOTS, SLOT])
        X = sb("X", [P, KD, TOK])
        small = sb("small", [P, max(b for _, b in small_at.values())])
        fixed = sb("fixed", [P, 2 * P])
        mod = sb("mod", [P, 48, 2])
        gain = sb("gain", [P, 2, KD, 2])
        silu_c = sb("silu_c", [P, 2, KD, 2])
        std = sb("std", [P, TOK])
        sq_sum = sb("sq_sum", [P, TOK])
        with nc.sbuf_tensor("arena", [P, ARENA], F32) as arena:
            pass
        with (nc.sbuf_tensor("hidden_hi", [P, KF, TOK], F32R) as hidden_hi,
              nc.sbuf_tensor("hidden_lo", [P, KF, TOK], F32R) as hidden_lo,
              nc.sbuf_tensor("up_tmp", [P, 3, TOK], F32) as up_tmp):
            pass
        stack.enter_context(nc.sbuf_tensor("arena_end", [P, ARENA], F32))
        crow = arena[:, 0:2 * 3 * P].rearrange("p (g n) -> p g n", g=2)
        with nc.sbuf_tensor("scratch", [P, 2 * KD * TOK], F32) as scratch:
            pass
        with (nc.sbuf_tensor("cq_hi", [P, 6, LAT], F32R) as cq_hi,
              nc.sbuf_tensor("cq_lo", [P, 6, LAT], F32R) as cq_lo,
              nc.sbuf_tensor("ckv_hi", [P, 2, TOK], F32R) as ckv_hi,
              nc.sbuf_tensor("ckv_lo", [P, 2, TOK], F32R) as ckv_lo):
            pass
        h_hi, h_lo = sbr("h_hi", [P, KD, TOK]), sbr("h_lo", [P, KD, TOK])
        work = sb("work", [P, 3, TOK])
        bank = [stack.enter_context(nc.psum_tensor(f"bank{i}", [P, 512], F32)) for i in range(8)]

        def S(name, *dims):
            a, b = small_at[name]
            v = small[:, a:b]
            if dims:
                return v.rearrange("p (a b) -> p a b", a=dims[0])
            return v

        def tables(layer):
            at = tables_at[layer]
            start = ARENA - max(b for _, b in at.values())

            def C(name, a=None):
                v = arena[:, start + at[name][0]:start + at[name][1]]
                return v.rearrange("p (a b) -> p a b", a=a) if a else v
            return C, arena[:, start:]

        (C0, room0), (C1, room1), (C2, room2) = (tables(i) for i in range(3))
        ident, ones = fixed[:, 0:P], fixed[:, P:2 * P]

        class Carve:
            def __init__(self, tensor, at=0, limit=ARENA):
                self.tensor, self.at, self.limit = tensor, at, limit

            def __call__(self, *dims):
                n = int(np.prod(dims))
                v = self.tensor[:, self.at:self.at + n]
                self.at += n
                assert self.at <= self.limit, self.at
                if len(dims) == 2:
                    return v.rearrange("p (a b) -> p a b", a=dims[0])
                if len(dims) == 3:
                    return v.rearrange("p (a b c) -> p a b c", a=dims[0], b=dims[1])
                return v

        def attention_memory(c):
            return dict(masked=[c(512), c(512)], prob=[c(512), c(512)],
                        turned=[c(4, LAT), c(4, LAT)],
                        peak=c(32), nmax=c(32), total=c(32), esink=c(32), nsink=c(8))

        def limit(layer):
            return ARENA - max(b for _, b in tables_at[layer].values())

        c = Carve(arena, 0, limit(0))
        qm, km = c(MH, LAT), c(MH, TOK)
        vm, va, gates = c(TT, 512), c(TT, P), c(TT, 16)
        om, qa, ka = c(MH, LAT), c(4, LAT), c(2, TOK)
        att0 = attention_memory(Carve(arena, c.at, limit(0)))
        lf, gtmp = c(TT, 16), c(TT, 16)
        g_cum, g_bias = c(2, TT, MH), c(2, TT, MH)
        rows, run_max, top = c(4, LAT), c(2 * 512), c(2)
        conv = c(2, TOK)
        narg = c(2, 3, LAT)
        den_a, den_e, hid = c(512), c(512), c(512)
        hm, sq_m, sig = c(MH, LAT), c(MH, LAT), c(MH, LAT)
        c = Carve(scratch)
        ex, prob_m = c(2, TT, LAT), c(2 * TT, LAT)
        c = Carve(arena, 0, limit(1))
        t1 = c(24, TOK)
        vr, y1 = c(TT, 512), c(8, TOK)
        dt, dtmp, la = c(TT, 16), c(TT, 16), c(TT, 16)
        gs, ngs = c(2, TT, RH), c(2, TT, RH)
        log_r, nega = c(16), c(16)
        conv1 = c(2, TOK)
        c = Carve(scratch, 0, 8192)
        xt, grow = c(TT, 512), c(2, TOK)
        swap_r = Carve(scratch, c.at)(KD, LAT)
        y_sq = Carve(scratch, c.at)(4, 512)
        ea, eb, pr = c(3, 512), c(3, 512), c(3, 512)
        c = Carve(arena, 0, limit(2))
        qh, kh, vl = c(LH, LAT), c(LH, TOK), c(TT, 1024)
        att2 = attention_memory(Carve(arena, c.at, limit(2)))
        cq, ckv, kpe = c(6, LAT), c(2, TOK), c(TOK)
        kswap = c(2, 2 * LAT)
        sq_l = c(2, TOK)

        def cq_sq(i):
            return scratch[:, 5632 + i * LAT:5632 + (i + 1) * LAT]


        names = [
            "small_in", "fixed_in", "x_in", "ctx2_in", "tables_in", "out_done",
            "rounded", "split", "steps", "taken",
            "silu_ready", "rows_in", "columns", "mod_ready",
            "squared", "added", "sums_in", "sum_ready", "std_ready", "h_work", "h_round", "h_split",
            "x_ready", "y_ready",
            "vector_order", "scalar_order",
            "conv_act", "lf_in", "lf_exp", "lf_ready", "cum_ready", "cum_taken", "rows_ready",
            "rows_taken", "ml_bcast", "ml_s", "ml_arg", "ml_e", "ml_p", "ml_num", "ml_h", "ml_sq",
            "ml_sum", "ml_std", "ml_y", "rope_ready",
            "att_s", "att_m", "att_e", "att_p", "att_t", "att_pt", "att_o", "att_y",
            "up_conv", "up_act", "hid_done",
            "swap_done", "conv_ready", "rt_s", "rt_arg", "rt_e", "rt_p", "rt_o", "rt_y",
            "gn_in", "gn_sum", "gn_std", "gn_act", "gn_done", "sd_t", "sd_tt", "sd_b", "sd_s",
            "sd_arg", "sd_e", "sd_p", "sd_o", "sd_y", "sn_in", "sn_sum", "sn_std",
            "lq_in", "lq_sum", "lq_std", "lq_done", "kpe_in", "kpe_done"]
        s = {n: sem(n) for n in names}
        full = [sem(f"slot_full{i}") for i in range(SLOTS)]

        all_units = [(ph[n], u) for n in run for u in range(ph[n].units)]
        split_units = [(f, u) for f, u in all_units if f.split]

        def loaded(engine, f, j, r):
            g = f.first_unit + j
            engine.wait_ge(full[g % SLOTS], r * (16 * ROUND // SLOTS) + 16 * (g // SLOTS + 1))

        def raw_slot(f, j):
            return raw[:, (f.first_unit + j) % SLOTS, 0:f.width]

        def part_slot(part, f, j, k=None):
            v = part[:, (f.first_split + j) % SLOTS, 0:f.width]
            return v.rearrange("p (k n) -> p k n", k=k) if k else v

        def bank_of(t):
            return bank[t % BANKS]

        block = stack.enter_context(nc.Block())

        @block.sync
        def _(sp):
            sp.dma_start(small[:, :], dram["small"]).then_inc(s["small_in"], 16)

            def load(g):
                f, u = all_units[g]
                if g >= SLOTS:
                    f0, u0 = all_units[g - SLOTS]
                    if f0.split:
                        sp.wait_ge(s["split"], f0.first_split + u0 + 1)
                    else:
                        sp.wait_ge(s["steps"], f0.steps_after(u0))
                sp.dma_start(raw_slot(f, u), dram[f.name][u]).then_inc(full[g % SLOTS], 16)

            def load_in_phase(f):
                def body(u, j, r):
                    if f.split:
                        sp.wait_ge(s["split"], r * ROUND + (f.first_split + j - SLOTS + 1))
                    else:
                        sp.wait_ge(s["steps"], r * ROUND + (f.first_step + j - SLOTS + 1))
                    sp.dma_start(raw_slot(f, j), dram[f.name][u]).then_inc(full[(f.first_unit + j) % SLOTS], 16)
                return body

            g = 0
            for name in run:
                f = ph[name]
                for u in range(min(f.units, SLOTS)):
                    load(g + u)
                    if g + u == 0:
                        sp.dma_start(fixed[:, :], dram["table3"]).then_inc(s["fixed_in"], 16)
                    if g + u == 2:
                        sp.dma_start(X[:, :, L0:L1], dram["x"]).then_inc(s["x_in"], 16)
                        sp.dma_start(X[:, :, 0:L0], dram["ctx"]).then_inc(s["x_in"], 16)
                        sp.dma_start(room0, dram["table0"]).then_inc(s["tables_in"], 16)
                if f.units > SLOTS:
                    unit_rounds(sp, SLOTS, f.units, load_in_phase(f))
                g += f.units
            sp.wait_ge(s["x_ready"], 2 if layers == 3 else 1)
            if layers == 2:
                sp.wait_ge(s["taken"], ph["ada2"].first_taken)
            sp.dma_start(dram["out"], X[:, :, L0:L1]).then_inc(s["out_done"], 16)
            sp.wait_ge(s["out_done"], 16)

        @block.tensor
        def _(pe):
            norms = [0]
            h_ready = [0]

            def room(t, r=0, per_round=0):
                if t >= BANKS:
                    pe.wait_ge(s["taken"], r * per_round + (t - BANKS + 1))

            def three(out, w_h, w_l, x_h, x_l, first, last):
                pe.matmul(out, w_h, x_h, start=first, stop=False)
                pe.matmul(out, w_h, x_l, start=False, stop=False)
                return pe.matmul(out, w_l, x_h, start=False, stop=last)

            def adaln(n):
                f = ph[f"ada{n}"]
                pe.wait_ge(s["silu_ready"], min(n, 1) + 1)
                if n:
                    pe.wait_ge(s["mod_ready"], n)
                else:
                    pe.wait_ge(s["fixed_in"], 16)

                def body(u, j, r):
                    loaded(pe, f, j, r)
                    w = raw_slot(f, j).rearrange("p (k n) -> p k n", k=KD)
                    g, i = j // 3, j % 3
                    for k in range(KD):
                        last = pe.matmul(bank[6 + g][0:2, i * P:(i + 1) * P], silu_c[:, min(n, 1), k, :],
                                         w[:, k, :], start=(k == 0), stop=(k == KD - 1))
                    last.then_inc(s["steps"], 1)
                    if j == ROUND - 1:
                        for g in range(2):
                            pe.wait_ge(s["rows_in"], r * 2 + (16 * n + g + 1))
                            for i in range(3):
                                last = pe.matmul(bank[5][:, bass.ds(r * 12 + (6 * g + 2 * i), 2)],
                                                 crow[0:2, g, i * P:(i + 1) * P], ident[0:2, 0:2],
                                                 start=True, stop=True)
                        last.then_inc(s["columns"], 1)

                unit_rounds(pe, 0, f.units, body)

            def feature_sums(t0, t1):
                norms[0] += 1
                pe.wait_ge(s["sums_in"], norms[0])
                if norms[0] == 1:
                    pe.wait_ge(s["fixed_in"], 16)
                pe.matmul(bank[4][:, t0:t1], ones, sq_sum[:, t0:t1], start=True, stop=True)\
                  .then_inc(s["sum_ready"], 1)

            def next_h():
                base = h_ready[0]
                h_ready[0] += KD
                return lambda k: pe.wait_ge(s["h_split"], base + k + 1)

            def linear(name, t0, t1, K=KD, hi=None, lo=None, M=P, per=1, gate=None, halves=1):
                f = ph[name]
                hi, lo = (h_hi, h_lo) if hi is None else (hi, lo)
                n = t1 - t0

                def body(u, j, r):
                    pe.wait_ge(s["split"], r * ROUND + (f.first_split + j + 1))
                    w_h, w_l = (part_slot(x, f, j, K * per) for x in (w_hi, w_lo))
                    if per > 1:
                        w_h, w_l = (part_slot(x, f, j).rearrange("p (k n) -> p k n", k=K) for x in (w_hi, w_lo))
                    half = j % halves
                    t = f.first_taken + j // halves
                    if half == 0:
                        room(t, r, ROUND // halves)
                    for q in range(per):
                        for k in range(K):
                            if gate and u is j and j < halves:
                                gate(half * K + k)
                            last = three(bank_of(t)[0:M, q * n:(q + 1) * n],
                                         w_h[:, k, q * M:(q + 1) * M], w_l[:, k, q * M:(q + 1) * M],
                                         hi[:, half * K + k, t0:t1], lo[:, half * K + k, t0:t1],
                                         half == 0 and k == 0, half == halves - 1 and k == K - 1)
                    last.then_inc(s["steps"], 1)

                if gate:
                    for u in range(halves):
                        body(u, u, 0)
                    unit_rounds(pe, halves, f.units, body)
                else:
                    unit_rounds(pe, 0, f.units, body)

            def token_linear(name, K=KD, hi=None, lo=None, gate=None):
                f = ph[name]
                hi, lo = (h_hi, h_lo) if hi is None else (hi, lo)
                pair = 2 if f.steps == 2 else 1
                for u in range(0, f.units, pair):
                    pe.wait_ge(s["split"], f.first_split + u + pair)
                    if pair == 2:
                        a, b = ((f.first_split + u + i) % SLOTS for i in range(2))
                        two = slice(a, b + 1) if b > a else slice(a, None, -a)
                        w_h, w_l = (x[:, two, 0:f.width].rearrange("p s (k n) -> p k s n", k=K) for x in (w_hi, w_lo))
                    else:
                        w_h, w_l = (part_slot(x, f, u, K) for x in (w_hi, w_lo))
                    cols = pair * f.width // K
                    for i in range(TT):
                        t = f.first_taken + u * f.takes + i
                        room(t)
                        out = bank_of(t)[:, 0:cols]
                        if pair == 2:
                            out = out.rearrange("p (s n) -> p s n", s=2)
                        for k in range(K):
                            if gate and u == 0 and i == 0:
                                gate(k)
                            last = three(out, hi[:, k, i * P:(i + 1) * P], lo[:, k, i * P:(i + 1) * P],
                                         w_h[:, k], w_l[:, k], k == 0, k == K - 1)
                        last.then_inc(s["steps"], 1)

            def cumulate(src, off, heads, b, C):
                for d in range(2):
                    order = (0, 1, 2, 3) if d == 0 else (1, 0, 3, 2)
                    for n, i in enumerate(order):
                        col = (d * TT + i) * heads
                        out = b[:, col:col + heads]
                        for e in range(n):
                            pe.matmul(out, ones, src[:, order[e], off[d]:off[d] + heads],
                                      start=(e == 0), stop=False)
                        last = pe.matmul(out, C("upto" if d == 0 else "since"),
                                         src[:, i, off[d]:off[d] + heads], start=(n == 0), stop=True)
                return last

            def mlstm():
                pe.wait_ge(s["lf_ready"], 1)
                cumulate(lf, (4, 12), MH, bank[6], C0).then_inc(s["cum_ready"], 1)
                pe.wait_ge(s["cum_taken"], 1)
                for d in range(2):
                    for i in range(TT):
                        pe.matmul(bank[d][0:MH, i * P:(i + 1) * P], g_bias[:, d, i, :], ident,
                                  start=True, stop=True)
                for d in range(2):
                    for i in range(2):
                        last = pe.matmul(bank[2][0:MH, d * LAT + i * P:d * LAT + (i + 1) * P],
                                         g_cum[:, d, 2 + i, :], ident, start=True, stop=True)
                last.then_inc(s["rows_ready"], 1)
                pe.wait_ge(s["rows_taken"], 1)

                def before(h):
                    pick = ident[0:MH, h:h + 1].to_broadcast([MH, P])
                    if h:
                        pe.wait_ge(s["ml_e"], 2 * h)
                        pe.wait_ge(s["ml_arg"], h)
                    for i in range(2):
                        last = pe.matmul(bank[i][:, :], pick, rows[0:MH, 2 * i:2 * i + 2, :],
                                         start=True, stop=True)
                    last.then_inc(s["ml_bcast"], 1)
                    if h:
                        pe.wait_ge(s["ml_p"], h)
                    for i in range(TT):
                        last = pe.matmul(bank[2 + i // 2][:, (i % 2) * LAT:(i % 2 + 1) * LAT],
                                         km[:, h, i * P:(i + 1) * P], qm[:, h, :], start=True, stop=True)
                    last.then_inc(s["ml_s"], 1)

                def sums(h):
                    pe.wait_ge(s["ml_p"], h + 1)
                    if h:
                        pe.wait_ge(s["ml_h"], h)
                    for d in range(2):
                        for i in range(TT):
                            pe.matmul(bank[4][:, d * LAT:(d + 1) * LAT], vm[:, i, h * MD:(h + 1) * MD],
                                      prob_m[:, d * TT + i, :], start=(i == 0), stop=(i == TT - 1))
                    for d in range(2):
                        for i in range(TT):
                            last = pe.matmul(bank[5][:, d * LAT:(d + 1) * LAT], ones,
                                             prob_m[:, d * TT + i, :], start=(i == 0), stop=(i == TT - 1))
                    last.then_inc(s["ml_num"], 1)

                for h in range(MH):
                    before(h)
                    sums(h)
                pe.wait_ge(s["ml_sq"], 1)
                for i in range(2):
                    last = pe.matmul(bank[i][:, :], ones, sq_m[:, 2 * i:2 * i + 2, :], start=True, stop=True)
                last.then_inc(s["ml_sum"], 1)

            def attention(m, a0, heads, q, k, v):
                count = 2 * heads

                def scores(a):
                    h, t = divmod(a, 2)
                    if a >= 2:
                        pe.wait_ge(s["att_e"], a0 + a - 1)
                    pe.matmul(bank[a % 2][:, :], q(h)[:, t * P:(t + 1) * P], k(h),
                              start=True, stop=True).then_inc(s["att_s"], 1)

                def turn(a):
                    pe.wait_ge(s["att_p"], a0 + a + 1)
                    if a >= 2:
                        pe.wait_ge(s["att_pt"], a0 + a - 1)
                    for i in range(TT):
                        last = pe.transpose(bank[2 + a % 2][:, i * P:(i + 1) * P],
                                            m["prob"][a % 2][:, i * P:(i + 1) * P], ident)
                    last.then_inc(s["att_t"], 1)

                def values(h):
                    pe.wait_ge(s["att_pt"], a0 + 2 * h + 2)
                    if h >= 4 and h % 2 == 0:
                        pe.wait_ge(s["att_y"], a0 // 4 + h // 2 - 1)
                    for i in range(TT):
                        last = pe.matmul(bank[4 + (h // 2) % 2][64 * (h % 2):64 * (h % 2) + 64, 0:LAT],
                                         v(h, i), m["turned"][h % 2][:, i, :],
                                         start=(i == 0), stop=(i == TT - 1))
                    last.then_inc(s["att_o"], 1)

                scores(0)
                scores(1)
                for a in range(count):
                    turn(a)
                    if a + 2 < count:
                        scores(a + 2)
                    if a % 2 and a > 2:
                        values(a // 2 - 1)
                values(heads - 1)

            def mixer1():
                def ret_scores(h):
                    t, p0, b = h // 2, 64 * (h % 2), 3 * (h % 2)
                    if h >= 2:
                        pe.wait_ge(s["rt_p"], h - 1)
                    for i in range(2):
                        pe.matmul(bank[b + i][:, :], t1[p0:p0 + 64, 4 + t, i * P:(i + 1) * P],
                                  t1[p0:p0 + 64, t, :], start=True, stop=True)
                    for i in range(2, TT):
                        last = pe.matmul(bank[b + 2][:, (i - 2) * LAT:(i - 1) * LAT],
                                         t1[p0:p0 + 64, 4 + t, i * P:(i + 1) * P],
                                         t1[p0:p0 + 64, t, L0:L1], start=True, stop=True)
                    last.then_inc(s["rt_s"], 1)

                def weighted(h, v, ready, taken, out, done):
                    t, p0 = h // 2, 64 * (h % 2)
                    pe.wait_ge(ready, h + 1)
                    if t >= 2 and h % 2 == 0:
                        pe.wait_ge(taken, t - 1)
                    b = bank[out + t % 2]
                    for i in range(TT):
                        lat = i >= 2
                        last = pe.matmul(b[p0:p0 + 64, L0 if lat else 0:L1], v[:, i, h * 64:(h + 1) * 64],
                                         pr[:, 2, (i - 2) * LAT:(i - 1) * LAT] if lat else pr[:, i, :],
                                         start=(i == 0), stop=(i == TT - 1))
                    last.then_inc(done, 1)

                pe.wait_ge(s["rope_ready"], 2)
                ret_scores(0)
                for h in range(RH):
                    if h + 1 < RH:
                        ret_scores(h + 1)
                    weighted(h, vr, s["rt_p"], s["rt_y"], 6, s["rt_o"])
                for r in range(2):
                    for i in range(4):
                        if r == 0:
                            pe.wait_ge(s["rt_y"], 4)
                        else:
                            pe.wait_ge(s["gn_in"], i + 1)
                        src = y1[:, i, :] if r == 0 else y_sq[:, i, :]
                        pe.matmul(bank[i][:, :], C1("half_mean"), src, start=True, stop=True)\
                          .then_inc(s["gn_sum"], 1)
                for i in range(TT):
                    pe.wait_ge(s["conv_act"], 8 + 8)
                    if i == 0:
                        pe.wait_ge(s["gn_done"], 1)
                    for j in range(4):
                        last = pe.transpose(bank[i][:, j * P:(j + 1) * P], t1[:, 16 + j, i * P:(i + 1) * P], ident)
                    last.then_inc(s["sd_t"], 1)
                pe.wait_ge(s["lf_ready"], 2)
                cumulate(la, (0, 8), RH, bank[7], C1).then_inc(s["cum_ready"], 1)
                pe.wait_ge(s["cum_taken"], 2)
                for d in range(2):
                    for i in range(TT):
                        last = pe.matmul(bank[5 + d][0:RH, i * P:(i + 1) * P], gs[:, d, i, :], ident,
                                         start=True, stop=True)
                last.then_inc(s["rows_ready"], 1)
                pe.wait_ge(s["rows_taken"], 2)
                pe.wait_ge(s["sd_tt"], TT)

                def ssd_scores(g):
                    if g:
                        pe.wait_ge(s["sd_p"], 4)
                    for i in range(2):
                        pe.matmul(bank[i][:, :], t1[:, 20 + g, i * P:(i + 1) * P], t1[:, 22 + g, :],
                                  start=True, stop=True)
                    for i in range(2, TT):
                        last = pe.matmul(bank[2][:, (i - 2) * LAT:(i - 1) * LAT],
                                         t1[:, 20 + g, i * P:(i + 1) * P], t1[:, 22 + g, L0:L1],
                                         start=True, stop=True)
                    last.then_inc(s["sd_s"], 1)

                def spread(h):
                    pick = ident[0:RH, h:h + 1].to_broadcast([RH, P])
                    if h:
                        pe.wait_ge(s["sd_arg"], 2 * h)
                    for d in range(2):
                        pe.matmul(bank[3 + d][:, :], pick, grow[0:RH, d, :], start=True, stop=True)\
                          .then_inc(s["sd_b"], 1)

                ssd_scores(0)
                spread(0)
                for h in range(RH):
                    if h + 1 < RH:
                        spread(h + 1)
                    weighted(h, xt, s["sd_p"], s["sd_y"], 5, s["sd_o"])
                    if h == 3:
                        ssd_scores(1)
                for i in range(4):
                    pe.wait_ge(s["sn_in"], i + 1)
                    last = pe.matmul(bank[7][:, :], ones, y_sq[:, i, :], start=(i == 0), stop=(i == 3))
                last.then_inc(s["sn_sum"], 1)

            def latent_norms():
                for i in range(6):
                    pe.wait_ge(s["lq_in"], i + 1)
                    last = pe.matmul(bank[6][:, 0:LAT], ones, cq_sq(i), start=(i == 0), stop=(i == 5))
                last.then_inc(s["lq_sum"], 1)
                for i in range(2):
                    pe.wait_ge(s["lq_in"], 7 + i)
                    last = pe.matmul(bank[7][:, :], ones, sq_l[:, i, :], start=(i == 0), stop=(i == 1))
                last.then_inc(s["lq_sum"], 1)

            def ffn(n, t0, t1):
                feature_sums(t0, t1)
                linear(f"up{n}", t0, t1, gate=next_h())
                linear(f"down{n}", t0, t1, K=KF // 2, hi=hidden_hi, lo=hidden_lo, halves=2,
                       gate=lambda k: pe.wait_ge(s["hid_done"], KF * n + k + 1))

            adaln(0)
            feature_sums(0, TOK)
            token_linear("va_gates", gate=next_h())
            token_linear("vm")
            linear("km", 0, TOK)
            linear("qm", L0, L1)
            linear("ka", 0, TOK)
            linear("qa", L0, L1)
            linear("om", L0, L1)
            mlstm()
            pe.wait_ge(s["rope_ready"], 1)
            pe.wait_ge(s["ml_std"], 1)
            attention(att0, 0, AH,
                      lambda h: qa[64 * (h % 2):64 * (h % 2) + 64, h // 2, :],
                      lambda h: ka[64 * (h % 2):64 * (h % 2) + 64, h // 4, :],
                      lambda h, i: va[:, i, (h // 4) * 64:(h // 4) * 64 + 64])
            pe.wait_ge(s["ml_y"], 1)
            pe.wait_ge(s["att_y"], AH // 2)
            linear("out0", L0, L1)
            ffn(0, L0, L1)
            feature_sums(L0, L1)
            if layers == 1:
                return
            adaln(1)
            feature_sums(0, TOK)
            linear("in1", 0, TOK, gate=next_h())
            token_linear("vr")
            token_linear("dt")
            mixer1()
            linear("out1", 0, TOK, gate=next_h())
            ffn(1, 0, TOK)
            if layers == 2:
                return
            adaln(2)
            feature_sums(0, TOK)
            linear("cq", L0, L1, gate=next_h())
            linear("ckv", 0, TOK)
            linear("kpe", 0, TOK)
            latent_norms()
            linear("uq", 0, LAT, K=6, hi=cq_hi, lo=cq_lo, M=LQ, per=2,
                   gate=lambda k: pe.wait_ge(s["lq_done"], 1))
            pe.wait_ge(s["lq_done"], 2)
            f = ph["uk"]
            for u in range(f.units):
                pe.wait_ge(s["split"], f.first_split + u + 1)
                w_h, w_l = (part_slot(x, f, u, 2) for x in (w_hi, w_lo))
                for i in range(4):
                    t = f.first_taken + 4 * u + i
                    room(t)
                    for k in range(2):
                        last = three(bank_of(t)[:, :], w_h[:, k, i * P:(i + 1) * P], w_l[:, k, i * P:(i + 1) * P],
                                     ckv_hi[:, k, :], ckv_lo[:, k, :], k == 0, k == 1)
                    last.then_inc(s["steps"], 1)
            token_linear("uv", K=2, hi=ckv_hi, lo=ckv_lo)
            pe.wait_ge(s["taken"], ph["out2"].first_taken)
            pe.wait_ge(s["kpe_done"], 1)
            attention(att2, 2 * AH, LH, lambda h: qh[0:LQ, h, :], lambda h: kh[0:LQ, h, :],
                      lambda h, i: vl[:, i, h * LV:(h + 1) * LV])
            pe.wait_ge(s["att_y"], AH // 2 + LH // 2)
            linear("out2", L0, L1)
            ffn(2, L0, L1)
            feature_sums(L0, L1)

        @block.scalar
        def _(act):
            chain = Chain(act, s["scalar_order"])
            norms = [0]
            h_count = [0]
            rounded = [0]

            def round_next():
                q = rounded[0]
                rounded[0] += 1
                f, u = split_units[q]
                loaded(act, f, u, 0)
                if q >= SLOTS:
                    f0, u0 = split_units[q - SLOTS]
                    act.wait_ge(s["steps"], f0.steps_after(u0))
                act.activation(part_slot(w_hi, f, u), raw_slot(f, u), ACT.Copy).then_inc(s["rounded"], 1)

            def phase(name, job=None, more=True):
                f = ph[name]
                assert rounded[0] == f.first_split + min(AHEAD, f.units) or f.units < AHEAD, name

                def alone(u):
                    q = f.first_split + u + AHEAD
                    if q < len(split_units) and (more or u + AHEAD < f.units) and rounded[0] <= q:
                        round_next()
                    if job:
                        job(u, u, 0)

                def body(u, j, r):
                    w = j + AHEAD
                    loaded(act, f, w, r)
                    act.wait_ge(s["steps"], r * ROUND + (f.first_step + w - SLOTS + 1))
                    act.activation(part_slot(w_hi, f, w), raw_slot(f, w), ACT.Copy).then_inc(s["rounded"], 1)
                    if job:
                        job(u, j, r)

                if f.units - AHEAD - 1 >= 2 * ROUND and f.steps == 1 and f.takes == 1:
                    alone(0)
                    unit_rounds(act, 1, f.units - AHEAD, body)
                    rounded[0] += f.units - AHEAD - 1
                    for u in range(f.units - AHEAD, f.units):
                        alone(u)
                else:
                    for u in range(f.units):
                        alone(u)

            def square(k, t0, t1):
                if k > SLOTS:
                    act.wait_ge(s["added"], norms[0] * (KD - 1) + k - 3)
                dst = work[:, k % 3, t0:t1] if k else sq_sum[:, t0:t1]
                act.activation(dst, X[:, k, t0:t1], ACT.Square).then_inc(s["squared"], 1)

            def squares(t0, t1):
                for k in range(KD):
                    square(k, t0, t1)

            def rms_std(t0, t1):
                norms[0] += 1
                act.wait_ge(s["sum_ready"], norms[0])
                act.activation(std[:, t0:t1], bank[4][:, t0:t1], ACT.Sqrt, scale=1.0 / D, bias=EPS)\
                   .then_inc(s["std_ready"], 1)

            def round_h(src, t0, t1):
                for k in range(KD):
                    act.wait_ge(s["h_work"], h_count[0] + k + 1)
                    act.activation(h_hi[:, k, t0:t1], src(k)[:, t0:t1], ACT.Copy).then_inc(s["h_round"], 1)
                h_count[0] += KD

            def work_tile(k):
                return work[:, k % 3, :]

            def softplus_part(ready, x):
                act.wait_ge(s["lf_in"], ready)
                chain.then(act.activation(x, x, ACT.Exp))
                act.activation(x, x, ACT.Ln, bias=1.0).then_inc(s["lf_exp"], 1)

            def attention(m, a0, heads, scale, sinks):
                def exps(a):
                    act.wait_ge(s["att_m"], a0 + a + 1)
                    if a >= 2:
                        act.wait_ge(s["att_t"], a0 + a - 1)
                    src = m["masked"][a % 2] if sinks else bank[a % 2][:, :]
                    e = act.activation(m["prob"][a % 2], src, ACT.Exp, bias=m["nmax"][:, a:a + 1],
                                       scale=scale, accum_out=m["total"][:, a:a + 1])
                    if sinks:
                        e = act.activation(m["esink"][:, a:a + 1], S("sink")[:, a // 2:a // 2 + 1],
                                           ACT.Exp, bias=m["nmax"][:, a:a + 1])
                    e.then_inc(s["att_e"], 1)

                def keep(a):
                    h, t = divmod(a, 2)
                    act.wait_ge(s["att_t"], a0 + a + 1)
                    if h >= 2:
                        act.wait_ge(s["att_o"], a0 // 2 + h - 1)
                    act.activation(m["turned"][h % 2][:, :, t * P:(t + 1) * P],
                                   bank[2 + a % 2][:, :].rearrange("p (k q) -> p k q", k=TT),
                                   ACT.Copy).then_inc(s["att_pt"], 1)

                exps(0)
                for a in range(2 * heads):
                    if a + 1 < 2 * heads:
                        exps(a + 1)
                    keep(a)

            def out_and_squares(name, t0, t1):
                f = ph[name]

                def job(u, j, r):
                    act.wait_ge(s["taken"], f.first_taken + u + 1)
                    square(u, t0, t1)
                phase(name, job)

            def down_and_squares(name, t0, t1, more):
                f = ph[name]

                def job(u, j, r):
                    if u % 2:
                        act.wait_ge(s["taken"], f.first_taken + u // 2 + 1)
                        square(u // 2, t0, t1)
                phase(name, job, more)

            def silu_gates(n, t0, t1):
                f = ph[f"up{n}"]

                def job(u, j, r):
                    if j % 2 == 0:
                        act.wait_ge(s["steps"], r * ROUND + (f.first_step + j + 1))
                        act.wait_ge(s["taken"], r * ROUND + (f.first_taken + j - 4))
                        act.activation(up_tmp[:, (j // 2) % 3, t0:t1], bank_of(f.first_taken + j)[:, 0:t1 - t0],
                                       ACT.Silu).then_inc(s["up_act"], 1)
                phase(f"up{n}", job)

            act.wait_ge(s["small_in"], 16)
            for n in range(2):
                act.activation(silu_c[:, n, :, :], S(f"c{n}", KD), ACT.Silu).then_inc(s["silu_ready"], 1)
            act.wait_ge(s["x_in"], 32)
            squares(0, TOK)
            rms_std(0, TOK)
            round_next()
            round_next()
            round_h(work_tile, 0, TOK)
            phase("va_gates")
            phase("vm")

            def conv_silu(name, dst, first, n):
                f = ph[name]

                def job(u, j, r):
                    act.wait_ge(s["taken"], f.first_taken + u + 1)
                    act.activation(dst[:, u, :], conv[:, (first + u) % 2, 0:n], ACT.Silu)\
                       .then_inc(s["conv_act"], 1)
                phase(name, job)

            conv_silu("km", km, 0, TOK)
            conv_silu("qm", qm, 4, LAT)
            phase("ka")
            phase("qa")
            phase("om")
            softplus_part(1, gtmp)
            for h in range(MH):
                act.wait_ge(s["ml_arg"], h + 1)
                if h:
                    act.wait_ge(s["ml_p"], h)
                for d in range(2):
                    for i in range(TT):
                        src = narg[:, d, 0, :] if i < 2 else narg[:, d, i - 1, :]
                        last = act.activation(ex[:, d, i, :], src, ACT.Exp, bias=g_bias[:, d, i, h:h + 1])
                last.then_inc(s["ml_e"], 1)
                if h:
                    act.wait_ge(s["ml_h"], h)
                act.activation(den_e, bank[1][:, :], ACT.Exp, scale=-1.0).then_inc(s["ml_e"], 1)
            act.wait_ge(s["ml_sum"], 1)
            for i in range(2):
                act.activation(sq_m[:, 2 * i:2 * i + 2, :], bank[i][:, :].rearrange("p (a b) -> p a b", a=2),
                               ACT.Sqrt, scale=1.0 / MD, bias=EPS)
            act.activation(sig, om, ACT.Sigmoid).then_inc(s["ml_std"], 1)
            act.wait_ge(s["ml_y"], 1)
            attention(att0, 0, AH, AD ** -0.5, True)
            out_and_squares("out0", L0, L1)
            rms_std(L0, L1)
            round_h(work_tile, L0, L1)

            def gelu(u, j, r):
                if j % 2 == 0:
                    act.wait_ge(s["up_conv"], r * (ROUND // 2) + (j // 2 + 1))
                    x = up_tmp[:, (j // 2) % 3, 0:LAT]
                    act.activation(x, x, ACT.Gelu_apprx_tanh).then_inc(s["up_act"], 1)

            phase("up0", gelu)
            down_and_squares("down0", L0, L1, False)
            rms_std(L0, L1)
            if layers == 1:
                return

            act.wait_ge(s["x_ready"], 1)
            act.dma_start(room1, dram["table1"]).then_inc(s["tables_in"], 16)
            act.wait_ge(s["ctx2_in"], 16)
            squares(0, TOK)
            rms_std(0, TOK)
            round_next()
            round_next()
            round_h(work_tile, 0, TOK)
            phase("in1")
            phase("vr")
            phase("dt")
            softplus_part(2, dtmp[:, 0, :])
            softplus_part(3, dtmp)
            act.activation(nega, S("a_log"), ACT.Exp).then_inc(s["lf_exp"], 1)
            for i in range(8):
                act.wait_ge(s["conv_ready"], i + 1)
                act.activation(t1[:, 16 + i, :], conv1[:, i % 2, :], ACT.Silu).then_inc(s["conv_act"], 1)
            for h in range(RH):
                act.wait_ge(s["rt_arg"], h + 1)
                if h:
                    act.wait_ge(s["rt_p"], h)
                act.activation(ea[:, 0:2, 0:LAT], ea[:, 2, :].rearrange("p (a b) -> p a b", a=2), ACT.Exp)
                for d, dst in ((0, ea), (1, eb)):
                    last = act.activation(dst[:, 0:2, L0:L1], C1("far_f" if d == 0 else "far_b", 2), ACT.Exp,
                                          scale=log_r[:, d * RH + h:d * RH + h + 1])
                last.then_inc(s["rt_e"], 1)
            for i in range(4):
                act.wait_ge(s["gn_sum"], 4 + i + 1)
                last = act.activation(y_sq[:, i, :], bank[i][:, :], ACT.Sqrt, bias=EPS)
            last.then_inc(s["gn_std"], 1)
            for i in range(4):
                act.activation(t1[:, 8 + i, :], t1[:, 8 + i, :], ACT.Silu)
                last = act.activation(t1[:, 12 + i, :], t1[:, 12 + i, :], ACT.Silu)
            last.then_inc(s["gn_act"], 1)
            for i in range(TT):
                act.wait_ge(s["sd_t"], i + 1)
                act.activation(xt[:, i, :], bank[i][:, :], ACT.Copy).then_inc(s["sd_tt"], 1)
            for h in range(RH):
                for d, e in ((0, ea), (1, eb)):
                    act.wait_ge(s["sd_arg"], 2 * h + d + 1)
                    for i in range(2):
                        act.activation(e[:, i, :], e[:, i, :], ACT.Exp, bias=ngs[:, d, i, h:h + 1])
                    for i in range(2, TT):
                        part = e[:, 2, (i - 2) * LAT:(i - 1) * LAT]
                        last = act.activation(part, part, ACT.Exp, bias=ngs[:, d, i, h:h + 1])
                    last.then_inc(s["sd_e"], 1)
            act.wait_ge(s["sn_sum"], 1)
            act.activation(std[:, :], bank[7][:, :], ACT.Sqrt, scale=1.0 / 512, bias=EPS).then_inc(s["sn_std"], 1)
            round_h(lambda k: y1[:, k, :], 0, TOK)
            out_and_squares("out1", 0, TOK)
            rms_std(0, TOK)
            round_h(work_tile, 0, TOK)
            silu_gates(1, 0, TOK)
            down_and_squares("down1", 0, TOK, False)
            if layers == 2:
                return

            act.dma_start(room2, dram["table2"]).then_inc(s["tables_in"], 16)
            rms_std(0, TOK)
            round_next()
            round_next()
            round_h(work_tile, 0, TOK)
            phase("cq")
            phase("ckv")
            phase("kpe")
            act.wait_ge(s["lq_sum"], 1)
            act.activation(std[:, L0:L1], bank[6][:, 0:LAT], ACT.Sqrt, scale=1.0 / 768, bias=EPS)\
               .then_inc(s["lq_std"], 1)
            act.wait_ge(s["lq_sum"], 2)
            act.wait_ge(s["lq_done"], 1)
            act.activation(std[:, :], bank[7][:, :], ACT.Sqrt, scale=1.0 / 256, bias=EPS)\
               .then_inc(s["lq_std"], 1)
            act.wait_ge(s["kpe_in"], 1)
            act.activation(kh[LN:LQ, :, :], kpe[LN:LQ, :].unsqueeze(1).to_broadcast([LR, LH, TOK]),
                           ACT.Copy).then_inc(s["kpe_done"], 1)
            phase("uq")
            phase("uk")
            phase("uv")
            attention(att2, 2 * AH, LH, LQ ** -0.5, False)
            out_and_squares("out2", L0, L1)
            rms_std(L0, L1)
            round_h(work_tile, L0, L1)
            silu_gates(2, L0, L1)
            down_and_squares("down2", L0, L1, False)
            rms_std(L0, L1)

        @block.gpsimd
        def _(pool):
            done = [0]
            h_count = [0]

            def low_next():
                q = done[0]
                done[0] += 1
                f, u = split_units[q]
                pool.wait_ge(s["rounded"], q + 1)
                pool.tensor_tensor(part_slot(w_lo, f, u), raw_slot(f, u), part_slot(w_hi, f, u).bitcast(F32),
                                   ALU.subtract).then_inc(s["split"], 1)

            def lows(*names):
                for name in names:
                    f = ph[name]
                    start = AHEAD if name == names[0] else 0
                    if f.units - start >= 2 * ROUND:
                        def body(u, j, r, f=f):
                            pool.wait_ge(s["rounded"], r * ROUND + (f.first_split + j + 1))
                            pool.tensor_tensor(part_slot(w_lo, f, j), raw_slot(f, j),
                                               part_slot(w_hi, f, j).bitcast(F32),
                                               ALU.subtract).then_inc(s["split"], 1)
                        unit_rounds(pool, start, f.units, body)
                        done[0] += f.units - start
                    else:
                        while done[0] < f.first_split + f.units:
                            low_next()

            def low_h(src, t0, t1):
                for k in range(KD):
                    pool.wait_ge(s["h_round"], h_count[0] + k + 1)
                    pool.tensor_tensor(h_lo[:, k, t0:t1], src(k)[:, t0:t1], h_hi[:, k, t0:t1].bitcast(F32),
                                       ALU.subtract).then_inc(s["h_split"], 1)
                h_count[0] += KD

            def work_tile(k):
                return work[:, k % 3, :]

            def two():
                low_next()
                low_next()

            two()
            low_h(work_tile, 0, TOK)
            if layers > 1:
                pool.dma_start(X[:, :, 0:L0], dram["ctx_2"]).then_inc(s["ctx2_in"], 16)
            lows("va_gates", "vm", "km", "qm", "ka", "qa", "om", "out0")
            two()
            low_h(work_tile, L0, L1)
            lows("up0", "down0")
            if layers == 1:
                return
            two()
            low_h(work_tile, 0, TOK)
            lows("in1", "vr", "dt")
            two()
            pool.wait_ge(s["taken"], ph["out1"].first_taken)
            pool.wait_ge(s["split"], done[0])
            for q in range(4):
                if q:
                    pool.wait_ge(s["swap_done"], q)
                src = t1[32 * (q ^ 1):32 * (q ^ 1) + 32, 0:8, L0:L1]
                pool.tensor_copy(swap_r[32 * q:32 * q + 32, :, :], src).then_inc(s["swap_done"], 1)
            pool.wait_ge(s["swap_done"], 4)
            low_h(lambda k: y1[:, k, :], 0, TOK)
            lows("out1")
            two()
            low_h(work_tile, 0, TOK)
            lows("up1", "down1")
            if layers == 2:
                return
            two()
            low_h(work_tile, 0, TOK)
            lows("cq", "ckv", "kpe", "uq", "uk", "uv", "out2")
            two()
            low_h(work_tile, L0, L1)
            lows("up2", "down2")

        @block.vector
        def _(dve):
            chain = Chain(dve, s["vector_order"])
            then = chain.then
            norms = [0]
            h_count = [0]

            def copy(out, in_):
                return dve.tensor_scalar(out, in_, 1.0, None, ALU.mult)

            def low(out, x, hi):
                return dve.tensor_tensor(out, x, hi.bitcast(F32), ALU.subtract)

            def product_in(f, j, r=0):
                dve.wait_ge(s["steps"], r * (ROUND * f.steps) + (f.first_step + j + 1))

            def adaln(n):
                f = ph[f"ada{n}"]

                def body(u, j, r):
                    if j % 3 == 2:
                        product_in(f, j, r)
                        copy(crow[0:2, j // 3, :], bank[6 + j // 3][0:2, 0:3 * P]).then_inc(s["rows_in"], 1)

                unit_rounds(dve, 0, f.units, body)
                dve.wait_ge(s["columns"], 8 * (n + 1))
                then(dve.tensor_tensor(mod[:, :, :], bank[5][:, 0:96].rearrange("p (a b) -> p a b", b=2),
                                       S(f"b_ada{n}").unsqueeze(2).to_broadcast([P, 48, 2]), ALU.add))
                for w in range(2):
                    sc = mod[:, 24 * w + 8:24 * w + 16, :]
                    if n == 0:
                        g = S("norm_mix" if w == 0 else "norm_ffn").unsqueeze(2).to_broadcast([P, KD, 2])
                        last = dve.scalar_tensor_tensor(out=gain[:, w, :, :], in0=sc, scalar=1.0, in1=g,
                                                        op0=ALU.add, op1=ALU.mult)
                    else:
                        last = dve.tensor_scalar(gain[:, w, :, :], sc, 1.0, None, ALU.add)
                last.then_inc(s["mod_ready"], 1)
                dve.wait_ge(s["mod_ready"], n + 1)

            def add_square(k, t0, t1):
                n = norms[0] * (KD - 1) + k
                dve.wait_ge(s["squared"], norms[0] * KD + k + 1)
                if k > 1:
                    dve.wait_ge(s["added"], n - 1)
                dve.tensor_tensor(sq_sum[:, t0:t1], sq_sum[:, t0:t1], work[:, k % 3, t0:t1], ALU.add)\
                   .then_inc(s["added"], 1)
                if k == KD - 1:
                    dve.wait_ge(s["added"], n)
                    norms[0] += 1
                    dve.nop().then_inc(s["sums_in"], 1)

            def add_squares(t0, t1):
                for k in range(1, KD):
                    add_square(k, t0, t1)

            def inverse_rms(t0, t1):
                dve.wait_ge(s["std_ready"], norms[0])
                then(dve.reciprocal(std[:, t0:t1], std[:, t0:t1]))

            def norm(which, both):
                t0 = 0 if both else L0
                inverse_rms(t0, L1)
                for k in range(KD):
                    if k >= 3:
                        dve.wait_ge(s["h_split"], h_count[0] + k - 2)
                    w = work[:, k % 3, :]
                    then(dve.tensor_tensor(w[:, t0:L1], X[:, k, t0:L1], std[:, t0:L1], ALU.mult))
                    for a, b, m in ([(0, L0, 1)] if both else []) + [(L0, L1, 0)]:
                        last = dve.tensor_scalar(w[:, a:b], w[:, a:b], gain[:, which, k, m:m + 1],
                                                 mod[:, 24 * which + k, m:m + 1], ALU.mult, ALU.add)
                    last.then_inc(s["h_work"], 1)
                h_count[0] += KD

            def final_norm(name):
                inverse_rms(L0, L1)
                for k in range(KD):
                    x = X[:, k, L0:L1]
                    last = dve.scalar_tensor_tensor(out=x, in0=x, scalar=S(name)[:, k:k + 1],
                                                    in1=std[:, L0:L1], op0=ALU.mult, op1=ALU.mult)
                last.then_inc(s["x_ready"], 1)

            def each_product(name, body, chain_links=0):
                f = ph[name]
                takes = int(f.takes)

                def unit(u, j, r):
                    for i in range(takes):
                        dve.wait_ge(s["steps"], r * (ROUND * f.steps) + (f.first_step + j * takes + i + 1))
                        body(u * takes + i, bank_of(f.first_taken + j * takes + i)).then_inc(s["taken"], 1)

                unit_rounds(dve, 0, f.units, unit, chain, chain_links)

            def taken(name):
                dve.wait_ge(s["taken"], ph[name].first_taken)

            def conv_taps(dst, src, taps, bias, segs):
                half = len(taps) // 2
                d, x = (v.rearrange("p (a b) -> p a b", a=segs) for v in (dst, src))
                w = d.shape[2]
                then(dve.tensor_scalar(dst, src, taps[half], bias, ALU.mult, ALU.add))
                last = None
                for n, tap in enumerate(taps):
                    o = n - half
                    if o == 0:
                        continue
                    if last is not None:
                        then(last)
                    lo, hi = max(0, -o), w - max(0, o)
                    last = dve.scalar_tensor_tensor(out=d[:, :, lo:hi], in0=x[:, :, lo + o:hi + o],
                                                    scalar=tap, in1=d[:, :, lo:hi], op0=ALU.mult, op1=ALU.add)
                return last

            def minus_abs(dst, x):
                dve.scalar_tensor_tensor(out=dst, in0=x, scalar=-1.0, in1=x, op0=ALU.mult, op1=ALU.min)\
                   .then_inc(s["lf_in"], 1)

            def log_gates():
                minus_abs(gtmp, gates)
                dve.wait_ge(s["lf_exp"], 1)
                dve.scalar_tensor_tensor(out=lf, in0=gates, scalar=0.0, in1=gtmp, op0=ALU.min,
                                         op1=ALU.subtract).then_inc(s["lf_ready"], 1)

            def mlstm():
                log_gates()
                dve.wait_ge(s["cum_ready"], 1)
                then(copy(g_cum, bank[6][:, 0:2 * TT * MH].rearrange("p (d i h) -> p d i h", d=2, i=TT)))
                for d in range(2):
                    last = dve.tensor_tensor(g_bias[:, d, :, :], gates[:, :, 8 * d:8 * d + 4], g_cum[:, d, :, :],
                                             ALU.subtract)
                last.then_inc(s["cum_taken"], 1)
                dve.wait_ge(s["rows_ready"], 1)
                then(copy(run_max[0:MH, 0:512], bank[0][0:MH, :]))
                then(copy(run_max[0:MH, 512:1024], bank[1][0:MH, :]))
                for d in range(2):
                    then(dve.reduce_max(top[0:MH, d:d + 1], run_max[0:MH, d * 512:d * 512 + L0], AX_X))
                then(dve.tensor_scalar(top[0:MH, :], top[0:MH, :], 0.0, None, ALU.max))
                b = run_max[0:MH, L0:L1]
                dve.tensor_tensor_scan(rows[0:MH, 0, :], b, b, top[0:MH, 0:1], ALU.max, ALU.max)
                b = run_max[0:MH, 1023:767:-1]
                then(dve.tensor_tensor_scan(rows[0:MH, 1, ::-1], b, b, top[0:MH, 1:2], ALU.max, ALU.max))
                dve.tensor_tensor(rows[0:MH, 2:4, :], rows[0:MH, 0:2, :],
                                  bank[2][0:MH, :].rearrange("p (a b) -> p a b", a=2), ALU.add)\
                   .then_inc(s["rows_taken"], 1)
                for h in range(MH):
                    dve.wait_ge(s["ml_bcast"], h + 1)
                    if h:
                        dve.wait_ge(s["ml_e"], 2 * h)
                    for d in range(2):
                        m = bank[0][:, d * LAT:(d + 1) * LAT]
                        dve.tensor_scalar(narg[:, d, 0, :], m, -1.0, None, ALU.mult)
                        last = dve.scalar_tensor_tensor(
                            out=narg[:, d, 1:3, :], in0=m.unsqueeze(1).to_broadcast([P, 2, LAT]), scalar=-1.0,
                            in1=C0("after" if d == 0 else "before", 2), op0=ALU.mult, op1=ALU.add)
                    last.then_inc(s["ml_arg"], 1)
                    dve.wait_ge(s["ml_s"], h + 1)
                    dve.wait_ge(s["ml_e"], 2 * h + 1)
                    if h:
                        dve.wait_ge(s["ml_num"], h)
                    for d in range(2):
                        for i in range(2):
                            last = dve.scalar_tensor_tensor(
                                out=prob_m[:, d * TT + 2 * i:d * TT + 2 * i + 2, :],
                                in0=bank[2 + i][:, :].rearrange("p (a b) -> p a b", a=2), scalar=MD ** -0.5,
                                in1=ex[:, d, 2 * i:2 * i + 2, :], op0=ALU.mult, op1=ALU.mult)
                    last.then_inc(s["ml_p"], 1)
                    dve.wait_ge(s["ml_num"], h + 1)
                    then(dve.tensor_scalar(den_a, bank[5][:, :], -1.0, None, ALU.mult))
                    then(dve.tensor_tensor(den_a, den_a, bank[5][:, :], ALU.max))
                    dve.wait_ge(s["ml_e"], 2 * h + 2)
                    then(dve.tensor_tensor(den_a, den_a, den_e, ALU.max))
                    then(dve.reciprocal(den_a, den_a))
                    then(dve.tensor_tensor(hid, den_a, bank[4][:, :], ALU.mult))
                    dve.tensor_tensor(hm[:, h, :], hid[:, 0:LAT], hid[:, LAT:2 * LAT], ALU.add)\
                       .then_inc(s["ml_h"], 1)
                dve.wait_ge(s["ml_h"], MH)
                dve.tensor_tensor(sq_m, hm, hm, ALU.mult).then_inc(s["ml_sq"], 1)
                dve.wait_ge(s["ml_std"], 1)
                then(dve.reciprocal(sq_m, sq_m))
                then(dve.tensor_tensor(sig, sig, sq_m, ALU.mult))
                for h in range(MH):
                    last = dve.scalar_tensor_tensor(out=hm[:, h, :], in0=hm[:, h, :],
                                                    scalar=S("mlstm_norm")[:, h:h + 1], in1=sig[:, h, :],
                                                    op0=ALU.mult, op1=ALU.mult)
                then(last)
                then(copy(h_hi[:, 0:MH, L0:L1], hm))
                low(h_lo[:, 0:MH, L0:L1], hm, h_hi[:, 0:MH, L0:L1]).then_inc(s["ml_y"], 1)
                dve.wait_ge(s["ml_y"], 1)

            swap16 = list(range(16, 32)) + list(range(16))

            def attention(m, a0, heads, scale, sinks, tile0):
                if sinks:
                    then(dve.tensor_scalar(m["nsink"], S("sink"), -1.0, None, ALU.mult))

                def peaks(a):
                    h, t = divmod(a, 2)
                    dve.wait_ge(s["att_s"], a0 + a + 1)
                    if sinks:
                        if a >= 2:
                            dve.wait_ge(s["att_e"], a0 + a - 1)
                        then(dve.tensor_tensor_reduce(m["masked"][a % 2], bank[a % 2][:, :],
                                                      C0("window", 2)[:, t, :], 1.0, -3e38, ALU.add, ALU.max,
                                                      m["peak"][:, a:a + 1]))
                        dve.tensor_scalar(m["nmax"][:, a:a + 1], m["peak"][:, a:a + 1], -scale,
                                          m["nsink"][:, h:h + 1], ALU.mult, ALU.min).then_inc(s["att_m"], 1)
                    else:
                        then(dve.reduce_max(m["peak"][:, a:a + 1], bank[a % 2][:, :], AX_X))
                        dve.tensor_scalar(m["nmax"][:, a:a + 1], m["peak"][:, a:a + 1], -scale, None,
                                          ALU.mult).then_inc(s["att_m"], 1)

                def divide(a):
                    dve.wait_ge(s["att_e"], a0 + a + 1)
                    one = m["total"][:, a:a + 1]
                    if sinks:
                        then(dve.tensor_tensor(one, one, m["esink"][:, a:a + 1], ALU.add))
                    then(dve.reciprocal(one, one))
                    dve.tensor_scalar(m["prob"][a % 2], m["prob"][a % 2], one, None, ALU.mult)\
                       .then_inc(s["att_p"], 1)

                def outputs(t):
                    dve.wait_ge(s["att_o"], a0 // 2 + 2 * t + 2)
                    y = bank[4 + t % 2][:, 0:LAT]
                    hi = h_hi[:, tile0 + t, L0:L1]
                    then(copy(hi, y))
                    low(h_lo[:, tile0 + t, L0:L1], y, hi).then_inc(s["att_y"], 1)

                peaks(0)
                for a in range(2 * heads):
                    if a + 1 < 2 * heads:
                        peaks(a + 1)
                    divide(a)
                    if a >= 7 and (a - 7) % 4 == 0:
                        outputs((a - 7) // 4)
                outputs(heads // 2 - 1)
                dve.wait_ge(s["att_y"], a0 // 4 + heads // 2)

            def residual(name, chunk, both):
                f = ph[name]
                units = f.units // KD
                t0 = 0 if both else L0
                for k in range(KD):
                    product_in(f, units * (k + 1) - 1)
                    b = bank_of(f.first_taken + k)
                    for a, e, m in ([(0, L0, 1)] if both else []) + [(L0, L1, 0)]:
                        last = dve.scalar_tensor_tensor(out=X[:, k, a:e], in0=b[:, a - t0:e - t0],
                                                        scalar=mod[:, 8 * chunk + k, m:m + 1],
                                                        in1=X[:, k, a:e], op0=ALU.mult, op1=ALU.add)
                    last.then_inc(s["taken"], 1)
                    if k > 1:
                        add_square(k - 1, t0, L1)
                add_square(KD - 1, t0, L1)

            def hidden(i, w, t0, t1):
                hi, lo = (x[:, bass.ds(i, 1), t0:t1].rearrange("p a b -> p (a b)") for x in (hidden_hi, hidden_lo))
                then(copy(hi, w))
                low(lo, w, hi).then_inc(s["hid_done"], 1)

            def gated(f, j, r, t0, t1, at):
                i = r * (ROUND // 2) + j // 2
                product_in(f, j, r)
                w = work[:, (j // 2) % 3, t0:t1]
                dve.tensor_tensor(w, up_tmp[:, (j // 2) % 3, at:at + t1 - t0],
                                  bank_of(f.first_taken + j)[:, 0:t1 - t0], ALU.mult).then_inc(s["taken"], 2)
                dve.wait_ge(s["taken"], r * ROUND + (f.first_taken + j + 1))
                hidden(i, w, t0, t1)

            def ffn0():
                norm(1, False)
                w, b = S("ffn_conv_w", 3), S("ffn_conv_b")
                f = ph["up0"]

                def unit(u, j, r):
                    i = r * (ROUND // 2) + j // 2
                    if j % 2 == 0:
                        product_in(f, j, r)
                        conv_taps(up_tmp[:, (j // 2) % 3, 0:LAT], bank_of(f.first_taken + j)[:, 0:LAT],
                                  [w[:, q, bass.ds(i, 1)] for q in range(3)], b[:, bass.ds(i, 1)], 1)\
                            .then_inc(s["up_conv"], 1)
                    else:
                        dve.wait_ge(s["up_act"], r * (ROUND // 2) + (j // 2 + 1))
                        gated(f, j, r, L0, L1, 0)

                unit_rounds(dve, 0, f.units, unit, chain, 9)
                residual("down0", 5, False)

            def swiglu(n, both):
                t0 = 0 if both else L0
                norm(1, both)
                f = ph[f"up{n}"]

                def unit(u, j, r):
                    if j % 2:
                        dve.wait_ge(s["up_act"], r * (ROUND // 2) + (KF * n + j // 2 + 1))
                        gated(f, j, r, t0, L1, t0)

                unit_rounds(dve, 0, f.units, unit, chain, 3)
                residual(f"down{n}", 5, both)

            def mixer1():
                def keep(p, b):
                    return copy(t1[:, bass.ds(p, 1), :].rearrange("p a b -> p (a b)"), b[:, :])
                each_product("in1", keep)
                each_product("vr", lambda p, b: copy(vr[:, p % TT, p // TT * 256:(p // TT + 1) * 256], b[:, 0:256]))
                each_product("dt", lambda p, b: dve.tensor_tensor(dt[:, p, :], b[:, 0:16], S("dt_bias"), ALU.add))
                taken("out1")
                lg = S("decay_logit")
                minus_abs(dtmp[:, 0, :], lg)
                dve.wait_ge(s["lf_exp"], 2)
                then(dve.scalar_tensor_tensor(out=log_r, in0=lg, scalar=0.0, in1=dtmp[:, 0, :], op0=ALU.min,
                                              op1=ALU.subtract))
                minus_abs(dtmp, dt)
                dve.wait_ge(s["lf_exp"], 4)
                then(dve.scalar_tensor_tensor(out=dt, in0=dt, scalar=0.0, in1=dtmp, op0=ALU.max, op1=ALU.add))
                dve.scalar_tensor_tensor(out=la, in0=dt, scalar=-1.0,
                                         in1=nega.unsqueeze(1).to_broadcast([P, TT, 16]),
                                         op0=ALU.mult, op1=ALU.mult).then_inc(s["lf_ready"], 1)
                w, b = S("ssd_conv_w", 5), S("ssd_conv_b")
                for i in range(8):
                    if i >= 2:
                        dve.wait_ge(s["conv_act"], 8 + i - 1)
                    conv_taps(conv1[:, i % 2, :], t1[:, 16 + i, :], [w[:, q, i:i + 1] for q in range(5)],
                              b[:, i:i + 1], 2).then_inc(s["conv_ready"], 1)
                dve.wait_ge(s["swap_done"], 4)
                dve.wait_ge(s["tables_in"], 32)
                lat = t1[:, 0:8, L0:L1]
                cs, sn = (C1(x).unsqueeze(1).to_broadcast([P, KD, LAT]) for x in ("cos", "sin"))
                dve.tensor_tensor(swap_r, swap_r, sn, ALU.mult)
                then(dve.tensor_tensor(lat, lat, cs, ALU.mult))
                dve.tensor_tensor(lat, lat, swap_r, ALU.add).then_inc(s["rope_ready"], 1)
                dve.wait_ge(s["rope_ready"], 2)
                for h in range(RH):
                    if h:
                        dve.wait_ge(s["rt_e"], h)
                    rf, rb = log_r[:, h:h + 1], log_r[:, RH + h:RH + h + 1]
                    arg = ea[:, 2, :]
                    then(dve.tensor_scalar(arg, C1("dist_b"), rb, None, ALU.mult))
                    dve.scalar_tensor_tensor(out=arg, in0=C1("dist_f"), scalar=rf, in1=arg, op0=ALU.mult,
                                             op1=ALU.add).then_inc(s["rt_arg"], 1)
                    dve.wait_ge(s["rt_e"], h + 1)
                    then(dve.tensor_tensor(ea[:, 0:2, L0:L1], ea[:, 0:2, L0:L1], eb[:, 0:2, L0:L1], ALU.add))
                    dve.wait_ge(s["rt_s"], h + 1)
                    if h:
                        dve.wait_ge(s["rt_o"], h)
                    sb0 = 3 * (h % 2)
                    for i in range(2):
                        dve.scalar_tensor_tensor(out=pr[:, i, :], in0=bank[sb0 + i][:, :], scalar=0.125,
                                                 in1=ea[:, i, :], op0=ALU.mult, op1=ALU.mult)
                    dve.scalar_tensor_tensor(
                        out=pr[:, 2, :].rearrange("p (a b) -> p a b", a=2),
                        in0=bank[sb0 + 2][:, :].rearrange("p (a b) -> p a b", a=2), scalar=0.125,
                        in1=ea[:, 0:2, 0:LAT], op0=ALU.mult, op1=ALU.mult).then_inc(s["rt_p"], 1)
                    if h % 2 and h > 1:
                        dve.wait_ge(s["rt_o"], h - 1)
                        copy(y1[:, h // 2 - 1, :], bank[6 + (h // 2 - 1) % 2][:, :]).then_inc(s["rt_y"], 1)
                dve.wait_ge(s["rt_o"], RH)
                copy(y1[:, 3, :], bank[7][:, :]).then_inc(s["rt_y"], 1)
                dve.wait_ge(s["rt_y"], 4)
                for i in range(4):
                    dve.wait_ge(s["gn_sum"], i + 1)
                    then(dve.tensor_tensor(y1[:, i, :], y1[:, i, :], bank[i][:, :], ALU.subtract))
                    dve.tensor_tensor(y_sq[:, i, :], y1[:, i, :], y1[:, i, :], ALU.mult).then_inc(s["gn_in"], 1)
                dve.wait_ge(s["gn_std"], 1)
                then(dve.reciprocal(y_sq, y_sq))
                for i in range(4):
                    last = dve.scalar_tensor_tensor(out=y_sq[:, i, :], in0=y_sq[:, i, :],
                                                    scalar=S("gn_w")[:, i:i + 1], in1=y1[:, i, :],
                                                    op0=ALU.mult, op1=ALU.mult)
                then(last)
                dve.wait_ge(s["gn_act"], 1)
                dve.tensor_tensor(y1[:, 0:4, :], y_sq, t1[:, 8:12, :], ALU.mult).then_inc(s["gn_done"], 1)
                dve.wait_ge(s["gn_done"], 1)
                dve.wait_ge(s["cum_ready"], 2)
                cum = bank[7][:, 0:2 * TT * RH].rearrange("p (d i h) -> p d i h", d=2, i=TT)
                dve.tensor_scalar(ngs, cum, -1.0, None, ALU.mult)
                copy(gs, cum).then_inc(s["cum_taken"], 1)
                dve.wait_ge(s["rows_ready"], 2)
                copy(grow[0:RH, 0, :], bank[5][0:RH, :])
                copy(grow[0:RH, 1, :], bank[6][0:RH, :]).then_inc(s["rows_taken"], 1)

                def parts(v, i):
                    return v[:, i, :] if i < 2 else v[:, 2, (i - 2) * LAT:(i - 1) * LAT]

                for h in range(RH):
                    for d, e in ((0, ea), (1, eb)):
                        dve.wait_ge(s["sd_b"], 2 * h + d + 1)
                        g = bank[3 + d][:, :]
                        mask = C1("after" if d == 0 else "before", 2)
                        gl = g[:, L0:L1].unsqueeze(1).to_broadcast([P, 2, LAT])
                        gc = g[:, 0:L0].unsqueeze(1).to_broadcast([P, 2, LAT])
                        dve.tensor_tensor(e[:, 0:2, 0:L0], gc, mask, ALU.add)
                        copy(e[:, 0:2, L0:L1], gl)
                        dve.tensor_tensor(e[:, 2, :].rearrange("p (a b) -> p a b", a=2), gl, mask, ALU.add)\
                           .then_inc(s["sd_arg"], 1)
                    dve.wait_ge(s["sd_e"], 2 * h + 1)
                    for i in range(TT):
                        last = dve.tensor_scalar(parts(ea, i), parts(ea, i), dt[:, i, h:h + 1], None, ALU.mult)
                    then(last)
                    dve.wait_ge(s["sd_e"], 2 * h + 2)
                    for i in range(TT):
                        last = dve.scalar_tensor_tensor(out=parts(eb, i), in0=parts(eb, i),
                                                        scalar=dt[:, i, RH + h:RH + h + 1], in1=parts(ea, i),
                                                        op0=ALU.mult, op1=ALU.add)
                    then(last)
                    dve.wait_ge(s["sd_s"], h // 4 + 1)
                    if h:
                        dve.wait_ge(s["sd_o"], h)
                    for i in range(3):
                        last = dve.tensor_tensor(pr[:, i, :], eb[:, i, :], bank[i][:, :], ALU.mult)
                    last.then_inc(s["sd_p"], 1)
                    dve.wait_ge(s["sd_p"], h + 1)
                    if h % 2 and h > 1:
                        dve.wait_ge(s["sd_o"], h - 1)
                        copy(y1[:, 4 + h // 2 - 1, :], bank[5 + (h // 2 - 1) % 2][:, :]).then_inc(s["sd_y"], 1)
                dve.wait_ge(s["sd_o"], RH)
                copy(y1[:, 7, :], bank[6][:, :]).then_inc(s["sd_y"], 1)
                dve.wait_ge(s["sd_y"], 4)
                for i in range(4):
                    y = y1[:, 4 + i, :]
                    then(dve.scalar_tensor_tensor(out=y, in0=t1[:, 16 + i, :], scalar=S("ssd_d")[:, i:i + 1],
                                                  in1=y, op0=ALU.mult, op1=ALU.add))
                    then(dve.tensor_tensor(y, y, t1[:, 12 + i, :], ALU.mult))
                    dve.tensor_tensor(y_sq[:, i, :], y, y, ALU.mult).then_inc(s["sn_in"], 1)
                dve.wait_ge(s["sn_std"], 1)
                then(dve.reciprocal(std[:, :], std[:, :]))
                for i in range(4):
                    dve.nop().then_inc(s["h_work"], 1)
                for i in range(4):
                    y = y1[:, 4 + i, :]
                    dve.scalar_tensor_tensor(out=y, in0=y, scalar=S("ssd_norm")[:, i:i + 1],
                                             in1=std[:, :], op0=ALU.mult, op1=ALU.mult).then_inc(s["h_work"], 1)
                h_count[0] += KD

            def mixer2():
                each_product("cq", lambda p, b: copy(cq[:, p, :], b[:, 0:LAT]))
                each_product("ckv", lambda p, b: copy(ckv[:, p, :], b[:, :]))
                each_product("kpe", lambda p, b: copy(kpe[LN:LQ, :], b[LN:LQ, :]))
                taken("uq")
                for i in range(6):
                    dve.tensor_tensor(cq_sq(i), cq[:, i, :], cq[:, i, :], ALU.mult).then_inc(s["lq_in"], 1)
                for i in range(2):
                    dve.tensor_tensor(sq_l[:, i, :], ckv[:, i, :], ckv[:, i, :], ALU.mult).then_inc(s["lq_in"], 1)
                dve.wait_ge(s["lq_std"], 1)
                then(dve.reciprocal(std[:, L0:L1], std[:, L0:L1]))
                for i in range(6):
                    last = dve.scalar_tensor_tensor(out=cq[:, i, :], in0=cq[:, i, :], scalar=S("q_norm")[:, i:i + 1],
                                                    in1=std[:, L0:L1], op0=ALU.mult, op1=ALU.mult)
                then(last)
                then(copy(cq_hi[:, :, :], cq))
                low(cq_lo[:, :, :], cq, cq_hi[:, :, :]).then_inc(s["lq_done"], 1)
                dve.wait_ge(s["lq_std"], 2)
                dve.wait_ge(s["lq_done"], 1)
                then(dve.reciprocal(std[:, :], std[:, :]))
                for i in range(2):
                    last = dve.scalar_tensor_tensor(out=ckv[:, i, :], in0=ckv[:, i, :],
                                                    scalar=S("kv_norm")[:, i:i + 1], in1=std[:, :],
                                                    op0=ALU.mult, op1=ALU.mult)
                then(last)
                then(copy(ckv_hi[:, :, :], ckv))
                low(ckv_lo[:, :, :], ckv, ckv_hi[:, :, :]).then_inc(s["lq_done"], 1)
                dve.wait_ge(s["tables_in"], 48)
                cs, sn = (C2(x)[LN:LQ, :] for x in ("cos", "sin"))

                def rotate(v, sw, n):
                    c3, s3 = (x.unsqueeze(1).to_broadcast([LR, n, LAT]) for x in (cs, sn))
                    then(dve.stream_shuffle(sw, v, swap16))
                    dve.tensor_tensor(v, v, c3, ALU.mult)
                    then(dve.tensor_tensor(sw, sw, s3, ALU.mult))
                    return dve.tensor_tensor(v, v, sw, ALU.add)

                rotate(kpe[LN:LQ, L0:L1].unsqueeze(1), kswap[LN:LQ, 0, 0:LAT].unsqueeze(1), 1)\
                    .then_inc(s["kpe_in"], 1)
                each_product("uq", lambda p, b: copy(
                    qh[0:LQ, bass.ds(2 * p, 2), :].rearrange("p a b -> p (a b)"), b[0:LQ, :]))
                taken("uk")
                dve.wait_ge(s["kpe_in"], 1)

                def plain_keys(p, b):
                    copy(kh[0:LN, 2 * p, :], b[0:LN, :])
                    return copy(kh[0:LN, 2 * p + 1, :], b[LN:P, :])

                each_product("uk", plain_keys)
                for u in range(LH // 2):
                    then(rotate(qh[LN:LQ, 2 * u:2 * u + 2, :],
                                kswap[LN:LQ, u % 2, :].rearrange("p (a b) -> p a b", a=2), 2))
                each_product("uv", lambda p, b: copy(vl[:, p % TT, p // TT * 512:(p // TT + 1) * 512], b[:, :]))
                taken("out2")
                attention(att2, 2 * AH, LH, LQ ** -0.5, False, 0)

            dve.wait_ge(s["small_in"], 16)
            dve.wait_ge(s["x_in"], 32)
            add_squares(0, TOK)
            adaln(0)
            norm(0, True)

            def va_gates(p, b):
                copy(va[:, p, :], b[:, 0:P])
                return dve.tensor_tensor(gates[:, p, :], b[:, P:P + 16], S("gate_b"), ALU.add)

            each_product("va_gates", va_gates)
            each_product("vm", lambda p, b: copy(vm[:, p % TT, p // TT * 256:(p // TT + 1) * 256], b[:, 0:256]))
            w, cb = S("qk_conv_w", 3), S("qk_conv_b")
            for name, before, first, n in (("km", 0, MH, TOK), ("qm", MH, 0, LAT)):
                def convolve(p, b, before=before, first=first, n=n):
                    if before + p >= 2:
                        dve.wait_ge(s["conv_act"], before + p - 1)
                    c = first + p
                    return conv_taps(conv[:, (before + p) % 2, 0:n], b[:, 0:n],
                                     [w[:, q, c:c + 1] for q in range(3)], cb[:, c:c + 1], n // 256)
                each_product(name, convolve)
            each_product("ka", lambda p, b: copy(ka[:, p, :], b[:, :]))
            each_product("qa", lambda p, b: copy(qa[:, p, :], b[:, 0:LAT]))
            each_product("om", lambda p, b: copy(om[:, p, :], b[:, 0:LAT]))
            taken("out0")
            dve.wait_ge(s["tables_in"], 16)
            cs, sn = (C0(x).unsqueeze(1) for x in ("cos", "sin"))
            for v, sw, n in ((qa, hm, 4), (ka[:, :, L0:L1], sq_m[:, 0:2, :], 2)):
                c3, s3 = cs.to_broadcast([P, n, LAT]), sn.to_broadcast([P, n, LAT])
                then(dve.stream_shuffle(sw, v, swap16))
                dve.tensor_tensor(v, v, c3, ALU.mult)
                then(dve.tensor_tensor(sw, sw, s3, ALU.mult))
                last = dve.tensor_tensor(v, v, sw, ALU.add)
            last.then_inc(s["rope_ready"], 1)
            dve.wait_ge(s["rope_ready"], 1)
            mlstm()
            attention(att0, 0, AH, AD ** -0.5, True, 4)
            residual("out0", 2, False)
            ffn0()
            final_norm("final_norm")
            if layers > 1:
                add_squares(0, TOK)
                adaln(1)
                norm(0, True)
                mixer1()
                residual("out1", 2, True)
                swiglu(1, True)
            if layers > 2:
                adaln(2)
                norm(0, True)
                mixer2()
                residual("out2", 2, False)
                swiglu(2, False)
                final_norm("final_norm_2")



def _columns(v):
    v = np.asarray(v)
    return v.reshape(-1, P).T


def _rows(v):
    return np.broadcast_to(np.asarray(v).reshape(1, -1), (P, np.asarray(v).size))


def _units(w, cols):
    w = np.asarray(w)
    k, n = w.shape
    return w.reshape(k // P, P, n // cols, cols).transpose(2, 1, 0, 3).reshape(n // cols, P, -1)


def _halves(w):
    w = np.asarray(w).reshape(2, FF // 2, KD, P).transpose(2, 0, 1, 3)
    return w.reshape(2 * KD, KF // 2, P, P).transpose(0, 2, 1, 3).reshape(2 * KD, P, -1)


def _pairs(a, b):
    a, b = np.asarray(a), np.asarray(b)
    return np.concatenate([a.reshape(D, -1, P), b.reshape(D, -1, P)], axis=2).reshape(D, -1)


def _tokens(x):
    return np.asarray(x)[0].T.reshape(KD, P, -1).transpose(1, 0, 2)


def _layout(i):
    small = {
        "c0": np.stack([_columns(i["c"][0]), _columns(i["c_ctx"])], 2).reshape(P, -1),
        "c1": np.stack([_columns(i["c_2"][0]), _columns(i["c_ctx_2"])], 2).reshape(P, -1),
        "b_ada0": _columns(i["b_ada"][0]), "b_ada1": _columns(i["b_ada_2"][0]),
        "b_ada2": _columns(i["b_ada_2"][1]),
        "norm_mix": _columns(i["norm_mix"][0]), "norm_ffn": _columns(i["norm_ffn"][0]),
        "gate_b": _rows(i["gate_b"][0]),
        "qk_conv_w": np.concatenate([_columns(t) for t in i["qk_conv_w"][0]], 1),
        "qk_conv_b": _columns(i["qk_conv_b"][0]), "mlstm_norm": _columns(i["mlstm_norm"][0]),
        "sink": _rows(i["attn_sink"][0]),
        "ffn_conv_w": np.concatenate([_columns(t) for t in i["ffn_conv_w"][0]], 1),
        "ffn_conv_b": _columns(i["ffn_conv_b"][0]), "final_norm": _columns(i["final_norm"]),
        "ssd_conv_w": np.concatenate([_columns(t) for t in i["ssd_conv_w_2"][0]], 1),
        "ssd_conv_b": _columns(i["ssd_conv_b_2"][0]), "dt_bias": _rows(i["ssd_dt_bias_2"][0]),
        "a_log": _rows(i["ssd_a_log_2"][0]), "ssd_d": _columns(np.repeat(i["ssd_d_2"][0], 64)),
        "ssd_norm": _columns(i["ssd_norm_w_2"][0]), "decay_logit": _rows(i["ret_decay_logit_2"][0]),
        "gn_w": _columns(i["ret_gn_w_2"][0]), "q_norm": _columns(i["mla_q_norm_w_2"][0]),
        "kv_norm": _columns(i["mla_kv_norm_w_2"][0]), "final_norm_2": _columns(i["final_norm_w_2"]),
    }
    w0, w1, w2 = (np.asarray(i[n][0]) for n in ("w_in", "ret_ssd_w_in_2", "mla_w_in_2"))
    m = MH * MD
    q0, k0, v0, o0, g0, qa0, ka0, va0 = np.split(w0, np.cumsum([m, m, m, m, 16, 512, 128]), axis=1)
    arrays = {"x": _tokens(i["x"]), "ctx": _tokens(i["ctx"]), "ctx_2": _tokens(i["ctx_2"]),
              "ada0": _units(i["w_ada"][0], P), "ada1": _units(i["w_ada_2"][0], P),
              "ada2": _units(i["w_ada_2"][1], P),
              "vm": _units(v0, P), "va_gates": _units(np.concatenate([va0, g0], 1), 144),
              "km": _units(k0, P), "qm": _units(q0, P),
              "ka": _units(np.concatenate([ka0[:, :64], ka0[:, :64], ka0[:, 64:], ka0[:, 64:]], 1), P),
              "qa": _units(qa0, P), "om": _units(o0, P), "out0": _units(i["w_out"][0], P)}
    up = np.asarray(i["w_up"][0])
    arrays["up0"] = _units(_pairs(up[:, :FF], up[:, FF:]), P)
    arrays["down0"] = _halves(i["w_down"][0])
    q1, k1, v1, g1, z1, xbc1, dt1 = np.split(w1, np.cumsum([512] * 5 + [1024]), axis=1)
    arrays["in1"] = _units(np.concatenate([q1, k1, g1, z1, xbc1], 1), P)
    arrays["vr"] = _units(v1, P)
    arrays["dt"] = _units(dt1, 16)
    arrays["out1"] = _units(i["ret_ssd_w_out_2"][0], P)
    for n in range(2):
        arrays[f"up{n + 1}"] = _units(_pairs(i["w_ffn_gate_2"][n], i["w_ffn_up_2"][n]), P)
        arrays[f"down{n + 1}"] = _halves(i["w_ffn_down_2"][n])
    arrays["cq"] = _units(w2[:, :768], P)
    arrays["ckv"] = _units(w2[:, 768:1024], P)
    arrays["kpe"] = _units(np.tile(w2[:, 1024:], (1, 4)), P)
    arrays["uq"] = _units(i["mla_w_uq_2"][0], 2 * LQ)
    ukv = np.asarray(i["mla_w_ukv_2"][0]).reshape(256, LH, LN + LV)
    arrays["uk"] = _units(ukv[:, :, :LN].reshape(256, -1), 512)
    arrays["uv"] = _units(ukv[:, :, LN:].reshape(256, -1), 512)
    arrays["out2"] = _units(i["mla_w_out_2"][0], P)
    arrays["small"] = np.concatenate(list(small.values()), 1)
    tables_at = []
    for n, tables in enumerate(constant_tables()):
        arrays[f"table{n}"] = np.concatenate(list(tables.values()), 1)
        tables_at.append(packed(tables)[0])
    return arrays, packed(small)[0], tables_at


def kernel(**inputs):
    import concourse.bacc as bacc
    from concourse.bass_utils import run_bass_kernel_spmd

    arrays, small_at, tables_at = _layout({k: np.asarray(v) for k, v in inputs.items()})
    nc = bacc.Bacc("TRN2", target_bir_lowering=False, num_devices=1)
    dram, feed = {}, {}
    for name, a in arrays.items():
        a = np.ascontiguousarray(a)
        feed[f"in_{name}"] = a
        dram[name] = nc.dram_tensor(f"in_{name}", a.shape, mybir.dt.from_np(a.dtype), kind="ExternalInput").ap()
    dram["out"] = nc.dram_tensor("out", (P, KD, LAT), F32, kind="ExternalOutput").ap()
    build(nc, dram, small_at, tables_at)
    r = run_bass_kernel_spmd(nc, [feed], core_ids=[0])
    y = np.asarray(r.results[0]["out"])
    return y.transpose(2, 1, 0).reshape(1, LAT, D)
```

```python
from contextlib import ExitStack

import numpy as np

import concourse.bass as bass
from concourse import mybir
from concourse.alu_op_type import AluOpType as ALU

ACT = mybir.ActivationFunctionType
F32 = mybir.dt.float32
F32R = mybir.dt.float32r
AX_X = mybir.AxisListType.X

P = 128
D = 1024
KD = D // P
CTX = LAT = 256
TOK = CTX + LAT
TT = TOK // P
L0, L1 = CTX, TOK
EPS = 1e-6
NEG = -1e30
FF = 2816
KF = FF // P
SLOTS = 3
SLOT = KD * P
THIRDS = ((0, 8), (8, 15), (15, KF))
BANKS = 3
ROUND = 6
ARENA = KF * 2 * TOK
AHEAD = 2

MH, MD = 4, 128
AH, AD = 8, 64
RH = 8
LH, LN, LR, LV = 16, 64, 32, 64
LQ = LN + LR



def constant_tables():
    p = np.arange(P)
    s = np.arange(2)[None, :, None] * P + p[:, None, None]
    t = np.arange(256)[None, None, :]
    upto, since = p[:, None] <= p[None, :], p[:, None] >= p[None, :]
    after = np.where(s <= t, 0.0, NEG)
    window = np.where(np.abs(s - t) <= 128, 0.0, NEG)
    row, col = np.arange(LAT) // 64, np.arange(LAT) % 64

    def rope(axes, pairs, signs):
        inv = np.float32(10000.0) ** (-np.arange(pairs, dtype=np.float32) / np.float32(pairs))
        ang = np.stack([np.float32(np.where(a, col, row)) * inv[x % pairs] for x, a in enumerate(axes)])
        return np.cos(ang), np.sin(ang) * signs[:, None]

    cos_a, sin_a = rope(p % 64 // 32, 16, np.where(p % 32 < 16, -1.0, 1.0))
    cos_r, sin_r = rope(p % 32 // 16, 16, np.where(p % 64 < 32, -1.0, 1.0))
    cos_l, sin_l = rope(p % 16 // 8, 8, np.where(p % 32 < 16, -1.0, 1.0))
    tables = (
        {"upto": upto, "since": since, "after": after, "before": np.where(s >= t, 0.0, NEG),
         "window": np.concatenate([np.zeros((P, 2, CTX)), window], axis=2),
         "cos": cos_a, "sin": sin_a},
        {"upto": upto, "since": since, "half_mean": (p[:, None] // 64 == p[None, :] // 64) / 64.0,
         "after": after, "before": np.where(s > t, 0.0, NEG),
         "dist_f": np.maximum(t - s, 0), "dist_b": np.maximum(s - t, 0),
         "far_f": CTX + t - s, "far_b": CTX + s - t, "cos": cos_r, "sin": sin_r},
        {"cos": cos_l, "sin": sin_l},
        {"ident": np.eye(P), "ones": np.ones((P, P)),
         "halves": (p[:, None] % 32 == 0) * (p[None, :] < 64) + (p[:, None] % 32 == 16) * (p[None, :] >= 64)},
    )
    return [{k: np.asarray(v, np.float32).reshape(P, -1) for k, v in x.items()} for x in tables]


def packed(parts):
    at, n = {}, 0
    for name, a in parts.items():
        at[name] = (n, n + a.shape[1])
        n += a.shape[1]
    return at, n



CARRIED = {"va_gates": (1, 2), "vm": (1, 2), "km": (1, 1), "qm": (1, 1), "ka": (1, 2), "qa": (1, 1), "om": (1, 1),
           "up0": (2, 1), "down0": (3, 1), "in1": (1, 1), "out1": (2, 1), "up1": (1, 1)}
CARRY = {"in1": 18}


class Phase:

    def __init__(self, name, units, width, steps=1, takes=1, parts=1):
        self.name, self.units, self.width = name, units, width
        self.steps, self.takes, self.parts = steps, takes, parts
        self.products = units * takes // parts
        self.round = 9 if parts == 3 else ROUND

    def tiles(self, u):
        return THIRDS[u % 3]

    def width_of(self, u):
        a, b = self.tiles(u)
        return self.width if self.parts == 1 else (b - a) * P

    def steps_after(self, u):
        if self.name in ("va_gates", "vm", "vr"):
            u = u // 2 * 2 + 1
        return self.first_step + (u + 1) * self.steps


def weight_phases():
    out = []

    def ffn(n):
        out.append(Phase(f"up{n}", 2 * KF, KD * P))
        out.append(Phase(f"down{n}", 3 * KD, SLOT, parts=3))

    out.append(Phase("va_gates", 2, KD // 2 * 144, 2, 2))
    out.append(Phase("vm", 4, KD * P, 2, 2))
    out.append(Phase("km", 4, KD * P))
    out.append(Phase("qm", 4, KD * P))
    out.append(Phase("ka", 2, KD * P))
    out.append(Phase("qa", 4, KD * P))
    out.append(Phase("om", 4, KD * P))
    out.append(Phase("out0", 8, KD * P))
    ffn(0)
    out.append(Phase("in1", 24, KD * P))
    out.append(Phase("vr", 4, KD * P, 2, 2))
    out.append(Phase("dt", 1, KD * 16, TT, TT))
    out.append(Phase("out1", 8, KD * P))
    ffn(1)
    out.append(Phase("cq", 6, KD * P))
    out.append(Phase("ckv", 2, KD * P))
    out.append(Phase("kpe", 1, KD * P))
    out.append(Phase("uq", LH, 6 * LQ))
    out.append(Phase("uk", 2, 2 * 512, 4, 4))
    out.append(Phase("uv", 2, 2 * 512, TT, TT))
    out.append(Phase("out2", 8, KD * P))
    ffn(2)
    unit = step = taken = 0
    ada = 16
    for f in out:
        f.every, f.number = CARRIED.get(f.name, (1, 0))
        f.first_ada, f.carry = ada, CARRY.get(f.name, f.units)
        ada += f.carry // f.every * f.number
        f.first_unit, f.first_step, f.first_taken = unit, step, taken
        unit += f.units
        step += f.units * f.steps
        taken += f.products
    assert ada == 3 * 48
    return {f.name: f for f in out}


class Chain:

    def __init__(self, engine, sem):
        self.engine, self.sem, self.n, self.moving = engine, sem, 0, 0

    def then(self, instruction):
        self.n += 1
        instruction.then_inc(self.sem, 1)
        self.engine.wait_ge(self.sem, self.moving + self.n)


def unit_rounds(engine, start, stop, body, chain=None, links=0, size=ROUND):
    rounds, left = divmod(stop - start, size)
    if rounds > 1:
        n0 = chain.n if chain else 0
        with engine.Fori(0, rounds) as r:
            if chain:
                chain.moving = r * links
            for j in range(start, start + size):
                body(r * size + j, j, r)
        if chain:
            assert chain.n == n0 + links, chain.n - n0
            chain.moving, chain.n = 0, n0 + rounds * links
    else:
        for u in range(start, start + rounds * size):
            body(u, u, 0)
    for u in range(start + rounds * size, stop):
        body(u, u, 0)


def build(nc, dram, small_at, tables_at, layers=3):
    ph = weight_phases()
    run = [n for n in ph]
    if layers < 3:
        run = run[:run.index("in1" if layers == 1 else "cq")]
    with ExitStack() as stack:
        def sb(name, shape):
            return stack.enter_context(nc.sbuf_tensor(name, shape, F32))

        def sbr(name, shape):
            return stack.enter_context(nc.sbuf_tensor(name, shape, F32R))

        def sem(name):
            return stack.enter_context(nc.semaphore(name))

        raw = sb("raw", [P, SLOTS, SLOT])
        w_hi = sbr("w_hi", [P, SLOTS, SLOT])
        w_lo = sbr("w_lo", [P, SLOTS, SLOT])
        X = sb("X", [P, KD, TOK])
        small = sb("small", [P, max(b for _, b in small_at.values())])
        fixed = sb("fixed", [P, 3 * P])
        ada_w = sb("ada_w", [P, SLOTS, D])
        cond = sb("cond", [P, 2, D])
        ada_sums = sb("ada_sums", [P, SLOTS, 2])
        mod = sb("mod", [P, 2, 48, 2])
        gain = sb("gain", [P, 2, KD, 2])
        std = sb("std", [P, TOK])
        token_std = sb("token_std", [P, TT])
        token_inv = sb("token_inv", [P, TT])
        token_m = sb("token_m", [P, 2, 2 * MH])
        sq_sum = sb("sq_sum", [P, TOK])
        with nc.sbuf_tensor("arena", [P, ARENA], F32) as arena:
            pass
        with (nc.sbuf_tensor("hidden_hi", [P, KF, TOK], F32R) as hidden_hi,
              nc.sbuf_tensor("hidden_lo", [P, KF, TOK], F32R) as hidden_lo):
            pass
        stack.enter_context(nc.sbuf_tensor("arena_end", [P, ARENA], F32))
        with nc.sbuf_tensor("scratch", [P, 2 * KD * TOK], F32) as scratch:
            pass
        with (nc.sbuf_tensor("cq_hi", [P, 6, LAT], F32R) as cq_hi,
              nc.sbuf_tensor("cq_lo", [P, 6, LAT], F32R) as cq_lo,
              nc.sbuf_tensor("ckv_hi", [P, 2, TOK], F32R) as ckv_hi,
              nc.sbuf_tensor("ckv_lo", [P, 2, TOK], F32R) as ckv_lo):
            pass
        h_hi, h_lo = sbr("h_hi", [P, KD, TOK]), sbr("h_lo", [P, KD, TOK])
        work = sb("work", [P, 3, TOK])
        bank = [stack.enter_context(nc.psum_tensor(f"bank{i}", [P, 512], F32)) for i in range(6)]
        products = stack.enter_context(nc.psum_tensor("products", [P, 1024], F32))
        bank += [products[:, 0:512], products[:, 512:1024]]

        def S(name, *dims):
            a, b = small_at[name]
            v = small[:, a:b]
            if dims:
                return v.rearrange("p (a b) -> p a b", a=dims[0])
            return v

        def tables(layer):
            at = tables_at[layer]
            start = ARENA - max(b for _, b in at.values())

            def C(name, a=None):
                v = arena[:, start + at[name][0]:start + at[name][1]]
                return v.rearrange("p (a b) -> p a b", a=a) if a else v
            return C, arena[:, start:]

        (C0, room0), (C1, room1), (C2, room2) = (tables(i) for i in range(3))
        ident, ones, halves = (fixed[:, i * P:(i + 1) * P] for i in range(3))

        class Carve:
            def __init__(self, tensor, at=0, limit=ARENA):
                self.tensor, self.at, self.limit = tensor, at, limit

            def __call__(self, *dims):
                n = int(np.prod(dims))
                v = self.tensor[:, self.at:self.at + n]
                self.at += n
                assert self.at <= self.limit, self.at
                if len(dims) == 2:
                    return v.rearrange("p (a b) -> p a b", a=dims[0])
                if len(dims) == 3:
                    return v.rearrange("p (a b c) -> p a b c", a=dims[0], b=dims[1])
                return v

        def attention_memory(c):
            return dict(masked=[c(512) for _ in range(3)], prob=[c(512) for _ in range(3)],
                        turned=[c(4, LAT), c(4, LAT)],
                        peak=c(32), nmax=c(32), total=c(32), esink=c(32), nsink=c(8))

        def limit(layer):
            return ARENA - max(b for _, b in tables_at[layer].values())

        c = Carve(arena, 0, limit(0))
        qm, km = c(MH, LAT), c(MH, TOK)
        vm, va, gates = c(TT, 512), c(TT, P), c(TT, 16)
        om, qa, ka = c(MH, LAT), c(4, LAT), c(2, TOK)
        att0 = attention_memory(Carve(arena, c.at, limit(0)))
        lf, gtmp = c(TT, 16), c(TT, 16)
        g_cum, g_bias = c(2, TT, MH), c(2, TT, MH)
        rows, run_max, top = c(4, LAT), c(2 * 512), c(2)
        conv = c(2, TOK)
        narg = c(2, 3, LAT)
        den_a, den_e, hid = c(512), [c(512), c(512)], c(512)
        hm, sq_m, sig = c(MH, LAT), c(MH, LAT), c(MH, LAT)
        c = Carve(scratch)
        ex, prob_m = c(2, TT, LAT), [c(2 * TT, LAT), c(2 * TT, LAT)]
        c = Carve(arena, 0, limit(1))
        t1 = c(24, TOK)
        vr, y1 = c(TT, 512), c(8, TOK)
        dt, log_r, nega, decay_tmp = c(TT, 16), c(16), c(16), c(16)
        c = Carve(scratch, 0, 8192)
        xt, grow = c(TT, 512), c(2, TOK)
        y_sq = Carve(scratch, c.at)(4, 512)
        c2 = Carve(t1.rearrange("p a b -> p (a b)"))
        ea, eb, pr = ([x(3, 512) for x in (c, c2)] for _ in range(3))
        c = Carve(scratch, 0, 7680)
        ra, rb, rp = ([c(*n), c(*n)] for n in ((3, 512), (2, LAT), (3, 512)))
        swap_r = y1[:, 0:4, :].rearrange("p a (b t) -> p (a b) t", b=2)
        conv1 = y1[:, 4:6, :]
        c = Carve(scratch, 3072 + 3 * 3 * 512, 8192)
        dtmp, la = c(TT, 16), c(TT, 16)
        gs, ngs = c(2, TT, RH), c(2, TT, RH)
        c = Carve(arena, 0, limit(2))
        qh, kh, vl = c(LH, LAT), c(LH, TOK), c(TT, 1024)
        att2 = attention_memory(Carve(arena, c.at, limit(2)))
        cq, ckv, kpe = c(6, LAT), c(2, TOK), c(TOK)
        kswap = c(2, 2 * LAT)
        sq_l = c(2, TOK)

        def cq_sq(i):
            return scratch[:, 5632 + i * LAT:5632 + (i + 1) * LAT]


        names = [
            "small_in", "fixed_in", "x_in", "ctx2_in", "tables_in", "out_done",
            "rounded", "split", "steps", "taken",
            "cond_in", "cond_ready", "ada_sum", "ada_used",
            "squared", "added", "sums_in", "sum_ready", "std_ready", "inverse_ready", "inverse_spread", "h_work", "h_round", "h_split",
            "x_ready",
            "vector_order", "scalar_order",
            "conv_act", "lf_in", "lf_exp", "lf_ready", "cum_ready", "cum_taken", "rows_ready",
            "rows_taken", "ml_bcast", "ml_s", "ml_arg", "ml_e", "ml_p", "ml_num", "ml_h", "ml_sq",
            "ml_sum", "ml_std", "ml_inv", "ml_spread", "ml_gate", "ml_y", "rope_ready",
            "att_s", "att_m", "att_e", "att_p", "att_t", "att_pt", "att_o", "att_y",
            "up_conv", "up_act", "hid_done",
            "swap_done", "rt_sum", "sd_dt", "rt_s", "rt_arg", "rt_e", "rt_p", "rt_o", "rt_y",
            "gn_mid", "gn_inv", "gn_in", "gn_sum", "gn_std", "gn_act", "gn_done", "sd_t", "sd_tt", "sd_b", "sd_s",
            "sd_arg", "sd_e", "sd_p", "sd_o", "sd_y", "sn_in", "sn_sum", "sn_std",
            "lq_in", "lq_sum", "lq_std", "lq_done", "kpe_in", "kpe_done"]
        s = {n: sem(n) for n in names}
        full = [sem(f"slot_full{i}") for i in range(SLOTS)]

        ada_full = [sem(f"ada_full{i}") for i in range(SLOTS)]

        all_units = [(ph[n], u) for n in run for u in range(ph[n].units)]

        def loaded(engine, f, j, r):
            g = f.first_unit + j
            engine.wait_ge(full[g % SLOTS], r * (16 * ROUND // SLOTS) + 16 * (g // SLOTS + 1))

        def raw_slot(f, j):
            return raw[:, (f.first_unit + j) % SLOTS, 0:f.width_of(j)]

        def part_slot(part, f, j, k=None):
            v = part[:, (f.first_unit + j) % SLOTS, 0:f.width_of(j)]
            return v.rearrange("p (k n) -> p k n", k=k) if k else v

        def source(f, j, r):
            if f.parts == 1:
                return dram[f.name][r * f.round + j]
            a, b = f.tiles(j)
            return dram[f.name][r * (f.round // 3) + j // 3][:, a * P:b * P]

        def bank_of(t):
            return bank[t % BANKS]

        def parts(v, i):
            return v[:, i, :] if i < 2 else v[:, 2, (i - 2) * LAT:(i - 1) * LAT]

        def decay_bank(q):
            return (bank[3], bank[4], bank[7])[q % 3]

        def score_bank(a):
            return (bank[0], bank[1], bank[6])[a % 3]

        block = stack.enter_context(nc.Block())

        @block.sync
        def _(sp):
            sp.dma_start(small[:, :], dram["small"]).then_inc(s["small_in"], 16)

            def load(g):
                f, u = all_units[g]
                if g >= SLOTS:
                    f0, u0 = all_units[g - SLOTS]
                    sp.wait_ge(s["split"], f0.first_unit + u0 + 1)
                sp.dma_start(raw_slot(f, u), source(f, u, 0)).then_inc(full[g % SLOTS], 16)
                if g >= SLOTS:
                    load_carried(f0, u0, 0)

            def load_ada(k, more=0):
                if k >= SLOTS:
                    sp.wait_ge(s["ada_used"], more + (k - SLOTS + 1))
                sp.dma_start(ada_w[:, k % SLOTS, :], dram[f"ada{k // 48}"][more + k % 48])\
                  .then_inc(ada_full[k % SLOTS], 16)

            def load_carried(f, j, r):
                if j % f.every == 0 and j < f.carry:
                    for q in range(f.number):
                        load_ada(f.first_ada + j // f.every * f.number + q, r * (f.round // f.every * f.number))

            def load_in_phase(f):
                def body(u, j, r):
                    sp.wait_ge(s["split"], r * f.round + (f.first_unit + j - SLOTS + 1))
                    sp.dma_start(raw_slot(f, j), source(f, j, r)).then_inc(full[(f.first_unit + j) % SLOTS], 16)
                    load_carried(f, j - SLOTS, r)
                return body

            sp.dma_start(cond[:, :, :], dram["cond0"]).then_inc(s["cond_in"], 16)
            for k in range(3):
                load_ada(k)
            sp.dma_start(X[:, :, L0:L1], dram["x"]).then_inc(s["x_in"], 16)
            sp.dma_start(X[:, :, 0:L0], dram["ctx"]).then_inc(s["x_in"], 16)
            sp.dma_start(fixed[:, :], dram["table3"]).then_inc(s["fixed_in"], 16)
            for k in range(3, 16):
                load_ada(k)
            g = 0
            for name in run:
                f = ph[name]
                if name == "up0":
                    sp.wait_ge(s["ada_used"], 48)
                    sp.dma_start(cond[:, :, :], dram["cond1"]).then_inc(s["cond_in"], 16)
                for u in range(min(f.units, SLOTS)):
                    load(g + u)
                    if g + u == 2:
                        sp.dma_start(room0, dram["table0"]).then_inc(s["tables_in"], 16)
                if f.units > SLOTS:
                    unit_rounds(sp, SLOTS, f.units, load_in_phase(f), size=f.round)
                g += f.units
            sp.wait_ge(s["x_ready"], 2 if layers == 3 else 1)
            if layers == 2:
                sp.wait_ge(s["taken"], ph["cq"].first_taken)
            sp.dma_start(dram["out"], X[:, :, L0:L1]).then_inc(s["out_done"], 16)
            sp.wait_ge(s["out_done"], 16)

        @block.tensor
        def _(pe):
            norms = [0]
            h_ready = [0]

            def room(t, r=0, per_round=0):
                if t >= BANKS:
                    pe.wait_ge(s["taken"], r * per_round + (t - BANKS + 1))

            def three(out, w_h, w_l, x_h, x_l, first, last):
                pe.matmul(out, w_h, x_h, start=first, stop=False)
                pe.matmul(out, w_h, x_l, start=False, stop=False)
                return pe.matmul(out, w_l, x_h, start=False, stop=last)

            def feature_sums(t0, t1):
                norms[0] += 1
                pe.wait_ge(s["sums_in"], norms[0])
                if norms[0] == 1:
                    pe.wait_ge(s["fixed_in"], 16)
                for i in range(t0 // P, t1 // P):
                    last = pe.matmul(bank[4][:, i:i + 1], sq_sum[:, i * P:(i + 1) * P], ones[:, 0:1],
                                     start=True, stop=True)
                last.then_inc(s["sum_ready"], 1)
                pe.wait_ge(s["inverse_ready"], norms[0])
                for i in range(t0 // P, t1 // P):
                    last = pe.matmul(bank[5][:, i * P:(i + 1) * P], token_inv[:, i:i + 1].to_broadcast([P, P]), ident,
                                     start=True, stop=True)
                last.then_inc(s["inverse_spread"], 1)

            def next_h():
                base = h_ready[0]
                h_ready[0] += KD
                return lambda k: pe.wait_ge(s["h_split"], base + k + 1)

            def linear(name, t0, t1, K=KD, hi=None, lo=None, M=P, gate=None):
                f = ph[name]
                hi, lo = (h_hi, h_lo) if hi is None else (hi, lo)
                n, parts = t1 - t0, f.parts

                def body(u, j, r):
                    pe.wait_ge(s["split"], r * f.round + (f.first_unit + j + 1))
                    k0, k1 = f.tiles(j) if parts > 1 else (0, K)
                    w_h, w_l = (part_slot(x, f, j, k1 - k0) for x in (w_hi, w_lo))
                    t = f.first_taken + j // parts
                    if j % parts == 0:
                        room(t, r, f.round // parts)
                    for k in range(k0, k1):
                        if gate and u is j and j < parts:
                            gate(k)
                        last = three(bank_of(t)[0:M, 0:n], w_h[:, k - k0], w_l[:, k - k0],
                                     hi[:, k, t0:t1], lo[:, k, t0:t1], k == 0, k == K - 1)
                    last.then_inc(s["steps"], 1)

                if gate:
                    for u in range(parts):
                        body(u, u, 0)
                    unit_rounds(pe, parts, f.units, body, size=f.round)
                else:
                    unit_rounds(pe, 0, f.units, body, size=f.round)

            def token_linear(name, K=KD, hi=None, lo=None, gate=None):
                f = ph[name]
                hi, lo = (h_hi, h_lo) if hi is None else (hi, lo)
                pair = 2 if f.steps == 2 else 1
                halves = name == "va_gates"
                for u in range(0, f.units, pair):
                    pe.wait_ge(s["split"], f.first_unit + u + pair)
                    if halves:
                        w_h, w_l = ([part_slot(x, f, k // (K // 2), K // 2)[:, k % (K // 2)] for k in range(K)]
                                    for x in (w_hi, w_lo))
                    elif pair == 2:
                        a, b = ((f.first_unit + u + i) % SLOTS for i in range(2))
                        two = slice(a, b + 1) if b > a else slice(a, None, -a)
                        w_h, w_l = ([x[:, two, 0:f.width].rearrange("p s (k n) -> p k s n", k=K)[:, k]
                                     for k in range(K)] for x in (w_hi, w_lo))
                    else:
                        w_h, w_l = ([part_slot(x, f, u, K)[:, k] for k in range(K)] for x in (w_hi, w_lo))
                    cols = pair * f.width // K
                    for i in range(TT):
                        t = f.first_taken + u * f.takes + i
                        room(t)
                        out = bank_of(t)[:, 0:cols]
                        if pair == 2 and not halves:
                            out = out.rearrange("p (s n) -> p s n", s=2)
                        for k in range(K):
                            if gate and u == 0 and i == 0:
                                gate(k)
                            last = three(out, hi[:, k, i * P:(i + 1) * P], lo[:, k, i * P:(i + 1) * P],
                                         w_h[k], w_l[k], k == 0, k == K - 1)
                        last.then_inc(s["steps"], 1)

            def cumulate(src, off, heads, b, C):
                for d in range(2):
                    order = (0, 1, 2, 3) if d == 0 else (1, 0, 3, 2)
                    for n, i in enumerate(order):
                        col = (d * TT + i) * heads
                        out = b[:, col:col + heads]
                        for e in range(n):
                            pe.matmul(out, ones, src[:, order[e], off[d]:off[d] + heads],
                                      start=(e == 0), stop=False)
                        last = pe.matmul(out, C("upto" if d == 0 else "since"),
                                         src[:, i, off[d]:off[d] + heads], start=(n == 0), stop=True)
                return last

            def gate_sums():
                pe.wait_ge(s["lf_ready"], 1)
                cumulate(lf, (4, 12), MH, bank[4], C0).then_inc(s["cum_ready"], 1)

            def gate_rows():
                pe.wait_ge(s["cum_taken"], 1)
                for d in range(2):
                    for i in range(TT):
                        pe.matmul(bank[3 + d][0:MH, i * P:(i + 1) * P], g_bias[:, d, i, :], ident,
                                  start=True, stop=True)
                for d in range(2):
                    for i in range(2):
                        last = pe.matmul(bank[5][0:MH, d * LAT + i * P:d * LAT + (i + 1) * P],
                                         g_cum[:, d, 2 + i, :], ident, start=True, stop=True)
                last.then_inc(s["rows_ready"], 1)

            def mlstm():
                pe.wait_ge(s["rows_taken"], 1)
                pe.wait_ge(s["taken"], ph["out0"].first_taken)

                def before(h):
                    pick = ident[0:MH, h:h + 1].to_broadcast([MH, P])
                    if h:
                        pe.wait_ge(s["ml_e"], 2 * h)
                        pe.wait_ge(s["ml_arg"], h)
                    for i in range(2):
                        last = pe.matmul(bank[i][:, :], pick, rows[0:MH, 2 * i:2 * i + 2, :],
                                         start=True, stop=True)
                    last.then_inc(s["ml_bcast"], 1)
                    if h:
                        pe.wait_ge(s["ml_p"], h)
                    for i in range(TT):
                        last = pe.matmul(bank[2 + i // 2][:, (i % 2) * LAT:(i % 2 + 1) * LAT],
                                         km[:, h, i * P:(i + 1) * P], qm[:, h, :], start=True, stop=True)
                    last.then_inc(s["ml_s"], 1)

                def sums(h):
                    pe.wait_ge(s["ml_p"], h + 1)
                    if h:
                        pe.wait_ge(s["ml_h"], h)
                    for d in range(2):
                        for i in range(TT):
                            pe.matmul(bank[4][:, d * LAT:(d + 1) * LAT], vm[:, i, h * MD:(h + 1) * MD],
                                      prob_m[h % 2][:, d * TT + i, :], start=(i == 0), stop=(i == TT - 1))
                    for d in range(2):
                        for i in range(TT):
                            last = pe.matmul(bank[5][:, d * LAT:(d + 1) * LAT], ones,
                                             prob_m[h % 2][:, d * TT + i, :], start=(i == 0), stop=(i == TT - 1))
                    last.then_inc(s["ml_num"], 1)

                before(0)
                for h in range(MH):
                    if h + 1 < MH:
                        before(h + 1)
                    sums(h)
                pe.wait_ge(s["ml_sq"], 1)
                for i in range(2 * MH):
                    last = pe.matmul(bank[6][:, i:i + 1], sq_m[:, i // 2, i % 2 * P:(i % 2 + 1) * P], ones[:, 0:1],
                                     start=True, stop=True)
                last.then_inc(s["ml_sum"], 1)
                pe.wait_ge(s["ml_inv"], 1)
                for i in range(2 * MH):
                    last = pe.matmul(bank[i // 4][:, i % 4 * P:(i % 4 + 1) * P],
                                     token_m[:, 1, i:i + 1].to_broadcast([P, P]), ident, start=True, stop=True)
                last.then_inc(s["ml_spread"], 1)

            def attention(m, a0, heads, q, k, v):
                count = 2 * heads

                def scores(a):
                    h, t = divmod(a, 2)
                    if a >= 3:
                        pe.wait_ge(s["att_e"], a0 + a - 2)
                    pe.matmul(score_bank(a)[:, :], q(h)[:, t * P:(t + 1) * P], k(h),
                              start=True, stop=True).then_inc(s["att_s"], 1)

                def turn(a):
                    pe.wait_ge(s["att_p"], a0 + a + 1)
                    if a >= 2:
                        pe.wait_ge(s["att_pt"], a0 + a - 1)
                    for i in range(TT):
                        last = pe.transpose(bank[2 + a % 2][:, i * P:(i + 1) * P],
                                            m["prob"][a % 3][:, i * P:(i + 1) * P], ident)
                    last.then_inc(s["att_t"], 1)

                def values(h):
                    pe.wait_ge(s["att_pt"], a0 + 2 * h + 2)
                    if h >= 4 and h % 2 == 0:
                        pe.wait_ge(s["att_y"], a0 // 4 + h // 2 - 1)
                    for i in range(TT):
                        last = pe.matmul(bank[4 + (h // 2) % 2][64 * (h % 2):64 * (h % 2) + 64, 0:LAT],
                                         v(h, i), m["turned"][h % 2][:, i, :],
                                         start=(i == 0), stop=(i == TT - 1))
                    last.then_inc(s["att_o"], 1)

                for a in range(3):
                    scores(a)
                for a in range(count):
                    turn(a)
                    if a + 3 < count:
                        scores(a + 3)
                    if a % 2 and a > 2:
                        values(a // 2 - 1)
                values(heads - 1)

            def mixer1():
                def ret_scores(h):
                    t, p0, b = h // 2, 64 * (h % 2), 3 * (h % 2)
                    if h >= 2:
                        pe.wait_ge(s["rt_p"], h - 1)
                    for i in range(2):
                        pe.matmul(bank[b + i][:, :], t1[p0:p0 + 64, 4 + t, i * P:(i + 1) * P],
                                  t1[p0:p0 + 64, t, :], start=True, stop=True)
                    for i in range(2, TT):
                        last = pe.matmul(bank[b + 2][:, (i - 2) * LAT:(i - 1) * LAT],
                                         t1[p0:p0 + 64, 4 + t, i * P:(i + 1) * P],
                                         t1[p0:p0 + 64, t, L0:L1], start=True, stop=True)
                    last.then_inc(s["rt_s"], 1)

                def weighted(h, v, ready, taken, out, done, pr):
                    t, p0 = h // 2, 64 * (h % 2)
                    pe.wait_ge(ready, h + 1)
                    if t >= 2 and h % 2 == 0:
                        pe.wait_ge(taken, t - 1)
                    b = bank[out + t % 2]
                    for i in range(TT):
                        lat = i >= 2
                        last = pe.matmul(b[p0:p0 + 64, L0 if lat else 0:L1], v[:, i, h * 64:(h + 1) * 64],
                                         pr[h % 2][:, 2, (i - 2) * LAT:(i - 1) * LAT] if lat else pr[h % 2][:, i, :],
                                         start=(i == 0), stop=(i == TT - 1))
                    last.then_inc(done, 1)

                pe.wait_ge(s["rope_ready"], 2)
                pe.wait_ge(s["taken"], ph["out1"].first_taken)
                ret_scores(0)
                for h in range(RH):
                    if h + 1 < RH:
                        ret_scores(h + 1)
                    weighted(h, vr, s["rt_p"], s["rt_y"], 6, s["rt_o"], rp)
                def turn_xs(i):
                    for j in range(4):
                        last = pe.transpose(bank[5 + i % 2][:, j * P:(j + 1) * P], t1[:, 16 + j, i * P:(i + 1) * P],
                                            ident)
                    last.then_inc(s["sd_t"], 1)

                pe.wait_ge(s["rt_y"], 4)
                for i in range(4):
                    pe.matmul(bank[i][:, :], C1("half_mean"), y1[:, i, :], start=True, stop=True)\
                      .then_inc(s["gn_sum"], 1)
                pe.wait_ge(s["conv_act"], 8 + 8)
                turn_xs(0)
                turn_xs(1)
                pe.wait_ge(s["lf_ready"], 2)
                cumulate(la, (0, 8), RH, bank[7], C1).then_inc(s["cum_ready"], 1)
                for i in range(4):
                    pe.wait_ge(s["gn_in"], i + 1)
                    last = pe.matmul(bank[4][32 * i:32 * i + 32, :], C1("half_mean")[:, ::4], y_sq[:, i, :],
                                     start=True, stop=True)
                last.then_inc(s["gn_sum"], 1)
                for i in range(2, TT):
                    pe.wait_ge(s["sd_tt"], i - 1)
                    turn_xs(i)
                pe.wait_ge(s["gn_inv"], 1)
                for i in range(4):
                    pe.matmul(bank[i][:, :], halves[32 * i:32 * i + 32, :], std[32 * i:32 * i + 32, :],
                              start=True, stop=True).then_inc(s["gn_sum"], 1)
                pe.wait_ge(s["cum_taken"], 2)
                pe.wait_ge(s["sd_tt"], TT)
                for d in range(2):
                    for i in range(TT):
                        last = pe.matmul(bank[5 + d][0:RH, i * P:(i + 1) * P], gs[:, d, i, :], ident,
                                         start=True, stop=True)
                last.then_inc(s["rows_ready"], 1)
                pe.wait_ge(s["gn_done"], 1)

                def ssd_scores(g):
                    if g:
                        pe.wait_ge(s["sd_p"], 4)
                    for i in range(2):
                        pe.matmul(bank[i][:, :], t1[:, 20 + g, i * P:(i + 1) * P], t1[:, 22 + g, :],
                                  start=True, stop=True)
                    for i in range(2, TT):
                        last = pe.matmul(bank[2][:, (i - 2) * LAT:(i - 1) * LAT],
                                         t1[:, 20 + g, i * P:(i + 1) * P], t1[:, 22 + g, L0:L1],
                                         start=True, stop=True)
                    last.then_inc(s["sd_s"], 1)

                def spread(q):
                    h, d = divmod(q, 2)
                    if q >= 3:
                        pe.wait_ge(s["sd_e"], q - 2)
                    pe.matmul(decay_bank(q)[:, :], ident[0:RH, h:h + 1].to_broadcast([RH, P]), grow[0:RH, d, :],
                              start=True, stop=True).then_inc(s["sd_b"], 1)

                ssd_scores(0)
                pe.wait_ge(s["rows_taken"], 2)
                for q in range(5):
                    spread(q)
                for h in range(RH):
                    if h + 3 <= RH:
                        spread(2 * h + 5)
                    weighted(h, xt, s["sd_p"], s["sd_y"], 5, s["sd_o"], pr)
                    if h + 4 <= RH:
                        spread(2 * h + 6)
                    if h == 3:
                        ssd_scores(1)
                for i in range(4):
                    pe.wait_ge(s["sn_in"], i + 1)
                    last = pe.matmul(bank[7][:, :], ones, y_sq[:, i, :], start=(i == 0), stop=(i == 3))
                last.then_inc(s["sn_sum"], 1)

            def latent_norms():
                for i in range(6):
                    pe.wait_ge(s["lq_in"], i + 1)
                    last = pe.matmul(bank[6][:, 0:LAT], ones, cq_sq(i), start=(i == 0), stop=(i == 5))
                last.then_inc(s["lq_sum"], 1)
                for i in range(2):
                    pe.wait_ge(s["lq_in"], 7 + i)
                    last = pe.matmul(bank[7][:, :], ones, sq_l[:, i, :], start=(i == 0), stop=(i == 1))
                last.then_inc(s["lq_sum"], 1)

            def ffn(n, t0, t1):
                feature_sums(t0, t1)
                linear(f"up{n}", t0, t1, gate=next_h())
                linear(f"down{n}", t0, t1, K=KF, hi=hidden_hi, lo=hidden_lo,
                       gate=lambda k: pe.wait_ge(s["hid_done"], KF * n + k + 4))

            feature_sums(0, TOK)
            token_linear("va_gates", gate=next_h())
            token_linear("vm")
            linear("km", 0, TOK)
            pe.wait_ge(s["tables_in"], 16)
            gate_sums()
            linear("qm", L0, L1)
            linear("ka", 0, TOK)
            gate_rows()
            linear("qa", L0, L1)
            linear("om", L0, L1)
            mlstm()
            pe.wait_ge(s["rope_ready"], 1)
            pe.wait_ge(s["ml_gate"], 1)
            attention(att0, 0, AH,
                      lambda h: qa[64 * (h % 2):64 * (h % 2) + 64, h // 2, :],
                      lambda h: ka[64 * (h % 2):64 * (h % 2) + 64, h // 4, :],
                      lambda h, i: va[:, i, (h // 4) * 64:(h // 4) * 64 + 64])
            pe.wait_ge(s["ml_y"], 1)
            pe.wait_ge(s["att_y"], AH // 2)
            linear("out0", L0, L1)
            ffn(0, L0, L1)
            feature_sums(L0, L1)
            if layers == 1:
                return
            feature_sums(0, TOK)
            linear("in1", 0, TOK, gate=next_h())
            token_linear("vr")
            token_linear("dt")
            mixer1()
            linear("out1", 0, TOK, gate=next_h())
            ffn(1, 0, TOK)
            if layers == 2:
                return
            feature_sums(0, TOK)
            linear("cq", L0, L1, gate=next_h())
            linear("ckv", 0, TOK)
            linear("kpe", 0, TOK)
            latent_norms()
            linear("uq", 0, LAT, K=6, hi=cq_hi, lo=cq_lo, M=LQ,
                   gate=lambda k: pe.wait_ge(s["lq_done"], 1))
            pe.wait_ge(s["lq_done"], 2)
            f = ph["uk"]
            for u in range(f.units):
                pe.wait_ge(s["split"], f.first_unit + u + 1)
                w_h, w_l = (part_slot(x, f, u, 2) for x in (w_hi, w_lo))
                for i in range(4):
                    t = f.first_taken + 4 * u + i
                    room(t)
                    for k in range(2):
                        last = three(bank_of(t)[:, :], w_h[:, k, i * P:(i + 1) * P], w_l[:, k, i * P:(i + 1) * P],
                                     ckv_hi[:, k, :], ckv_lo[:, k, :], k == 0, k == 1)
                    last.then_inc(s["steps"], 1)
            token_linear("uv", K=2, hi=ckv_hi, lo=ckv_lo)
            pe.wait_ge(s["taken"], ph["out2"].first_taken)
            pe.wait_ge(s["kpe_done"], 1)
            attention(att2, 2 * AH, LH, lambda h: qh[0:LQ, h, :], lambda h: kh[0:LQ, h, :],
                      lambda h, i: vl[:, i, h * LV:(h + 1) * LV])
            pe.wait_ge(s["att_y"], AH // 2 + LH // 2)
            linear("out2", L0, L1)
            ffn(2, L0, L1)
            feature_sums(L0, L1)

        @block.scalar
        def _(act):
            chain = Chain(act, s["scalar_order"])
            norms = [0]
            h_count = [0]
            rounded = [0]

            def round_next():
                q = rounded[0]
                rounded[0] += 1
                f, u = all_units[q]
                loaded(act, f, u, 0)
                if q >= SLOTS:
                    f0, u0 = all_units[q - SLOTS]
                    act.wait_ge(s["steps"], f0.steps_after(u0))
                act.activation(part_slot(w_hi, f, u), raw_slot(f, u), ACT.Copy).then_inc(s["rounded"], 1)

            def phase(name, job=None, more=True, looped=None):
                f = ph[name]
                assert rounded[0] == f.first_unit + min(AHEAD, f.units) or f.units < AHEAD, name

                def alone(u):
                    q = f.first_unit + u + AHEAD
                    if q < len(all_units) and (more or u + AHEAD < f.units) and rounded[0] <= q:
                        round_next()
                    if job:
                        job(u, u, 0)

                def body(u, j, r):
                    w = j + AHEAD
                    loaded(act, f, w, r)
                    act.wait_ge(s["steps"], r * ROUND + (f.first_step + w - SLOTS + 1))
                    act.activation(part_slot(w_hi, f, w), raw_slot(f, w), ACT.Copy).then_inc(s["rounded"], 1)
                    if job:
                        job(u, j, r)

                stop = looped or f.units - AHEAD
                if stop - 1 >= 2 * ROUND and f.parts == 1:
                    alone(0)
                    unit_rounds(act, 1, stop, body)
                    rounded[0] += stop - 1
                    for u in range(stop, f.units):
                        alone(u)
                else:
                    for u in range(f.units):
                        alone(u)

            def square(k, t0, t1):
                if k > SLOTS:
                    act.wait_ge(s["added"], norms[0] * (KD - 1) + k - 3)
                dst = work[:, k % 3, t0:t1] if k else sq_sum[:, t0:t1]
                act.activation(dst, X[:, k, t0:t1], ACT.Square).then_inc(s["squared"], 1)

            def squares(t0, t1):
                for k in range(KD):
                    square(k, t0, t1)

            def rms_std(t0, t1):
                norms[0] += 1
                act.wait_ge(s["sum_ready"], norms[0])
                act.activation(token_std[:, t0 // P:t1 // P], bank[4][:, t0 // P:t1 // P], ACT.Sqrt,
                               scale=1.0 / D, bias=EPS)\
                   .then_inc(s["std_ready"], 1)

            def round_h(src, t0, t1):
                for k in range(KD):
                    act.wait_ge(s["h_work"], h_count[0] + k + 1)
                    act.activation(h_hi[:, k, t0:t1], src(k)[:, t0:t1], ACT.Copy).then_inc(s["h_round"], 1)
                h_count[0] += KD

            def work_tile(k):
                return work[:, k % 3, :]

            def softplus_part(ready, x):
                act.wait_ge(s["lf_in"], ready)
                chain.then(act.activation(x, x, ACT.Exp))
                act.activation(x, x, ACT.Ln, bias=1.0).then_inc(s["lf_exp"], 1)

            def attention(m, a0, heads, scale, sinks):
                def exps(a):
                    act.wait_ge(s["att_m"], a0 + a + 1)
                    if a >= 3:
                        act.wait_ge(s["att_t"], a0 + a - 2)
                    src = m["masked"][a % 3] if sinks else score_bank(a)[:, :]
                    e = act.activation(m["prob"][a % 3], src, ACT.Exp, bias=m["nmax"][:, a:a + 1],
                                       scale=scale, accum_out=m["total"][:, a:a + 1])
                    if sinks:
                        e = act.activation(m["esink"][:, a:a + 1], S("sink")[:, a // 2:a // 2 + 1],
                                           ACT.Exp, bias=m["nmax"][:, a:a + 1])
                    e.then_inc(s["att_e"], 1)

                def keep(a):
                    h, t = divmod(a, 2)
                    act.wait_ge(s["att_t"], a0 + a + 1)
                    if h >= 2:
                        act.wait_ge(s["att_o"], a0 // 2 + h - 1)
                    act.activation(m["turned"][h % 2][:, :, t * P:(t + 1) * P],
                                   bank[2 + a % 2][:, :].rearrange("p (k q) -> p k q", k=TT),
                                   ACT.Copy).then_inc(s["att_pt"], 1)

                exps(0)
                exps(1)
                for a in range(2 * heads):
                    keep(a)
                    if a + 2 < 2 * heads:
                        exps(a + 2)

            def out_and_squares(name, t0, t1):
                f = ph[name]

                def job(u, j, r):
                    act.wait_ge(s["taken"], f.first_taken + u + 1)
                    square(u, t0, t1)
                phase(name, job)

            def down_and_squares(name, t0, t1, more):
                f = ph[name]

                def job(u, j, r):
                    if u % 3 == 2:
                        act.wait_ge(s["taken"], f.first_taken + u // 3 + 1)
                        square(u // 3, t0, t1)
                phase(name, job, more)

            def silu_gates(n, t0, t1):
                f = ph[f"up{n}"]

                def job(u, j, r):
                    if j % 2 == 0:
                        act.wait_ge(s["steps"], r * ROUND + (f.first_step + j + 1))
                        act.wait_ge(s["hid_done"], r * (ROUND // 2) + (KF * n + j // 2 + 1))
                        act.activation(work[:, (j // 2) % 3, t0:t1], bank_of(f.first_taken + j)[:, 0:t1 - t0],
                                       ACT.Silu).then_inc(s["up_act"], 1)
                phase(f"up{n}", job)

            def silu_cond(n):
                act.wait_ge(s["cond_in"], 16 * (n + 1))
                act.activation(cond[:, :, :], cond[:, :, :], ACT.Silu).then_inc(s["cond_ready"], 1)

            silu_cond(0)
            act.wait_ge(s["small_in"], 16)
            act.wait_ge(s["x_in"], 32)
            squares(0, TOK)
            rms_std(0, TOK)
            round_next()
            round_next()
            round_h(work_tile, 0, TOK)
            phase("va_gates")
            softplus_part(1, gtmp)
            phase("vm")

            def conv_silu(name, dst, first, n):
                f = ph[name]

                def job(u, j, r):
                    act.wait_ge(s["taken"], f.first_taken + u + 1)
                    act.activation(dst[:, u, :], conv[:, (first + u) % 2, 0:n], ACT.Silu)\
                       .then_inc(s["conv_act"], 1)
                phase(name, job)

            conv_silu("km", km, 0, TOK)
            conv_silu("qm", qm, 4, LAT)
            phase("ka")
            phase("qa")
            phase("om")
            for h in range(MH):
                act.wait_ge(s["ml_arg"], h + 1)
                if h:
                    act.wait_ge(s["ml_p"], h)
                for d in range(2):
                    for i in range(TT):
                        src = narg[:, d, 0, :] if i < 2 else narg[:, d, i - 1, :]
                        last = act.activation(ex[:, d, i, :], src, ACT.Exp, bias=g_bias[:, d, i, h:h + 1])
                last.then_inc(s["ml_e"], 1)
                if h >= 2:
                    act.wait_ge(s["ml_h"], h - 1)
                act.activation(den_e[h % 2], bank[1][:, :], ACT.Exp, scale=-1.0).then_inc(s["ml_e"], 1)
            act.wait_ge(s["ml_sum"], 1)
            act.activation(token_m[:, 0, :], bank[6][:, 0:2 * MH], ACT.Sqrt, scale=1.0 / MD, bias=EPS)\
               .then_inc(s["ml_std"], 1)
            act.activation(sig, om, ACT.Sigmoid).then_inc(s["ml_std"], 1)
            act.wait_ge(s["ml_y"], 1)
            attention(att0, 0, AH, AD ** -0.5, True)
            out_and_squares("out0", L0, L1)
            rms_std(L0, L1)
            round_h(work_tile, L0, L1)

            def gelu(u, j, r):
                if j % 2 == 0:
                    act.wait_ge(s["up_conv"], r * (ROUND // 2) + (j // 2 + 1))
                    x = work[:, (j // 2) % 3, L0:L1]
                    act.activation(x, x, ACT.Gelu_apprx_tanh).then_inc(s["up_act"], 1)

            silu_cond(1)
            phase("up0", gelu)
            down_and_squares("down0", L0, L1, False)
            rms_std(L0, L1)
            if layers == 1:
                return

            act.wait_ge(s["x_ready"], 1)
            act.dma_start(room1, dram["table1"]).then_inc(s["tables_in"], 16)
            act.wait_ge(s["ctx2_in"], 16)
            squares(0, TOK)
            rms_std(0, TOK)
            round_next()
            round_next()
            round_h(work_tile, 0, TOK)

            def silu_xbc(u, j, r):
                if u == 13:
                    act.wait_ge(s["taken"], ph["in1"].first_taken + 8)
                    act.wait_ge(s["steps"], ph["in1"].first_step + 12)
                    for q in range(4):
                        act.dma_start(swap_r[32 * q:32 * q + 32, :, :],
                                      t1[32 * (q ^ 1):32 * (q ^ 1) + 32, 0:8, L0:L1]).then_inc(s["swap_done"], 16)
                if 14 <= u < 22:
                    act.wait_ge(s["taken"], ph["in1"].first_taken + u - 5)
                    act.activation(t1[:, u - 6, :], t1[:, u - 6, :], ACT.Silu).then_inc(s["gn_act"], 1)
                if u >= 16:
                    act.wait_ge(s["taken"], ph["in1"].first_taken + u + 1)
                    act.activation(t1[:, u, :], conv1[:, u % 2, :], ACT.Silu).then_inc(s["conv_act"], 1)

            softplus_part(2, decay_tmp)
            act.activation(nega, S("a_log"), ACT.Exp).then_inc(s["lf_exp"], 1)
            phase("in1", lambda u, j, r: silu_xbc(u, j, r) if j > 12 else None, looped=13)
            phase("vr")
            phase("dt")
            for h in range(RH):
                act.wait_ge(s["rt_arg"], h + 1)
                a, b = ra[h % 2], rb[h % 2]
                act.activation(a[:, 0:2, 0:LAT], a[:, 2, :].rearrange("p (a b) -> p a b", a=2), ACT.Exp)
                for d, dst in ((0, a[:, 0:2, L0:L1]), (1, b)):
                    last = act.activation(dst, C1("far_f" if d == 0 else "far_b", 2), ACT.Exp,
                                          scale=log_r[:, d * RH + h:d * RH + h + 1])
                last.then_inc(s["rt_e"], 1)
            softplus_part(3, dtmp)
            for i in range(4):
                act.wait_ge(s["gn_mid"], i + 1)
                act.activation(y_sq[:, i, :], y1[:, i, :], ACT.Square).then_inc(s["gn_in"], 1)

            def keep_xs(i):
                act.wait_ge(s["sd_t"], i + 1)
                act.activation(xt[:, i, :], bank[5 + i % 2][:, :], ACT.Copy).then_inc(s["sd_tt"], 1)

            keep_xs(0)
            keep_xs(1)
            act.wait_ge(s["gn_sum"], 5)
            act.activation(std[:, :], bank[4][:, :], ACT.Sqrt, bias=EPS).then_inc(s["gn_std"], 1)
            for i in range(2, TT):
                keep_xs(i)
            for h in range(RH):
                for d, e in ((0, ea[h % 2]), (1, eb[h % 2])):
                    act.wait_ge(s["sd_arg"], 2 * h + d + 1)
                    far = decay_bank(2 * h + d)[:, L0:L1]
                    for i in range(2):
                        act.activation(e[:, i, 0:L0], e[:, i, 0:L0], ACT.Exp, bias=ngs[:, d, i, h:h + 1])
                        act.activation(e[:, i, L0:L1], far, ACT.Exp, bias=ngs[:, d, i, h:h + 1])
                    for i in range(2, TT):
                        part = e[:, 2, (i - 2) * LAT:(i - 1) * LAT]
                        last = act.activation(part, part, ACT.Exp, bias=ngs[:, d, i, h:h + 1])
                    last.then_inc(s["sd_e"], 1)
            act.wait_ge(s["sn_sum"], 1)
            act.activation(std[:, :], bank[7][:, :], ACT.Sqrt, scale=1.0 / 512, bias=EPS).then_inc(s["sn_std"], 1)
            round_h(lambda k: y1[:, k, :], 0, TOK)
            out_and_squares("out1", 0, TOK)
            rms_std(0, TOK)
            round_h(work_tile, 0, TOK)
            silu_gates(1, 0, TOK)
            down_and_squares("down1", 0, TOK, False)
            if layers == 2:
                return

            act.dma_start(room2, dram["table2"]).then_inc(s["tables_in"], 16)
            rms_std(0, TOK)
            round_next()
            round_next()
            round_h(work_tile, 0, TOK)
            phase("cq")
            phase("ckv")
            phase("kpe")
            act.wait_ge(s["lq_sum"], 1)
            act.activation(std[:, L0:L1], bank[6][:, 0:LAT], ACT.Sqrt, scale=1.0 / 768, bias=EPS)\
               .then_inc(s["lq_std"], 1)
            act.wait_ge(s["lq_sum"], 2)
            act.wait_ge(s["lq_done"], 1)
            act.activation(std[:, :], bank[7][:, :], ACT.Sqrt, scale=1.0 / 256, bias=EPS)\
               .then_inc(s["lq_std"], 1)
            act.wait_ge(s["kpe_in"], 1)
            act.activation(kh[LN:LQ, :, :], kpe[LN:LQ, :].unsqueeze(1).to_broadcast([LR, LH, TOK]),
                           ACT.Copy).then_inc(s["kpe_done"], 1)
            phase("uq")
            phase("uk")
            phase("uv")
            attention(att2, 2 * AH, LH, LQ ** -0.5, False)
            out_and_squares("out2", L0, L1)
            rms_std(L0, L1)
            round_h(work_tile, L0, L1)
            silu_gates(2, L0, L1)
            down_and_squares("down2", L0, L1, False)
            rms_std(L0, L1)

        @block.gpsimd
        def _(pool):
            done = [0]
            h_count = [0]

            def low_next():
                q = done[0]
                done[0] += 1
                f, u = all_units[q]
                pool.wait_ge(s["rounded"], q + 1)
                pool.tensor_tensor(part_slot(w_lo, f, u), raw_slot(f, u), part_slot(w_hi, f, u).bitcast(F32),
                                   ALU.subtract).then_inc(s["split"], 1)

            def lows(*names):
                for name in names:
                    f = ph[name]
                    start = AHEAD if name == names[0] else 0
                    if f.units - start >= 2 * f.round:
                        def body(u, j, r, f=f):
                            pool.wait_ge(s["rounded"], r * f.round + (f.first_unit + j + 1))
                            pool.tensor_tensor(part_slot(w_lo, f, j), raw_slot(f, j),
                                               part_slot(w_hi, f, j).bitcast(F32),
                                               ALU.subtract).then_inc(s["split"], 1)
                        unit_rounds(pool, start, f.units, body, size=f.round)
                        done[0] += f.units - start
                    else:
                        while done[0] < f.first_unit + f.units:
                            low_next()

            def low_h(src, t0, t1):
                for k in range(KD):
                    pool.wait_ge(s["h_round"], h_count[0] + k + 1)
                    pool.tensor_tensor(h_lo[:, k, t0:t1], src(k)[:, t0:t1], h_hi[:, k, t0:t1].bitcast(F32),
                                       ALU.subtract).then_inc(s["h_split"], 1)
                h_count[0] += KD

            def work_tile(k):
                return work[:, k % 3, :]

            def two():
                low_next()
                low_next()

            two()
            low_h(work_tile, 0, TOK)
            if layers > 1:
                pool.dma_start(X[:, :, 0:L0], dram["ctx_2"]).then_inc(s["ctx2_in"], 16)
            lows("va_gates", "vm", "km", "qm", "ka", "qa", "om", "out0")
            two()
            low_h(work_tile, L0, L1)
            lows("up0", "down0")
            if layers == 1:
                return
            two()
            low_h(work_tile, 0, TOK)
            lows("in1", "vr", "dt")
            two()
            for h in range(RH):
                pool.wait_ge(s["rt_e"], h + 1)
                far = ra[h % 2][:, 0:2, L0:L1]
                pool.tensor_tensor(far, far, rb[h % 2], ALU.add).then_inc(s["rt_sum"], 1)
            for h in range(RH):
                pool.wait_ge(s["sd_e"], 2 * h + 1)
                for i in range(TT):
                    part = parts(ea[h % 2], i)
                    weight = dt[:, i, h:h + 1].to_broadcast(list(part.shape))
                    last = pool.tensor_tensor(part, part, weight, ALU.mult)
                last.then_inc(s["sd_dt"], 1)
            low_h(lambda k: y1[:, k, :], 0, TOK)
            lows("out1")
            two()
            low_h(work_tile, 0, TOK)
            lows("up1", "down1")
            if layers == 2:
                return
            two()
            low_h(work_tile, 0, TOK)
            lows("cq", "ckv", "kpe", "uq", "uk", "uv", "out2")
            two()
            low_h(work_tile, L0, L1)
            lows("up2", "down2")

        @block.vector
        def _(dve):
            chain = Chain(dve, s["vector_order"])
            then = chain.then
            norms = [0]
            h_count = [0]

            def copy(out, in_):
                return dve.tensor_scalar(out, in_, 1.0, None, ALU.mult)

            def low(out, x, hi):
                return dve.tensor_tensor(out, x, hi.bitcast(F32), ALU.subtract)

            def product_in(f, j, r=0):
                dve.wait_ge(s["steps"], r * (ROUND * f.steps) + (f.first_step + j + 1))

            layer = [0]

            def ada_unit(k, r=0, each=0):
                dve.wait_ge(ada_full[k % SLOTS], r * (16 * each // SLOTS) + 16 * (k // SLOTS + 1))
                for m in range(2):
                    if k or m:
                        dve.wait_ge(s["ada_sum"], r * (2 * each) + (2 * k + m))
                    dve.tensor_tensor_reduce(products[:, :], ada_w[:, k % SLOTS, :], cond[:, m, :], 1.0, 0.0,
                                             ALU.mult, ALU.add, ada_sums[:, k % SLOTS, m:m + 1]).then_inc(s["ada_sum"], 1)
                dve.wait_ge(s["ada_sum"], r * (2 * each) + (2 * k + 2))
                copy(mod[:, k // 48 % 2, bass.ds(r * each + k % 48, 1), :].rearrange("p a b -> p (a b)"), ada_sums[:, k % SLOTS, :])\
                    .then_inc(s["ada_used"], 1)

            def carried(f, j, r=0):
                if f.name == "up0" and j == 0:
                    dve.wait_ge(s["cond_ready"], 2)
                if j % f.every == 0 and j < f.carry:
                    for q in range(f.number):
                        ada_unit(f.first_ada + j // f.every * f.number + q, r, ROUND // f.every * f.number)

            def add_bias(a, b):
                n = layer[0]
                dve.wait_ge(s["ada_used"], 48 * n + b)
                m = mod[:, n % 2, a:b, :]
                then(dve.tensor_tensor(m, m, S(f"b_ada{n}")[:, a:b].unsqueeze(2).to_broadcast([P, b - a, 2]),
                                       ALU.add))

            def norm_gain(which):
                n = layer[0]
                sc = mod[:, n % 2, 24 * which + 8:24 * which + 16, :]
                if n == 0:
                    g = S("norm_mix" if which == 0 else "norm_ffn").unsqueeze(2).to_broadcast([P, KD, 2])
                    then(dve.scalar_tensor_tensor(out=gain[:, which, :, :], in0=sc, scalar=1.0, in1=g,
                                                  op0=ALU.add, op1=ALU.mult))
                else:
                    then(dve.tensor_scalar(gain[:, which, :, :], sc, 1.0, None, ALU.add))

            def add_square(k, t0, t1):
                n = norms[0] * (KD - 1) + k
                dve.wait_ge(s["squared"], norms[0] * KD + k + 1)
                if k > 1:
                    dve.wait_ge(s["added"], n - 1)
                dve.tensor_tensor(sq_sum[:, t0:t1], sq_sum[:, t0:t1], work[:, k % 3, t0:t1], ALU.add)\
                   .then_inc(s["added"], 1)
                if k == KD - 1:
                    dve.wait_ge(s["added"], n)
                    norms[0] += 1
                    dve.nop().then_inc(s["sums_in"], 1)

            def add_squares(t0, t1):
                for k in range(1, KD):
                    add_square(k, t0, t1)

            def inverse_rms(t0, t1):
                dve.wait_ge(s["std_ready"], norms[0])
                a, b = t0 // P, t1 // P
                dve.reciprocal(token_inv[:, a:b], token_std[:, a:b]).then_inc(s["inverse_ready"], 1)
                dve.wait_ge(s["inverse_spread"], norms[0])

            def norm(which, both):
                t0 = 0 if both else L0
                norm_gain(which)
                inverse_rms(t0, L1)
                for k in range(KD):
                    if k >= 3:
                        dve.wait_ge(s["h_split"], h_count[0] + k - 2)
                    w = work[:, k % 3, :]
                    then(dve.tensor_tensor(w[:, t0:L1], X[:, k, t0:L1], bank[5][:, t0:L1], ALU.mult))
                    for a, b, m in ([(0, L0, 1)] if both else []) + [(L0, L1, 0)]:
                        last = dve.tensor_scalar(w[:, a:b], w[:, a:b], gain[:, which, k, m:m + 1],
                                                 mod[:, layer[0] % 2, 24 * which + k, m:m + 1], ALU.mult, ALU.add)
                    last.then_inc(s["h_work"], 1)
                h_count[0] += KD

            def final_norm(name):
                inverse_rms(L0, L1)
                for k in range(KD):
                    x = X[:, k, L0:L1]
                    last = dve.scalar_tensor_tensor(out=x, in0=x, scalar=S(name)[:, k:k + 1],
                                                    in1=bank[5][:, L0:L1], op0=ALU.mult, op1=ALU.mult)
                last.then_inc(s["x_ready"], 1)

            def each_product(name, body, start=0, stop=None):
                f = ph[name]
                takes = int(f.takes)

                def unit(u, j, r):
                    for i in range(takes):
                        dve.wait_ge(s["steps"], r * (ROUND * f.steps) + (f.first_step + j * takes + i + 1))
                        body(u * takes + i, bank_of(f.first_taken + j * takes + i)).then_inc(s["taken"], 1)
                    carried(f, j, r)

                unit_rounds(dve, start, stop or f.units, unit)

            def taken(name):
                dve.wait_ge(s["taken"], ph[name].first_taken)

            def conv_taps(dst, src, taps, bias, segs):
                half = len(taps) // 2
                d, x = (v.rearrange("p (a b) -> p a b", a=segs) for v in (dst, src))
                w = d.shape[2]
                then(dve.tensor_scalar(dst, src, taps[half], bias, ALU.mult, ALU.add))
                last = None
                for n, tap in enumerate(taps):
                    o = n - half
                    if o == 0:
                        continue
                    if last is not None:
                        then(last)
                    lo, hi = max(0, -o), w - max(0, o)
                    last = dve.scalar_tensor_tensor(out=d[:, :, lo:hi], in0=x[:, :, lo + o:hi + o],
                                                    scalar=tap, in1=d[:, :, lo:hi], op0=ALU.mult, op1=ALU.add)
                return last

            def minus_abs(dst, x):
                dve.scalar_tensor_tensor(out=dst, in0=x, scalar=-1.0, in1=x, op0=ALU.mult, op1=ALU.min)\
                   .then_inc(s["lf_in"], 1)

            def log_gates():
                dve.wait_ge(s["lf_exp"], 1)
                dve.scalar_tensor_tensor(out=lf, in0=gates, scalar=0.0, in1=gtmp, op0=ALU.min,
                                         op1=ALU.subtract).then_inc(s["lf_ready"], 1)

            def gate_columns():
                dve.wait_ge(s["cum_ready"], 1)
                then(copy(g_cum, bank[4][:, 0:2 * TT * MH].rearrange("p (d i h) -> p d i h", d=2, i=TT)))
                for d in range(2):
                    last = dve.tensor_tensor(g_bias[:, d, :, :], gates[:, :, 8 * d:8 * d + 4], g_cum[:, d, :, :],
                                             ALU.subtract)
                last.then_inc(s["cum_taken"], 1)

            def running_maxima():
                dve.wait_ge(s["rows_ready"], 1)
                then(copy(run_max[0:MH, 0:512], bank[3][0:MH, :]))
                then(copy(run_max[0:MH, 512:1024], bank[4][0:MH, :]))
                for d in range(2):
                    then(dve.reduce_max(top[0:MH, d:d + 1], run_max[0:MH, d * 512:d * 512 + L0], AX_X))
                then(dve.tensor_scalar(top[0:MH, :], top[0:MH, :], 0.0, None, ALU.max))
                b = run_max[0:MH, L0:L1]
                dve.tensor_tensor_scan(rows[0:MH, 0, :], b, b, top[0:MH, 0:1], ALU.max, ALU.max)
                b = run_max[0:MH, 1023:767:-1]
                then(dve.tensor_tensor_scan(rows[0:MH, 1, ::-1], b, b, top[0:MH, 1:2], ALU.max, ALU.max))
                dve.tensor_tensor(rows[0:MH, 2:4, :], rows[0:MH, 0:2, :],
                                  bank[5][0:MH, :].rearrange("p (a b) -> p a b", a=2), ALU.add)\
                   .then_inc(s["rows_taken"], 1)

            def mlstm():
                def arguments(h):
                    dve.wait_ge(s["ml_bcast"], h + 1)
                    if h:
                        dve.wait_ge(s["ml_e"], 2 * h - 1)
                    for d in range(2):
                        m = bank[0][:, d * LAT:(d + 1) * LAT]
                        dve.tensor_scalar(narg[:, d, 0, :], m, -1.0, None, ALU.mult)
                        last = dve.scalar_tensor_tensor(
                            out=narg[:, d, 1:3, :], in0=m.unsqueeze(1).to_broadcast([P, 2, LAT]), scalar=-1.0,
                            in1=C0("after" if d == 0 else "before", 2), op0=ALU.mult, op1=ALU.add)
                    last.then_inc(s["ml_arg"], 1)

                def weigh(h):
                    dve.wait_ge(s["ml_s"], h + 1)
                    dve.wait_ge(s["ml_e"], 2 * h + 1)
                    if h > 1:
                        dve.wait_ge(s["ml_num"], h - 1)
                    for d in range(2):
                        for i in range(2):
                            last = dve.scalar_tensor_tensor(
                                out=prob_m[h % 2][:, d * TT + 2 * i:d * TT + 2 * i + 2, :],
                                in0=bank[2 + i][:, :].rearrange("p (a b) -> p a b", a=2), scalar=MD ** -0.5,
                                in1=ex[:, d, 2 * i:2 * i + 2, :], op0=ALU.mult, op1=ALU.mult)
                    last.then_inc(s["ml_p"], 1)

                def ratio(h):
                    dve.wait_ge(s["ml_num"], h + 1)
                    then(dve.tensor_scalar(den_a, bank[5][:, :], -1.0, None, ALU.mult))
                    then(dve.tensor_tensor(den_a, den_a, bank[5][:, :], ALU.max))
                    dve.wait_ge(s["ml_e"], 2 * h + 2)
                    then(dve.tensor_tensor(den_a, den_a, den_e[h % 2], ALU.max))
                    then(dve.reciprocal(den_a, den_a))
                    then(dve.tensor_tensor(hid, den_a, bank[4][:, :], ALU.mult))
                    dve.tensor_tensor(hm[:, h, :], hid[:, 0:LAT], hid[:, LAT:2 * LAT], ALU.add)\
                       .then_inc(s["ml_h"], 1)

                arguments(0)
                weigh(0)
                for h in range(MH):
                    if h + 1 < MH:
                        arguments(h + 1)
                        weigh(h + 1)
                    ratio(h)
                dve.wait_ge(s["ml_h"], MH)
                dve.tensor_tensor(sq_m, hm, hm, ALU.mult).then_inc(s["ml_sq"], 1)
                dve.wait_ge(s["ml_std"], 1)
                dve.reciprocal(token_m[:, 1, :], token_m[:, 0, :]).then_inc(s["ml_inv"], 1)
                dve.wait_ge(s["ml_std"], 2)
                dve.wait_ge(s["ml_spread"], 1)
                for i in range(2):
                    g = sig[:, 2 * i:2 * i + 2, :]
                    last = dve.tensor_tensor(g, g, bank[i][:, :].rearrange("p (a b) -> p a b", a=2), ALU.mult)
                last.then_inc(s["ml_gate"], 1)
                dve.wait_ge(s["ml_gate"], 1)
                for h in range(MH):
                    last = dve.scalar_tensor_tensor(out=hm[:, h, :], in0=hm[:, h, :],
                                                    scalar=S("mlstm_norm")[:, h:h + 1], in1=sig[:, h, :],
                                                    op0=ALU.mult, op1=ALU.mult)
                then(last)
                then(copy(h_hi[:, 0:MH, L0:L1], hm))
                low(h_lo[:, 0:MH, L0:L1], hm, h_hi[:, 0:MH, L0:L1]).then_inc(s["ml_y"], 1)
                dve.wait_ge(s["ml_y"], 1)

            swap16 = list(range(16, 32)) + list(range(16))

            def attention(m, a0, heads, scale, sinks, tile0):
                if sinks:
                    then(dve.tensor_scalar(m["nsink"], S("sink"), -1.0, None, ALU.mult))

                def peaks(a):
                    h, t = divmod(a, 2)
                    dve.wait_ge(s["att_s"], a0 + a + 1)
                    if sinks:
                        if a >= 3:
                            dve.wait_ge(s["att_e"], a0 + a - 2)
                        then(dve.tensor_tensor_reduce(m["masked"][a % 3], score_bank(a)[:, :],
                                                      C0("window", 2)[:, t, :], 1.0, -3e38, ALU.add, ALU.max,
                                                      m["peak"][:, a:a + 1]))
                        dve.tensor_scalar(m["nmax"][:, a:a + 1], m["peak"][:, a:a + 1], -scale,
                                          m["nsink"][:, h:h + 1], ALU.mult, ALU.min).then_inc(s["att_m"], 1)
                    else:
                        then(dve.reduce_max(m["peak"][:, a:a + 1], score_bank(a)[:, :], AX_X))
                        dve.tensor_scalar(m["nmax"][:, a:a + 1], m["peak"][:, a:a + 1], -scale, None,
                                          ALU.mult).then_inc(s["att_m"], 1)

                def divide(a):
                    dve.wait_ge(s["att_e"], a0 + a + 1)
                    one = m["total"][:, a:a + 1]
                    if sinks:
                        then(dve.tensor_tensor(one, one, m["esink"][:, a:a + 1], ALU.add))
                    then(dve.reciprocal(one, one))
                    dve.tensor_scalar(m["prob"][a % 3], m["prob"][a % 3], one, None, ALU.mult)\
                       .then_inc(s["att_p"], 1)

                def outputs(t):
                    dve.wait_ge(s["att_o"], a0 // 2 + 2 * t + 2)
                    y = bank[4 + t % 2][:, 0:LAT]
                    hi = h_hi[:, tile0 + t, L0:L1]
                    then(copy(hi, y))
                    low(h_lo[:, tile0 + t, L0:L1], y, hi).then_inc(s["att_y"], 1)

                peaks(0)
                peaks(1)
                for a in range(2 * heads):
                    divide(a)
                    if a + 2 < 2 * heads:
                        peaks(a + 2)
                    if a >= 7 and (a - 7) % 4 == 0:
                        outputs((a - 7) // 4)
                outputs(heads // 2 - 1)
                dve.wait_ge(s["att_y"], a0 // 4 + heads // 2)

            def residual(name, chunk, both):
                f = ph[name]
                units = f.parts
                t0 = 0 if both else L0
                for k in range(KD):
                    product_in(f, units * (k + 1) - 1)
                    b = bank_of(f.first_taken + k)
                    for a, e, m in ([(0, L0, 1)] if both else []) + [(L0, L1, 0)]:
                        last = dve.scalar_tensor_tensor(out=X[:, k, a:e], in0=b[:, a - t0:e - t0],
                                                        scalar=mod[:, layer[0] % 2, 8 * chunk + k, m:m + 1],
                                                        in1=X[:, k, a:e], op0=ALU.mult, op1=ALU.add)
                    last.then_inc(s["taken"], 1)
                    carried(f, units * k)
                    if k > 1:
                        add_square(k - 1, t0, L1)
                add_square(KD - 1, t0, L1)

            def hidden(i, w, t0, t1):
                hi, lo = (x[:, bass.ds(i, 1), t0:t1].rearrange("p a b -> p (a b)") for x in (hidden_hi, hidden_lo))
                then(copy(hi, w))
                low(lo, w, hi).then_inc(s["hid_done"], 1)

            def gated(f, j, r, t0, t1):
                i = r * (ROUND // 2) + j // 2
                product_in(f, j, r)
                w = work[:, (j // 2) % 3, t0:t1]
                dve.tensor_tensor(w, w, bank_of(f.first_taken + j)[:, 0:t1 - t0], ALU.mult).then_inc(s["taken"], 2)
                dve.wait_ge(s["taken"], r * ROUND + (f.first_taken + j + 1))
                hidden(i, w, t0, t1)

            def ffn0():
                norm(1, False)
                dve.nop().then_inc(s["hid_done"], 3)
                w, b = S("ffn_conv_w", 3), S("ffn_conv_b")
                f = ph["up0"]

                def unit(u, j, r):
                    i = r * (ROUND // 2) + j // 2
                    if j % 2 == 0:
                        product_in(f, j, r)
                        dve.wait_ge(s["hid_done"], r * (ROUND // 2) + (j // 2 + 1))
                        conv_taps(work[:, (j // 2) % 3, L0:L1], bank_of(f.first_taken + j)[:, 0:LAT],
                                  [w[:, q, bass.ds(i, 1)] for q in range(3)], b[:, bass.ds(i, 1)], 1)\
                            .then_inc(s["up_conv"], 1)
                    else:
                        dve.wait_ge(s["up_act"], r * (ROUND // 2) + (j // 2 + 1))
                        gated(f, j, r, L0, L1)
                    carried(f, j, r)

                unit_rounds(dve, 0, f.units, unit, chain, 9)
                residual("down0", 5, False)

            def swiglu(n, both):
                t0 = 0 if both else L0
                norm(1, both)
                f = ph[f"up{n}"]

                def unit(u, j, r):
                    if j % 2:
                        dve.wait_ge(s["up_act"], r * (ROUND // 2) + (KF * n + j // 2 + 1))
                        gated(f, j, r, t0, L1)
                    carried(f, j, r)

                unit_rounds(dve, 0, f.units, unit, chain, 3)
                residual(f"down{n}", 5, both)

            def mixer1():
                def keep(p, b):
                    return copy(t1[:, bass.ds(p, 1), :].rearrange("p a b -> p (a b)"), b[:, :])
                w, cb = S("ssd_conv_w", 5), S("ssd_conv_b")

                def convolve(p, b):
                    i = p - 16
                    if i >= 2:
                        dve.wait_ge(s["conv_act"], 8 + i - 1)
                    return conv_taps(conv1[:, i % 2, :], b[:, :], [w[:, q, i:i + 1] for q in range(5)],
                                     cb[:, i:i + 1], 2)
                lg = S("decay_logit")
                minus_abs(decay_tmp, lg)
                each_product("in1", keep, 0, 12)
                dve.wait_ge(s["lf_exp"], 2)
                then(dve.scalar_tensor_tensor(out=log_r, in0=lg, scalar=0.0, in1=decay_tmp, op0=ALU.min,
                                              op1=ALU.subtract))
                each_product("in1", keep, 12, 16)
                each_product("in1", convolve, 16)
                dve.wait_ge(s["swap_done"], 64)
                dve.wait_ge(s["tables_in"], 32)
                lat = t1[:, 0:8, L0:L1]
                cs, sn = (C1(x).unsqueeze(1).to_broadcast([P, KD, LAT]) for x in ("cos", "sin"))
                dve.tensor_tensor(swap_r, swap_r, sn, ALU.mult)
                then(dve.tensor_tensor(lat, lat, cs, ALU.mult))
                dve.tensor_tensor(lat, lat, swap_r, ALU.add).then_inc(s["rope_ready"], 1)
                each_product("vr", lambda p, b: copy(vr[:, p % TT, p // TT * 256:(p // TT + 1) * 256], b[:, 0:256]))
                each_product("dt", lambda p, b: dve.tensor_tensor(dt[:, p, :], b[:, 0:16], S("dt_bias"), ALU.add))
                taken("out1")
                minus_abs(dtmp, dt)
                dve.wait_ge(s["rope_ready"], 2)
                def ret_arguments(h):
                    if h >= 2:
                        dve.wait_ge(s["rt_p"], h - 1)
                    arg = ra[h % 2][:, 2, :]
                    then(dve.tensor_scalar(arg, C1("dist_b"), log_r[:, RH + h:RH + h + 1], None, ALU.mult))
                    dve.scalar_tensor_tensor(out=arg, in0=C1("dist_f"), scalar=log_r[:, h:h + 1], in1=arg,
                                             op0=ALU.mult, op1=ALU.add).then_inc(s["rt_arg"], 1)

                ret_arguments(0)
                for h in range(RH):
                    if h + 1 < RH:
                        ret_arguments(h + 1)
                    a, q = ra[h % 2], rp[h % 2]
                    dve.wait_ge(s["rt_sum"], h + 1)
                    dve.wait_ge(s["rt_s"], h + 1)
                    if h >= 2:
                        dve.wait_ge(s["rt_o"], h - 1)
                    sb0 = 3 * (h % 2)
                    for i in range(2):
                        dve.scalar_tensor_tensor(out=q[:, i, :], in0=bank[sb0 + i][:, :], scalar=0.125,
                                                 in1=a[:, i, :], op0=ALU.mult, op1=ALU.mult)
                    dve.scalar_tensor_tensor(
                        out=q[:, 2, :].rearrange("p (a b) -> p a b", a=2),
                        in0=bank[sb0 + 2][:, :].rearrange("p (a b) -> p a b", a=2), scalar=0.125,
                        in1=a[:, 0:2, 0:LAT], op0=ALU.mult, op1=ALU.mult).then_inc(s["rt_p"], 1)
                    if h % 2 and h > 1:
                        dve.wait_ge(s["rt_o"], h - 1)
                        copy(y1[:, h // 2 - 1, :], bank[6 + (h // 2 - 1) % 2][:, :]).then_inc(s["rt_y"], 1)
                dve.wait_ge(s["rt_o"], RH)
                copy(y1[:, 3, :], bank[7][:, :]).then_inc(s["rt_y"], 1)
                dve.wait_ge(s["rt_y"], 4)
                dve.wait_ge(s["lf_exp"], 4)
                then(dve.scalar_tensor_tensor(out=dt, in0=dt, scalar=0.0, in1=dtmp, op0=ALU.max, op1=ALU.add))
                dve.scalar_tensor_tensor(out=la, in0=dt, scalar=-1.0,
                                         in1=nega.unsqueeze(1).to_broadcast([P, TT, 16]),
                                         op0=ALU.mult, op1=ALU.mult).then_inc(s["lf_ready"], 1)
                for i in range(4):
                    dve.wait_ge(s["gn_sum"], i + 1)
                    dve.tensor_tensor(y1[:, i, :], y1[:, i, :], bank[i][:, :], ALU.subtract)\
                       .then_inc(s["gn_mid"], 1)
                dve.wait_ge(s["cum_ready"], 2)
                cum = bank[7][:, 0:2 * TT * RH].rearrange("p (d i h) -> p d i h", d=2, i=TT)
                dve.tensor_scalar(ngs, cum, -1.0, None, ALU.mult)
                copy(gs, cum).then_inc(s["cum_taken"], 1)
                dve.wait_ge(s["gn_std"], 1)
                dve.reciprocal(std[:, :], std[:, :]).then_inc(s["gn_inv"], 1)
                for i in range(4):
                    dve.wait_ge(s["gn_sum"], 6 + i)
                    last = dve.scalar_tensor_tensor(out=y_sq[:, i, :], in0=bank[i][:, :],
                                                    scalar=S("gn_w")[:, i:i + 1], in1=y1[:, i, :],
                                                    op0=ALU.mult, op1=ALU.mult)
                then(last)
                dve.wait_ge(s["gn_act"], 8)
                dve.tensor_tensor(y1[:, 0:4, :], y_sq, t1[:, 8:12, :], ALU.mult).then_inc(s["gn_done"], 1)
                dve.wait_ge(s["gn_done"], 1)
                dve.wait_ge(s["rows_ready"], 2)
                copy(grow[0:RH, 0, :], bank[5][0:RH, :])
                copy(grow[0:RH, 1, :], bank[6][0:RH, :]).then_inc(s["rows_taken"], 1)

                def decay_arguments(h):
                    if h >= 2:
                        dve.wait_ge(s["sd_p"], h - 1)
                    for d, e in ((0, ea[h % 2]), (1, eb[h % 2])):
                        dve.wait_ge(s["sd_b"], 2 * h + d + 1)
                        g = decay_bank(2 * h + d)
                        mask = C1("after" if d == 0 else "before", 2)
                        gl = g[:, L0:L1].unsqueeze(1).to_broadcast([P, 2, LAT])
                        gc = g[:, 0:L0].unsqueeze(1).to_broadcast([P, 2, LAT])
                        dve.tensor_tensor(e[:, 0:2, 0:L0], gc, mask, ALU.add)
                        dve.tensor_tensor(e[:, 2, :].rearrange("p (a b) -> p a b", a=2), gl, mask, ALU.add)\
                           .then_inc(s["sd_arg"], 1)

                decay_arguments(0)
                for h in range(RH):
                    if h + 1 < RH:
                        decay_arguments(h + 1)
                    fwd, bwd, q = ea[h % 2], eb[h % 2], pr[h % 2]
                    dve.wait_ge(s["sd_dt"], h + 1)
                    dve.wait_ge(s["sd_e"], 2 * h + 2)
                    for i in range(TT):
                        last = dve.scalar_tensor_tensor(out=parts(bwd, i), in0=parts(bwd, i),
                                                        scalar=dt[:, i, RH + h:RH + h + 1], in1=parts(fwd, i),
                                                        op0=ALU.mult, op1=ALU.add)
                    then(last)
                    dve.wait_ge(s["sd_s"], h // 4 + 1)
                    if h >= 2:
                        dve.wait_ge(s["sd_o"], h - 1)
                    for i in range(3):
                        last = dve.tensor_tensor(q[:, i, :], bwd[:, i, :], bank[i][:, :], ALU.mult)
                    last.then_inc(s["sd_p"], 1)
                    if h % 2 and h > 1:
                        dve.wait_ge(s["sd_o"], h - 1)
                        copy(y1[:, 4 + h // 2 - 1, :], bank[5 + (h // 2 - 1) % 2][:, :]).then_inc(s["sd_y"], 1)
                dve.wait_ge(s["sd_o"], RH)
                copy(y1[:, 7, :], bank[6][:, :]).then_inc(s["sd_y"], 1)
                dve.wait_ge(s["sd_y"], 4)
                for i in range(4):
                    y = y1[:, 4 + i, :]
                    then(dve.scalar_tensor_tensor(out=y, in0=t1[:, 16 + i, :], scalar=S("ssd_d")[:, i:i + 1],
                                                  in1=y, op0=ALU.mult, op1=ALU.add))
                    then(dve.tensor_tensor(y, y, t1[:, 12 + i, :], ALU.mult))
                    dve.tensor_tensor(y_sq[:, i, :], y, y, ALU.mult).then_inc(s["sn_in"], 1)
                dve.wait_ge(s["sn_std"], 1)
                then(dve.reciprocal(std[:, :], std[:, :]))
                for i in range(4):
                    dve.nop().then_inc(s["h_work"], 1)
                for i in range(4):
                    y = y1[:, 4 + i, :]
                    dve.scalar_tensor_tensor(out=y, in0=y, scalar=S("ssd_norm")[:, i:i + 1],
                                             in1=std[:, :], op0=ALU.mult, op1=ALU.mult).then_inc(s["h_work"], 1)
                h_count[0] += KD

            def mixer2():
                each_product("cq", lambda p, b: copy(cq[:, p, :], b[:, 0:LAT]))
                each_product("ckv", lambda p, b: copy(ckv[:, p, :], b[:, :]))
                each_product("kpe", lambda p, b: copy(kpe[LN:LQ, :], b[LN:LQ, :]))
                taken("uq")
                for i in range(6):
                    dve.tensor_tensor(cq_sq(i), cq[:, i, :], cq[:, i, :], ALU.mult).then_inc(s["lq_in"], 1)
                for i in range(2):
                    dve.tensor_tensor(sq_l[:, i, :], ckv[:, i, :], ckv[:, i, :], ALU.mult).then_inc(s["lq_in"], 1)
                dve.wait_ge(s["lq_std"], 1)
                then(dve.reciprocal(std[:, L0:L1], std[:, L0:L1]))
                for i in range(6):
                    last = dve.scalar_tensor_tensor(out=cq[:, i, :], in0=cq[:, i, :], scalar=S("q_norm")[:, i:i + 1],
                                                    in1=std[:, L0:L1], op0=ALU.mult, op1=ALU.mult)
                then(last)
                then(copy(cq_hi[:, :, :], cq))
                low(cq_lo[:, :, :], cq, cq_hi[:, :, :]).then_inc(s["lq_done"], 1)
                dve.wait_ge(s["lq_std"], 2)
                dve.wait_ge(s["lq_done"], 1)
                then(dve.reciprocal(std[:, :], std[:, :]))
                for i in range(2):
                    last = dve.scalar_tensor_tensor(out=ckv[:, i, :], in0=ckv[:, i, :],
                                                    scalar=S("kv_norm")[:, i:i + 1], in1=std[:, :],
                                                    op0=ALU.mult, op1=ALU.mult)
                then(last)
                then(copy(ckv_hi[:, :, :], ckv))
                low(ckv_lo[:, :, :], ckv, ckv_hi[:, :, :]).then_inc(s["lq_done"], 1)
                dve.wait_ge(s["tables_in"], 48)
                cs, sn = (C2(x)[LN:LQ, :] for x in ("cos", "sin"))

                def rotate(v, sw, n):
                    c3, s3 = (x.unsqueeze(1).to_broadcast([LR, n, LAT]) for x in (cs, sn))
                    then(dve.stream_shuffle(sw, v, swap16))
                    dve.tensor_tensor(v, v, c3, ALU.mult)
                    then(dve.tensor_tensor(sw, sw, s3, ALU.mult))
                    return dve.tensor_tensor(v, v, sw, ALU.add)

                rotate(kpe[LN:LQ, L0:L1].unsqueeze(1), kswap[LN:LQ, 0, 0:LAT].unsqueeze(1), 1)\
                    .then_inc(s["kpe_in"], 1)
                each_product("uq", lambda p, b: copy(
                    qh[0:LQ, bass.ds(p, 1), :].rearrange("p a b -> p (a b)"), b[0:LQ, 0:LAT]))
                taken("uk")
                dve.wait_ge(s["kpe_in"], 1)

                def plain_keys(p, b):
                    copy(kh[0:LN, 2 * p, :], b[0:LN, :])
                    return copy(kh[0:LN, 2 * p + 1, :], b[LN:P, :])

                each_product("uk", plain_keys)
                for u in range(LH // 2):
                    then(rotate(qh[LN:LQ, 2 * u:2 * u + 2, :],
                                kswap[LN:LQ, u % 2, :].rearrange("p (a b) -> p a b", a=2), 2))
                each_product("uv", lambda p, b: copy(vl[:, p % TT, p // TT * 512:(p // TT + 1) * 512], b[:, :]))
                taken("out2")
                attention(att2, 2 * AH, LH, LQ ** -0.5, False, 0)

            dve.wait_ge(s["small_in"], 16)
            dve.wait_ge(s["x_in"], 32)
            dve.wait_ge(s["cond_ready"], 1)
            for k in range(8):
                ada_unit(k)
            add_squares(0, TOK)
            for k in range(8, 16):
                ada_unit(k)
            add_bias(0, 16)
            norm(0, True)

            def va_gates(p, b):
                copy(va[:, p, :], b[:, 0:P])
                return dve.tensor_tensor(gates[:, p, :], b[:, P:P + 16], S("gate_b"), ALU.add)

            each_product("va_gates", va_gates)
            dve.wait_ge(s["taken"], ph["vm"].first_taken)
            minus_abs(gtmp, gates)
            each_product("vm", lambda p, b: copy(vm[:, p % TT, p // TT * 256:(p // TT + 1) * 256], b[:, 0:256]))
            log_gates()
            w, cb = S("qk_conv_w", 3), S("qk_conv_b")
            for name, before, first, n in (("km", 0, MH, TOK), ("qm", MH, 0, LAT)):
                def convolve(p, b, before=before, first=first, n=n):
                    if before + p >= 2:
                        dve.wait_ge(s["conv_act"], before + p - 1)
                    c = first + p
                    return conv_taps(conv[:, (before + p) % 2, 0:n], b[:, 0:n],
                                     [w[:, q, c:c + 1] for q in range(3)], cb[:, c:c + 1], n // 256)
                each_product(name, convolve)
            gate_columns()
            each_product("ka", lambda p, b: copy(ka[:, p, :], b[:, :]))
            each_product("qa", lambda p, b: copy(qa[:, p, :], b[:, 0:LAT]))
            running_maxima()
            each_product("om", lambda p, b: copy(om[:, p, :], b[:, 0:LAT]))
            taken("out0")
            dve.wait_ge(s["tables_in"], 16)
            cs, sn = (C0(x).unsqueeze(1) for x in ("cos", "sin"))
            for v, sw, n in ((qa, hm, 4), (ka[:, :, L0:L1], sq_m[:, 0:2, :], 2)):
                c3, s3 = cs.to_broadcast([P, n, LAT]), sn.to_broadcast([P, n, LAT])
                then(dve.stream_shuffle(sw, v, swap16))
                dve.tensor_tensor(v, v, c3, ALU.mult)
                then(dve.tensor_tensor(sw, sw, s3, ALU.mult))
                last = dve.tensor_tensor(v, v, sw, ALU.add)
            last.then_inc(s["rope_ready"], 1)
            dve.wait_ge(s["rope_ready"], 1)
            mlstm()
            attention(att0, 0, AH, AD ** -0.5, True, 4)
            add_bias(16, 48)
            residual("out0", 2, False)
            ffn0()
            final_norm("final_norm")
            if layers > 1:
                layer[0] = 1
                add_squares(0, TOK)
                add_bias(0, 16)
                norm(0, True)
                mixer1()
                add_bias(16, 48)
                residual("out1", 2, True)
                swiglu(1, True)
            if layers > 2:
                layer[0] = 2
                add_bias(0, 48)
                norm(0, True)
                mixer2()
                residual("out2", 2, False)
                swiglu(2, False)
                final_norm("final_norm_2")



def _columns(v):
    v = np.asarray(v)
    return v.reshape(-1, P).T


def _rows(v):
    return np.broadcast_to(np.asarray(v).reshape(1, -1), (P, np.asarray(v).size))


def _units(w, cols):
    w = np.asarray(w)
    k, n = w.shape
    return w.reshape(k // P, P, n // cols, cols).transpose(2, 1, 0, 3).reshape(n // cols, P, -1)


def _outputs(w):
    w = np.asarray(w)
    return w.T.reshape(-1, P, w.shape[0])


def _pairs(a, b):
    a, b = np.asarray(a), np.asarray(b)
    return np.concatenate([a.reshape(D, -1, P), b.reshape(D, -1, P)], axis=2).reshape(D, -1)


def _tokens(x):
    return np.asarray(x)[0].T.reshape(KD, P, -1).transpose(1, 0, 2)


def _layout(i):
    small = {
        "b_ada0": _columns(i["b_ada"][0]), "b_ada1": _columns(i["b_ada_2"][0]),
        "b_ada2": _columns(i["b_ada_2"][1]),
        "norm_mix": _columns(i["norm_mix"][0]), "norm_ffn": _columns(i["norm_ffn"][0]),
        "gate_b": _rows(i["gate_b"][0]),
        "qk_conv_w": np.concatenate([_columns(t) for t in i["qk_conv_w"][0]], 1),
        "qk_conv_b": _columns(i["qk_conv_b"][0]), "mlstm_norm": _columns(i["mlstm_norm"][0]),
        "sink": _rows(i["attn_sink"][0]),
        "ffn_conv_w": np.concatenate([_columns(t) for t in i["ffn_conv_w"][0]], 1),
        "ffn_conv_b": _columns(i["ffn_conv_b"][0]), "final_norm": _columns(i["final_norm"]),
        "ssd_conv_w": np.concatenate([_columns(t) for t in i["ssd_conv_w_2"][0]], 1),
        "ssd_conv_b": _columns(i["ssd_conv_b_2"][0]), "dt_bias": _rows(i["ssd_dt_bias_2"][0]),
        "a_log": _rows(i["ssd_a_log_2"][0]), "ssd_d": _columns(np.repeat(i["ssd_d_2"][0], 64)),
        "ssd_norm": _columns(i["ssd_norm_w_2"][0]), "decay_logit": _rows(i["ret_decay_logit_2"][0]),
        "gn_w": _columns(i["ret_gn_w_2"][0]), "q_norm": _columns(i["mla_q_norm_w_2"][0]),
        "kv_norm": _columns(i["mla_kv_norm_w_2"][0]), "final_norm_2": _columns(i["final_norm_w_2"]),
    }
    w0, w1, w2 = (np.asarray(i[n][0]) for n in ("w_in", "ret_ssd_w_in_2", "mla_w_in_2"))
    m = MH * MD
    q0, k0, v0, o0, g0, qa0, ka0, va0 = np.split(w0, np.cumsum([m, m, m, m, 16, 512, 128]), axis=1)
    arrays = {"x": _tokens(i["x"]), "ctx": _tokens(i["ctx"]), "ctx_2": _tokens(i["ctx_2"]),
              "cond0": _rows(np.stack([i["c"][0], np.asarray(i["c_ctx"]).reshape(-1)])).reshape(P, 2, D),
              "cond1": _rows(np.stack([i["c_2"][0], np.asarray(i["c_ctx_2"]).reshape(-1)])).reshape(P, 2, D),
              "ada0": _outputs(i["w_ada"][0]), "ada1": _outputs(i["w_ada_2"][0]),
              "ada2": _outputs(i["w_ada_2"][1]),
              "vm": _units(v0, P),
              "va_gates": _units(np.concatenate([va0, g0], 1), 144).reshape(P, 2, -1).transpose(1, 0, 2),
              "km": _units(k0, P), "qm": _units(q0, P),
              "ka": _units(np.concatenate([ka0[:, :64], ka0[:, :64], ka0[:, 64:], ka0[:, 64:]], 1), P),
              "qa": _units(qa0, P), "om": _units(o0, P), "out0": _units(i["w_out"][0], P)}
    up = np.asarray(i["w_up"][0])
    arrays["up0"] = _units(_pairs(up[:, :FF], up[:, FF:]), P)
    arrays["down0"] = _units(i["w_down"][0], P)
    q1, k1, v1, g1, z1, xbc1, dt1 = np.split(w1, np.cumsum([512] * 5 + [1024]), axis=1)
    arrays["in1"] = _units(np.concatenate([q1, k1, g1, z1, xbc1], 1), P)
    arrays["vr"] = _units(v1, P)
    arrays["dt"] = _units(dt1, 16)
    arrays["out1"] = _units(i["ret_ssd_w_out_2"][0], P)
    for n in range(2):
        arrays[f"up{n + 1}"] = _units(_pairs(i["w_ffn_gate_2"][n], i["w_ffn_up_2"][n]), P)
        arrays[f"down{n + 1}"] = _units(i["w_ffn_down_2"][n], P)
    arrays["cq"] = _units(w2[:, :768], P)
    arrays["ckv"] = _units(w2[:, 768:1024], P)
    arrays["kpe"] = _units(np.tile(w2[:, 1024:], (1, 4)), P)
    arrays["uq"] = _units(i["mla_w_uq_2"][0], LQ)
    ukv = np.asarray(i["mla_w_ukv_2"][0]).reshape(256, LH, LN + LV)
    arrays["uk"] = _units(ukv[:, :, :LN].reshape(256, -1), 512)
    arrays["uv"] = _units(ukv[:, :, LN:].reshape(256, -1), 512)
    arrays["out2"] = _units(i["mla_w_out_2"][0], P)
    arrays["small"] = np.concatenate(list(small.values()), 1)
    tables_at = []
    for n, tables in enumerate(constant_tables()):
        arrays[f"table{n}"] = np.concatenate(list(tables.values()), 1)
        tables_at.append(packed(tables)[0])
    return arrays, packed(small)[0], tables_at


def kernel(**inputs):
    import concourse.bacc as bacc
    from concourse.bass_utils import run_bass_kernel_spmd

    arrays, small_at, tables_at = _layout({k: np.asarray(v) for k, v in inputs.items()})
    nc = bacc.Bacc("TRN2", target_bir_lowering=False, num_devices=1)
    dram, feed = {}, {}
    for name, a in arrays.items():
        a = np.ascontiguousarray(a)
        feed[f"in_{name}"] = a
        dram[name] = nc.dram_tensor(f"in_{name}", a.shape, mybir.dt.from_np(a.dtype), kind="ExternalInput").ap()
    dram["out"] = nc.dram_tensor("out", (P, KD, LAT), F32, kind="ExternalOutput").ap()
    build(nc, dram, small_at, tables_at)
    r = run_bass_kernel_spmd(nc, [feed], core_ids=[0])
    y = np.asarray(r.results[0]["out"])
    return y.transpose(2, 1, 0).reshape(1, LAT, D)
```
